# Optimizing a Trainium2 kernel written in Bass

```python
import jax, jax.numpy as jnp
from jax import lax
import numpy as np
import math

D_MODEL = 2048
BATCH = 1
SEQ = 256
DEPTH = 1

CHUNK = 64
EPS = 1e-6
M_HEADS = 4
M_DV = 256
M_DQK = 128
M_WIDTH = M_HEADS * M_DV
M_QK_WIDTH = M_HEADS * M_DQK
C_WIDTH = 1024
C_GROUPS = 8
C_KERNEL = 3
D_FF = 5504
F_KERNEL = 3
SPLIT_SIZES = (M_QK_WIDTH, M_QK_WIDTH, M_WIDTH, M_WIDTH, M_HEADS, M_HEADS,
               C_WIDTH, C_WIDTH, C_WIDTH, D_MODEL, D_MODEL)
IN_WIDTH = sum(SPLIT_SIZES)
F_GATE_OFFSET = 2 * M_QK_WIDTH + 2 * M_WIDTH + M_HEADS


def rmsnorm(x, g):
    x32 = x.astype(jnp.float32)
    y = x32 * lax.rsqrt(jnp.mean(x32 * x32, axis=-1, keepdims=True) + EPS)
    return (y * g.astype(jnp.float32)).astype(x.dtype)

def causal_dwconv(x, w, b=None):
    K = w.shape[0]
    T = x.shape[1]
    xp = jnp.pad(x, ((0, 0), (K - 1, 0), (0, 0)))
    y = xp[:, 0:T, :] * w[0]
    for j in range(1, K):
        y = y + xp[:, j:j + T, :] * w[j]
    if b is not None:
        y = y + b
    return y

def mlstm_chunkwise(q, k, v, i_pre, f_pre):
    B, T, H, DQK = q.shape
    DV = v.shape[-1]
    NC = T // CHUNK
    L = CHUNK
    f32 = jnp.float32

    def to_chunks(a):
        a = jnp.moveaxis(a.astype(f32), 2, 1)
        return a.reshape((B, H, NC, L) + a.shape[3:])

    qc = to_chunks(q)
    kc = to_chunks(k) * (DQK ** -0.5)
    vc = to_chunks(v)
    logi = to_chunks(i_pre)
    logf = jax.nn.log_sigmoid(to_chunks(f_pre))

    b = jnp.cumsum(logf, axis=-1)
    a = b[..., -1]
    w = a[..., None] - b + logi
    m_loc = jnp.max(w, axis=-1)
    p = jnp.exp(w - m_loc[..., None])
    C_loc = jnp.einsum('bhcs,bhcsv,bhcsk->bhcvk', p, vc, kc)
    n_loc = jnp.einsum('bhcs,bhcsk->bhck', p, kc)

    def step(carry, xs):
        C, n, m = carry
        a_c, ml, Cl, nl = xs
        m_new = jnp.maximum(a_c + m, ml)
        s_old = jnp.exp(a_c + m - m_new)
        s_new = jnp.exp(ml - m_new)
        C_new = s_old[..., None, None] * C + s_new[..., None, None] * Cl
        n_new = s_old[..., None] * n + s_new[..., None] * nl
        return (C_new, n_new, m_new), (C, n, m)

    init = (jnp.zeros((B, H, DV, DQK), f32), jnp.zeros((B, H, DQK), f32), jnp.zeros((B, H), f32))
    xs = (jnp.moveaxis(a, 2, 0), jnp.moveaxis(m_loc, 2, 0),
          jnp.moveaxis(C_loc, 2, 0), jnp.moveaxis(n_loc, 2, 0))
    _, (C_prev, n_prev, m_prev) = lax.scan(step, init, xs)
    C_prev = jnp.moveaxis(C_prev, 0, 2)
    n_prev = jnp.moveaxis(n_prev, 0, 2)
    m_prev = jnp.moveaxis(m_prev, 0, 2)

    causal = jnp.tril(jnp.ones((L, L), dtype=bool))
    Dm = b[..., :, None] - b[..., None, :] + logi[..., None, :]
    Dm = jnp.where(causal, Dm, -jnp.inf)
    m_inter = b + m_prev[..., None]
    m_t = jnp.maximum(jnp.max(Dm, axis=-1), m_inter)
    S = jnp.einsum('bhctk,bhcsk->bhcts', qc, kc) * jnp.exp(Dm - m_t[..., None])
    inter_scale = jnp.exp(m_inter - m_t)
    num = (jnp.einsum('bhcts,bhcsv->bhctv', S, vc)
           + inter_scale[..., None] * jnp.einsum('bhcvk,bhctk->bhctv', C_prev, qc))
    den = jnp.sum(S, axis=-1) + inter_scale * jnp.einsum('bhck,bhctk->bhct', n_prev, qc)
    h = num / jnp.maximum(jnp.abs(den), jnp.exp(-m_t))[..., None]
    h = h.reshape(B, H, T, DV)
    return jnp.moveaxis(h, 1, 2)

def first_inputs(seed: int = 0) -> dict:
    key = jax.random.key(seed)
    ks = jax.random.split(key, 16)
    f32 = jnp.float32
    nrm = lambda k, shape, scale: (jax.random.normal(k, shape, f32) * scale)
    x = jax.random.normal(ks[0], (BATCH, SEQ, D_MODEL), f32)
    norm_mix_g = 1.0 + nrm(ks[1], (D_MODEL,), 0.02)
    w_in = nrm(ks[2], (D_MODEL, IN_WIDTH), D_MODEL ** -0.5)
    b_in = nrm(ks[3], (IN_WIDTH,), 0.02)
    b_in = b_in.at[F_GATE_OFFSET:F_GATE_OFFSET + M_HEADS].add(jnp.linspace(3.0, 6.0, M_HEADS))
    mlstm_head_g = 1.0 + nrm(ks[4], (M_WIDTH,), 0.02)
    w_branch_m = nrm(ks[5], (M_WIDTH, D_MODEL), M_WIDTH ** -0.5)
    conv_w = nrm(ks[6], (C_KERNEL, C_WIDTH), C_KERNEL ** -0.5)
    w_branch_c = nrm(ks[7], (C_WIDTH, D_MODEL), C_WIDTH ** -0.5)
    w_out = nrm(ks[8], (D_MODEL, D_MODEL), D_MODEL ** -0.5)
    norm_ffn_g = 1.0 + nrm(ks[9], (D_MODEL,), 0.02)
    w_up = nrm(ks[10], (D_MODEL, 2 * D_FF), D_MODEL ** -0.5)
    ffn_conv_w = nrm(ks[11], (F_KERNEL, 2 * D_FF), F_KERNEL ** -0.5)
    ffn_conv_b = nrm(ks[12], (2 * D_FF,), 0.02)
    w_down = nrm(ks[13], (D_FF, D_MODEL), D_FF ** -0.5)
    norm_out_g = 1.0 + nrm(ks[14], (D_MODEL,), 0.02)
    return {"x": x, "norm_mix_g": norm_mix_g, "w_in": w_in, "b_in": b_in,
            "mlstm_head_g": mlstm_head_g, "w_branch_m": w_branch_m, "conv_w": conv_w,
            "w_branch_c": w_branch_c, "w_out": w_out, "norm_ffn_g": norm_ffn_g,
            "w_up": w_up, "ffn_conv_w": ffn_conv_w, "ffn_conv_b": ffn_conv_b,
            "w_down": w_down, "norm_out_g": norm_out_g}

def first_block(x, norm_mix_g, w_in, b_in, mlstm_head_g, w_branch_m, conv_w, w_branch_c,
              w_out, norm_ffn_g, w_up, ffn_conv_w, ffn_conv_b, w_down, norm_out_g):
    B, T, _ = x.shape
    h = x
    for _layer in range(DEPTH):
        hn = rmsnorm(h, norm_mix_g)
        proj = hn @ w_in + b_in
        offs = [int(o) for o in np.cumsum(SPLIT_SIZES)[:-1]]
        (q, k, v, o_pre, i_pre, f_pre, cb, cc, ch, gm_pre, gc_pre) = jnp.split(proj, offs, axis=-1)

        hm = mlstm_chunkwise(q.reshape(B, T, M_HEADS, M_DQK), k.reshape(B, T, M_HEADS, M_DQK),
                             v.reshape(B, T, M_HEADS, M_DV), i_pre, f_pre)
        hm = hm * lax.rsqrt(jnp.mean(hm * hm, axis=-1, keepdims=True) + EPS)
        hm = hm.reshape(B, T, M_WIDTH) * mlstm_head_g.astype(jnp.float32)
        hm = hm.astype(x.dtype) * jax.nn.sigmoid(o_pre)
        y_m = hm @ w_branch_m

        y_c = (cb * causal_dwconv(cc * ch, conv_w)) @ w_branch_c

        merged = jax.nn.sigmoid(gm_pre) * y_m + jax.nn.sigmoid(gc_pre) * y_c
        h = h + merged @ w_out

        hn = rmsnorm(h, norm_ffn_g)
        u = causal_dwconv(hn @ w_up, ffn_conv_w, ffn_conv_b)
        gate, val = jnp.split(u, 2, axis=-1)
        h = h + (jax.nn.silu(gate) * val) @ w_down
    return rmsnorm(h, norm_out_g)


DEPTH_2 = 2

N_MIXERS = 2
NORM_EPS = 1e-6

GLA_HEADS = 4
GLA_QK = D_MODEL // 2
GLA_V = D_MODEL
GLA_DK = GLA_QK // GLA_HEADS
GLA_DV = GLA_V // GLA_HEADS
GLA_GATE_RANK = 16
GLA_GATE_TAU = 16.0
GLA_CHUNK = 64
GLA_IN = 2 * GLA_QK + 2 * GLA_V + GLA_GATE_RANK

MLA_HEADS = 16
MLA_Q_RANK = 512
MLA_KV_RANK = 512
MLA_NOPE = 128
MLA_ROPE = 64
MLA_V = 128
MLA_WIDTH = MLA_HEADS * MLA_V
MLA_IN = MLA_Q_RANK + MLA_KV_RANK + MLA_ROPE + MLA_WIDTH
ROPE_THETA = 10000.0
Q_BLOCK = 128


def rms_norm(x, g, eps=NORM_EPS):
    xf = x.astype(jnp.float32)
    y = xf * lax.rsqrt(jnp.mean(xf * xf, axis=-1, keepdims=True) + eps)
    return (y * g.astype(jnp.float32)).astype(x.dtype)

def _to_chunks(t, n_chunks):
    B, S, H, D = t.shape
    return t.reshape(B, n_chunks, S // n_chunks, H, D).transpose(0, 3, 1, 2, 4)

def gla_mixer(h, w_in, w_gk2, b_gk, g_onorm, w_out):
    B, S, _ = h.shape
    nC = S // GLA_CHUNK
    proj = h @ w_in
    q, k, v, gate, gk_low = jnp.split(
        proj, [GLA_QK, 2 * GLA_QK, 2 * GLA_QK + GLA_V, 2 * GLA_QK + 2 * GLA_V], axis=-1)
    gk = gk_low @ w_gk2 + b_gk
    log_a = jax.nn.log_sigmoid(gk.astype(jnp.float32)) / GLA_GATE_TAU

    q = _to_chunks(q.reshape(B, S, GLA_HEADS, GLA_DK), nC) * (GLA_DK ** -0.5)
    k = _to_chunks(k.reshape(B, S, GLA_HEADS, GLA_DK), nC)
    v = _to_chunks(v.reshape(B, S, GLA_HEADS, GLA_DV), nC)
    log_a = _to_chunks(log_a.reshape(B, S, GLA_HEADS, GLA_DK), nC)

    b = jnp.cumsum(log_a, axis=3)
    b_last = b[..., -1:, :]
    q_e = q * jnp.exp(b)
    k_e = k * jnp.exp(-b)
    k_last = k * jnp.exp(b_last - b)

    A = jnp.einsum('bhncd,bhnsd->bhncs', q_e, k_e)
    causal = jnp.tril(jnp.ones((GLA_CHUNK, GLA_CHUNK), dtype=bool))
    A = jnp.where(causal, A, 0.0)
    o_intra = jnp.einsum('bhncs,bhnsv->bhncv', A, v.astype(A.dtype))

    def step(state, xs):
        q_c, kl_c, v_c, dl_c = xs
        o_c = jnp.einsum('bhcd,bhdv->bhcv', q_c, state)
        state = state * dl_c[..., :, None] + jnp.einsum('bhcd,bhcv->bhdv', kl_c, v_c)
        return state, o_c

    state0 = jnp.zeros((B, GLA_HEADS, GLA_DK, GLA_DV), dtype=jnp.float32)
    xs = (jnp.moveaxis(q_e, 2, 0).astype(jnp.float32),
          jnp.moveaxis(k_last, 2, 0).astype(jnp.float32),
          jnp.moveaxis(v, 2, 0).astype(jnp.float32),
          jnp.moveaxis(jnp.exp(b_last[..., 0, :]), 2, 0).astype(jnp.float32))
    _, o_inter = lax.scan(step, state0, xs)
    o = o_intra + jnp.moveaxis(o_inter, 0, 2)

    o = o.transpose(0, 2, 3, 1, 4).reshape(B, S, GLA_HEADS, GLA_DV).astype(h.dtype)
    o = rms_norm(o, g_onorm).reshape(B, S, GLA_V)
    return (o * jax.nn.silu(gate)) @ w_out

def _rope(t, cos, sin):
    half = t.shape[-1] // 2
    t1, t2 = t[..., :half], t[..., half:]
    return jnp.concatenate([t1 * cos - t2 * sin, t2 * cos + t1 * sin], axis=-1)

def mla_mixer(h, positions, w_in, g_qa, w_qb, g_kva, w_kvb, w_out):
    B, S, _ = h.shape
    proj = h @ w_in
    c_q, c_kv, k_rope, gate = jnp.split(
        proj, [MLA_Q_RANK, MLA_Q_RANK + MLA_KV_RANK, MLA_Q_RANK + MLA_KV_RANK + MLA_ROPE], axis=-1)
    q = (rms_norm(c_q, g_qa) @ w_qb).reshape(B, S, MLA_HEADS, MLA_NOPE + MLA_ROPE)
    kv = (rms_norm(c_kv, g_kva) @ w_kvb).reshape(B, S, MLA_HEADS, MLA_NOPE + MLA_V)
    q_nope, q_rope = q[..., :MLA_NOPE], q[..., MLA_NOPE:]
    k_nope, v = kv[..., :MLA_NOPE], kv[..., MLA_NOPE:]

    inv_freq = ROPE_THETA ** (-jnp.arange(0, MLA_ROPE, 2, dtype=jnp.float32) / MLA_ROPE)
    ang = positions.astype(jnp.float32)[..., None] * inv_freq
    cos, sin = jnp.cos(ang), jnp.sin(ang)
    q_rope = _rope(q_rope, cos[:, :, None, :], sin[:, :, None, :]).astype(h.dtype)
    k_rope = _rope(k_rope, cos, sin).astype(h.dtype)
    q = jnp.concatenate([q_nope, q_rope], axis=-1)
    k = jnp.concatenate(
        [k_nope, jnp.broadcast_to(k_rope[:, :, None, :], (B, S, MLA_HEADS, MLA_ROPE))], axis=-1)
    scale = (MLA_NOPE + MLA_ROPE) ** -0.5

    n_blocks = S // Q_BLOCK
    q_blocks = q.reshape(B, n_blocks, Q_BLOCK, MLA_HEADS, -1).transpose(1, 0, 2, 3, 4)
    starts = jnp.arange(n_blocks, dtype=jnp.int32) * Q_BLOCK
    k_idx = jnp.arange(S, dtype=jnp.int32)

    def attend(args):
        qb, start = args
        s = jnp.einsum('bqhd,bkhd->bhqk', qb, k).astype(jnp.float32) * scale
        q_idx = start + jnp.arange(Q_BLOCK, dtype=jnp.int32)
        s = jnp.where(k_idx[None, :] <= q_idx[:, None], s, jnp.finfo(jnp.float32).min)
        p = jax.nn.softmax(s, axis=-1).astype(v.dtype)
        return jnp.einsum('bhqk,bkhv->bqhv', p, v)

    o = lax.map(attend, (q_blocks, starts))
    o = o.transpose(1, 0, 2, 3, 4).reshape(B, S, MLA_WIDTH)
    return (o * jax.nn.silu(gate)) @ w_out

def second_inputs(seed: int = 0) -> dict:
    key = jax.random.key(seed)
    ks = jax.random.split(key, 16)

    def w(k, shape):
        return jax.random.normal(k, shape, jnp.float32) * (shape[0] ** -0.5)

    def gain(k, n):
        return 1.0 + 0.05 * jax.random.normal(k, (n,), jnp.float32)

    x = jax.random.normal(ks[0], (BATCH, SEQ, D_MODEL), jnp.float32)
    positions = jnp.broadcast_to(jnp.arange(SEQ, dtype=jnp.int32)[None, :], (BATCH, SEQ))
    return {
        "x": x,
        "positions": positions,
        "l0_pre_norm": gain(ks[1], D_MODEL),
        "l0_gla_w_in": w(ks[2], (D_MODEL, GLA_IN)),
        "l0_gla_w_gk2": w(ks[3], (GLA_GATE_RANK, GLA_QK)),
        "l0_gla_b_gk": 0.1 * jax.random.normal(ks[4], (GLA_QK,), jnp.float32),
        "l0_gla_g_onorm": gain(ks[5], GLA_DV),
        "l0_gla_w_out": w(ks[6], (GLA_V, D_MODEL)),
        "l0_post_norm": gain(ks[7], D_MODEL),
        "l1_pre_norm": gain(ks[8], D_MODEL),
        "l1_mla_w_in": w(ks[9], (D_MODEL, MLA_IN)),
        "l1_mla_g_qa": gain(ks[10], MLA_Q_RANK),
        "l1_mla_w_qb": w(ks[11], (MLA_Q_RANK, MLA_HEADS * (MLA_NOPE + MLA_ROPE))),
        "l1_mla_g_kva": gain(ks[12], MLA_KV_RANK),
        "l1_mla_w_kvb": w(ks[13], (MLA_KV_RANK, MLA_HEADS * (MLA_NOPE + MLA_V))),
        "l1_mla_w_out": w(ks[14], (MLA_WIDTH, D_MODEL)),
        "l1_post_norm": gain(ks[15], D_MODEL),
    }

def second_block(x, positions,
              l0_pre_norm, l0_gla_w_in, l0_gla_w_gk2, l0_gla_b_gk, l0_gla_g_onorm, l0_gla_w_out,
              l0_post_norm,
              l1_pre_norm, l1_mla_w_in, l1_mla_g_qa, l1_mla_w_qb, l1_mla_g_kva, l1_mla_w_kvb,
              l1_mla_w_out, l1_post_norm):
    layers = [
        (l0_pre_norm, (l0_gla_w_in, l0_gla_w_gk2, l0_gla_b_gk, l0_gla_g_onorm, l0_gla_w_out),
         l0_post_norm),
        (l1_pre_norm, (l1_mla_w_in, l1_mla_g_qa, l1_mla_w_qb, l1_mla_g_kva, l1_mla_w_kvb,
                       l1_mla_w_out), l1_post_norm),
    ]
    for i in range(DEPTH_2):
        g_pre, params, g_post = layers[i]
        h = rms_norm(x, g_pre)
        if i % N_MIXERS == 0:
            y = gla_mixer(h, *params)
        else:
            y = mla_mixer(h, positions, *params)
        x = x + rms_norm(y, g_post)
    return x


def setup_inputs(seed=0):
    out = dict(first_inputs(seed))
    for name, value in second_inputs(seed + 1).items():
        if name != "x":
            out[name + "_2"] = value
    return out


def reference(
    x, norm_mix_g, w_in, b_in, mlstm_head_g, w_branch_m, conv_w, w_branch_c, w_out, norm_ffn_g,
    w_up, ffn_conv_w, ffn_conv_b, w_down, norm_out_g, positions_2, l0_pre_norm_2, l0_gla_w_in_2,
    l0_gla_w_gk2_2, l0_gla_b_gk_2, l0_gla_g_onorm_2, l0_gla_w_out_2, l0_post_norm_2,
    l1_pre_norm_2, l1_mla_w_in_2, l1_mla_g_qa_2, l1_mla_w_qb_2, l1_mla_g_kva_2, l1_mla_w_kvb_2,
    l1_mla_w_out_2, l1_post_norm_2,
):
    x = first_block(
        x, norm_mix_g, w_in, b_in, mlstm_head_g, w_branch_m, conv_w, w_branch_c, w_out,
        norm_ffn_g, w_up, ffn_conv_w, ffn_conv_b, w_down, norm_out_g,
    )
    return second_block(
        x, positions_2, l0_pre_norm_2, l0_gla_w_in_2, l0_gla_w_gk2_2, l0_gla_b_gk_2,
        l0_gla_g_onorm_2, l0_gla_w_out_2, l0_post_norm_2, l1_pre_norm_2, l1_mla_w_in_2,
        l1_mla_g_qa_2, l1_mla_w_qb_2, l1_mla_g_kva_2, l1_mla_w_kvb_2, l1_mla_w_out_2,
        l1_post_norm_2,
    )


_drawn_inputs = setup_inputs


def setup_inputs(seed=0):
    import zlib

    import numpy as np

    out = dict(_drawn_inputs(seed))
    spreads = {}
    factors = {'mlstm_head_g': 4.639, 'norm_ffn_g': 2.7, 'ffn_conv_b': 2.699}
    for name, (base, spread) in spreads.items():
        noise = np.random.default_rng([zlib.crc32(name.encode()), seed]).standard_normal(out[name].shape)
        drawn = base * np.exp(spread * noise) if base else spread * noise
        out[name] = __import__('jax').numpy.asarray(drawn.astype(out[name].dtype))
    for name, factor in factors.items():
        out[name] = (out[name] * factor).astype(out[name].dtype)
    return out
```

```python
from contextlib import ExitStack

import concourse.bass as bass
from concourse import mybir

P = 128
T = 256
D = 2048
KT = D // P
CHUNK = 64
PI = 3.14159265358979
PI_INSIDE = 3.1415925
EPS = 1e-6
M_HEADS, M_DV, M_DQK = 4, 256, 128
C_TILES = 1024 // P
D_FF = 5504
F_TILES = D_FF // P
G_HEADS, G_DK, G_DV, G_RANK, G_TAU = 4, 256, 512, 16, 16.0
A_HEADS, A_RANK, A_NOPE, A_ROPE, A_V = 16, 512, 128, 64, 128
A_TILES = A_RANK // P
HALF = A_ROPE // 2
UNIT = 1024
RING = 4

PHASES = [
    ("gates", 1, 2, 1, 0, 0),
    ("mix", M_HEADS, 24, 5, 5, 1),
    ("merge", KT // 2, 12, 4, 4, 0),
    ("wout", KT // 2, 4, 1, 1, 0),
    ("wup", F_TILES, 4, 1, 1, 0),
    ("wdown", KT // 2, 12, 1, 1, 0),
    ("rank", 1, 2, 0, 1, 0),
    ("gla", G_HEADS, 24, 4, 4, 1),
    ("glaout", KT // 2, 4, 1, 1, 0),
    ("latent", A_TILES, 4, 1, 1, 0),
    ("krope", 1, 4, 1, 1, 0),
    ("mla", A_HEADS // 4, 16, 5, 4, 1),
    ("mlaout", KT // 2, 4, 1, 1, 0),
]
N_CHUNKS = sum(n * units for _, n, units, *_ in PHASES) // 2

PARAMS = [
    ("g_mix", KT), ("g_ffn", KT), ("g_out", KT), ("g_pre0", KT), ("g_post0", KT), ("g_pre1", KT),
    ("g_post1", KT), ("b_gate", 1), ("b_mix", M_HEADS * 10), ("b_merge", 2 * KT), ("g_head", 8),
    ("w_conv", 3 * C_TILES), ("w_ffn", 8 * F_TILES), ("g_gla", G_DV // P), ("g_latent", 8),
    ("inv_freq", 1),
]
N_PARAMS = sum(n for _, n in PARAMS)


def program(nc, x_in, stream_in, params_in, v_bias_in, gk2_in, positions_in, out):
    fp32, fp32r, i32 = mybir.dt.float32, mybir.dt.float32r, mybir.dt.int32
    ALU = mybir.AluOpType
    ACT = mybir.ActivationFunctionType
    AX = mybir.AxisListType.X

    base, total = {}, [0, 0, 0, 0]
    for name, n, *per in PHASES:
        base[name] = (list(total), per)
        total = [t + n * k for t, k in zip(total, per)]

    def count(which, name, i, j):
        start, per = base[name]
        k = start[which] + j
        return k if i is None else i * per[which] + k

    def unit_of(name, i, j):
        start, per = base[name]
        k = start[0] + j
        if i is None:
            return k, k % RING, k // RING
        assert per[0] % RING == 0
        return i * per[0] + k, k % RING, i * (per[0] // RING) + k // RING

    ctx = ExitStack()
    with ctx:
        def sb(name, shape, dt=fp32):
            return ctx.enter_context(nc.sbuf_tensor(name, shape, dt))

        def sem(name):
            return ctx.enter_context(nc.semaphore(name))

        x = sb("x", [P, KT, T])
        raw = sb("raw", [P, RING, UNIT])
        w_hi = sb("w_hi", [P, RING, UNIT], fp32r)
        w_lo = sb("w_lo", [P, RING, UNIT], fp32r)
        n_hi = sb("n_hi", [P, KT, T], fp32r)
        n_lo = sb("n_lo", [P, KT, T], fp32r)
        par = sb("par", [P, N_PARAMS])
        normed = sb("normed", [P, 4, T])
        square = sb("square", [P, 2, T])
        sumsq = sb("sumsq", [P, T])
        std = sb("std", [P, T])
        rstd = sb("rstd", [P, T])
        g_both = sb("g_both", [P, KT])
        ones = sb("ones", [P, P])
        ident = sb("ident", [P, P])
        cosine = sb("cosine", [P, T])
        sine = sb("sine", [P, T])
        eps_col = sb("eps_col", [P, 1])

        arena_start = -(-nc.sbuf_base // 64) * 64
        arena_end = nc.sbuf_usable_end

        class Arena:
            def __init__(self, at):
                self.at = at

            def place(self, name, shape, dt=fp32):
                n = 4
                for s in shape[1:]:
                    n *= s
                t = nc.alloc_sbuf_tensor_at(name, shape, dt, offset=self.at)
                self.at += -(-n // 32) * 32
                assert self.at <= arena_end, (name, self.at - arena_end)
                return t

        a = Arena(arena_start)
        yc_hi = a.place("yc_hi", [P, C_TILES, T], fp32r)
        yc_lo = a.place("yc_lo", [P, C_TILES, T], fp32r)
        hm_hi = a.place("hm_hi", [P, C_TILES, T], fp32r)
        hm_lo = a.place("hm_lo", [P, C_TILES, T], fp32r)
        sig_m = a.place("sig_m", [P, T])
        sig_c = a.place("sig_c", [P, T])
        part_m = a.place("part_m", [P, T])
        part_c = a.place("part_c", [P, T])
        merged = a.place("merged", [P, T])
        mixer_temps = a.at
        mg_hi = a.place("mg_hi", [P, KT, T], fp32r)
        mg_lo = a.place("mg_lo", [P, KT, T], fp32r)
        a = Arena(mixer_temps)
        decay0 = a.place("decay0", [P, M_HEADS, T])
        decay1 = a.place("decay1", [P, M_HEADS, P])
        floor = a.place("floor", [P, M_HEADS, T])
        v_bias = a.place("v_bias", [P, M_HEADS, M_DV])
        qT = a.place("qT", [P, T])
        kT = a.place("kT", [P, T])
        vm = a.place("vm", [P, 2, M_DV])
        sig_o = a.place("sig_o", [P, 2, T])
        st0 = a.place("st0", [P, T])
        st1 = a.place("st1", [P, P])
        den_abs = a.place("den_abs", [P, T])
        den = a.place("den", [P, T])
        rden = a.place("rden", [P, T])
        h = a.place("h", [P, 2, T])
        h_sq = a.place("h_sq", [P, 2, T])
        h_sum = a.place("h_sum", [P, T])
        h_std = a.place("h_std", [P, T])
        h_rstd = a.place("h_rstd", [P, T])
        h_norm = a.place("h_norm", [P, 2, T])
        hm = a.place("hm", [P, 2, T])
        cc = a.place("cc", [P, T])
        cu = a.place("cu", [P, T])
        cy = a.place("cy", [P, T])
        cz = a.place("cz", [P, T])
        i_row = a.place("i_row", [64, T])
        f_row = a.place("f_row", [64, T])
        f_abs = a.place("f_abs", [64, T])
        f_exp = a.place("f_exp", [64, T])
        f_log = a.place("f_log", [64, T])
        f_min = a.place("f_min", [64, T])
        logf = a.place("logf", [64, T])
        logf0 = a.place("logf0", [M_HEADS, T])
        ones_row = a.place("ones_row", [M_HEADS, T])
        b_row = a.place("b_row", [M_HEADS, T])
        a_row = a.place("a_row", [M_HEADS, T])
        mm_row = a.place("mm_row", [M_HEADS, 2, T])
        a_col = a.place("a_col", [P, 2, M_HEADS])
        head_row = a.place("head_row", [M_HEADS, M_HEADS, P])

        squares_all = Arena(arena_start).place("squares_all", [P, KT, T])

        a = Arena(arena_start)
        f_hi = a.place("f_hi", [P, F_TILES, T], fp32r)
        f_lo = a.place("f_lo", [P, F_TILES, T], fp32r)
        f_pre = a.place("f_pre", [P, 2, T])
        f_gate = a.place("f_gate", [P, T])
        f_val = a.place("f_val", [P, T])
        f_silu = a.place("f_silu", [P, T])
        f_act = a.place("f_act", [P, T])
        square_g = a.place("square_g", [P, 2, T])
        sumsq_g = a.place("sumsq_g", [P, T])
        mean_g = Arena(a.at).place("mean_g", [P, T])
        a = Arena(a.at - 3 * 4 * T)
        mean_part = a.place("mean_part", [P, T])
        rstd_both = a.place("rstd_both", [P, T])

        a = Arena(arena_start)
        og_hi = a.place("og_hi", [P, KT, T], fp32r)
        og_lo = a.place("og_lo", [P, KT, T], fp32r)
        y_at = a.at
        y = a.place("y", [P, KT, T])
        restart = a.place("restart", [P, 2, T])
        gcum = a.place("gcum", [P, G_HEADS, 2, T])
        to_end = a.place("to_end", [P, 2, T])
        e_pos = a.place("e_pos", [P, 2, T])
        e_neg = a.place("e_neg", [P, 2, T])
        e_end = a.place("e_end", [P, 2, T])
        q_e = a.place("q_e", [P, 2, T])
        q_x = a.place("q_x", [P, 2, 2 * CHUNK])
        q_y = a.place("q_y", [P, 2, CHUNK])
        k_sb = a.place("k_sb", [P, 2, T])
        k_e = a.place("k_e", [P, 2, T])
        k_l = a.place("k_l", [P, 2, T])
        a_t = a.place("a_t", [P, 2, T])
        kept = a.place("kept", [P, P])
        vg = a.place("vg", [P, 2, G_DV])
        o_sb = a.place("o_sb", [P, 4, T])
        o_sq = a.place("o_sq", [P, 4, T])
        a = Arena(y_at)
        rank_rows = a.place("rank_rows", [32, T])
        gk2 = a.place("gk2", [G_RANK + 1, G_HEADS * G_DK])
        g_abs = a.place("g_abs", [P, 2 * T])
        g_exp = a.place("g_exp", [P, 2 * T])
        g_log = a.place("g_log", [P, 2 * T])
        g_min = a.place("g_min", [P, 2 * T])
        log_a = a.place("log_a", [P, 2 * T])
        a = Arena(y_at)
        o_sg = a.place("o_sg", [P, 4, T])
        o_sum2 = a.place("o_sum2", [P, 2, T])
        o_sum = a.place("o_sum", [P, T])
        o_std = a.place("o_std", [P, T])
        o_rstd = a.place("o_rstd", [P, T])
        o_norm = a.place("o_norm", [P, 4, T])

        a = Arena(arena_start)
        mo_hi = a.place("mo_hi", [P, KT, T], fp32r)
        mo_lo = a.place("mo_lo", [P, KT, T], fp32r)
        y2_at = a.at
        y2 = a.place("y2", [P, KT, T])
        c_hi = a.place("c_hi", [P, 2 * A_TILES, T], fp32r)
        c_lo = a.place("c_lo", [P, 2 * A_TILES, T], fp32r)
        kr_m = a.place("kr_m", [P, 2, 4, T])
        causal = a.place("causal", [P, 3 * P])
        rope_t = a.place("rope_t", [P, 4, T])
        kn = a.place("kn", [P, 4, T])
        qn = a.place("qn", [P, 4, T])
        probs_t = a.place("probs_t", [P, 2, 3 * P])
        kr = Arena(a.at).place("kr", [P, 2, T])
        a_gate = a.place("a_gate", [P, 4, T])
        a_out = a.place("a_out", [P, 4, T])
        row_max = a.place("row_max", [P, 2, 2])
        neg_max = a.place("neg_max", [P, 2, 2])
        row_sum = a.place("row_sum", [P, 2, 2])
        row_inv = a.place("row_inv", [P, 2, 2])
        a = Arena(y2_at)
        latent = a.place("latent", [P, 2, A_TILES, T])
        l_square = a.place("l_square", [P, 2, T])
        l_sumsq = a.place("l_sumsq", [P, 2, T])
        l_std = a.place("l_std", [P, 2, T])
        l_rstd = a.place("l_rstd", [P, 2, T])
        a = Arena(y2_at)
        q_r = a.place("q_r", [P, 2, T])
        q_rope = a.place("q_rope", [P, 2, T])
        va = a.place("va", [P, 2, 4 * A_V])
        logits = a.place("logits", [P, 2, 3 * P])
        probs = a.place("probs", [P, 2, 3 * P])

        a = Arena(arena_start + 4 * 2 * C_TILES * T)
        pos_i = a.place("pos_i", [P, T], i32)
        ang = a.place("ang", [P, T])
        turns = a.place("turns", [P, T])
        turns_i = a.place("turns_i", [P, T], i32)
        red = a.place("red", [P, 2, T])
        wrap = a.place("wrap", [P, 2, T])

        def pcols(name):
            at = 0
            for n, k in PARAMS:
                if n == name:
                    return par[:, at:at + k]
                at += k

        par_mix = pcols("b_mix").rearrange("p (h c) -> p h c", h=M_HEADS)
        par_conv = pcols("w_conv").rearrange("p (h c) -> p h c", h=M_HEADS)
        par_head = pcols("g_head").rearrange("p (h c) -> p h c", h=M_HEADS)
        par_merge = pcols("b_merge").rearrange("p (m c) -> p m c", c=4)
        par_ffn = pcols("w_ffn").rearrange("p (f c) -> p f c", c=8)

        def gains(name):
            return pcols(name).rearrange("p (i m) -> p i m", m=2)

        def fours(columns):
            return columns.rearrange("p (g m) -> p g m", m=4)

        def pb(name):
            return ctx.enter_context(nc.psum_tensor(name, [P, 512], fp32))

        acc = [pb("acc0"), pb("acc1")]
        tok = [pb("tok0"), pb("tok1")]
        att = [pb(f"att{i}") for i in range(4)]

        loaded = sem("loaded")
        x_loaded = [sem(f"x_loaded{g}") for g in range(KT // 4)]
        gains_ready = sem("gains_ready")
        squares_ready = sem("squares_ready")
        bias_loaded = sem("bias_loaded")
        pos_loaded = sem("pos_loaded")
        gk2_loaded = sem("gk2_loaded")
        raw_ready = [sem("raw_ready0"), sem("raw_ready1")]
        hi_ready = sem("hi_ready")
        lo_ready = sem("lo_ready")
        unit_done = sem("unit_done")
        acc_taken = [sem("acc_taken0"), sem("acc_taken1")]
        tok_taken = sem("tok_taken")
        const_ready = sem("const_ready")
        sq_ready = sem("sq_ready")
        sq_added = sem("sq_added")
        stat_ready = sem("stat_ready")
        std_ready = sem("std_ready")
        rstd_ready = sem("rstd_ready")
        normed_ready = sem("normed_ready")
        nhi_ready = sem("nhi_ready")
        act_ready = sem("act_ready")
        scaled_ready = sem("scaled_ready")
        x_normed = sem("x_normed")
        mean_ready = sem("mean_ready")
        x_added = sem("x_added")
        x_added_pool = sem("x_added_pool")
        stored = sem("stored")
        dve_step = sem("dve_step")
        act_step = sem("act_step")
        pool_step = sem("pool_step")
        rows_ready = sem("rows_ready")
        rows_t_ready = sem("rows_t_ready")
        row_pre = sem("row_pre")
        row_log = sem("row_log")
        a_col_ready = sem("a_col_ready")
        bcast_ready = sem("bcast_ready")
        bcast_taken = sem("bcast_taken")
        decay_masked = sem("decay_masked")
        scores_ready = sem("scores_ready")
        st_ready = sem("st_ready")
        pv_ready = sem("pv_ready")
        den_ready = sem("den_ready")
        h_ready = sem("h_ready")
        hsq_ready = sem("hsq_ready")
        hsum_ready = sem("hsum_ready")
        hstat_ready = sem("hstat_ready")
        hstd_ready = sem("hstd_ready")
        hm_ready = sem("hm_ready")
        hmhi_ready = sem("hmhi_ready")
        hmlo_ready = sem("hmlo_ready")
        h_normed = sem("h_normed")
        ychi_ready = sem("ychi_ready")
        yclo_ready = sem("yclo_ready")
        merged_ready = sem("merged_ready")
        mghi_ready = sem("mghi_ready")
        mglo_ready = sem("mglo_ready")
        ftap_ready = sem("ftap_ready")
        fsilu_ready = sem("fsilu_ready")
        fact_ready = sem("fact_ready")
        fhi_ready = sem("fhi_ready")
        flo_ready = sem("flo_ready")
        rope_ready = sem("rope_ready")
        rope_red = sem("rope_red")
        gk_ready = sem("gk_ready")
        gk_taken = sem("gk_taken")
        glog_ready = sem("glog_ready")
        gcum_ready = sem("gcum_ready")
        restart_ready = sem("restart_ready")
        rank_ones = sem("rank_ones")
        at_init = sem("at_init")
        qx_ready = sem("qx_ready")
        kk_ready = sem("kk_ready")
        decays_ready = sem("decays_ready")
        to_end_ready = sem("to_end_ready")
        gscores_ready = sem("gscores_ready")
        at_ready = sem("at_ready")
        gpv_ready = sem("gpv_ready")
        osb_ready = sem("osb_ready")
        osq_ready = sem("osq_ready")
        osum_ready = sem("osum_ready")
        ostat_ready = sem("ostat_ready")
        ostd_ready = sem("ostd_ready")
        og_ready = sem("og_ready")
        oghi_ready = sem("oghi_ready")
        oglo_ready = sem("oglo_ready")
        lsq_added = sem("lsq_added")
        lstat_ready = sem("lstat_ready")
        lstd_ready = sem("lstd_ready")
        cnormed_ready = sem("cnormed_ready")
        chi_ready = sem("chi_ready")
        c_ready = sem("c_ready")
        krm_zero = sem("krm_zero")
        krm_ready = sem("krm_ready")
        causal_ready = sem("causal_ready")
        qrope_ready = sem("qrope_ready")
        logits_ready = sem("logits_ready")
        neg_ready = sem("neg_ready")
        exp_ready = sem("exp_ready")
        inv_ready = sem("inv_ready")
        probs_ready = sem("probs_ready")
        ptp_ready = sem("ptp_ready")
        ptr_ready = sem("ptr_ready")
        apv_ready = sem("apv_ready")
        aout_ready = sem("aout_ready")
        mohi_ready = sem("mohi_ready")
        molo_ready = sem("molo_ready")

        block = ctx.enter_context(nc.Block())

        def taken(eng, b, name, i, j):
            eng.wait_ge(acc_taken[b], count(1 + b, name, i, j + 1))

        class Chain:

            def __init__(self, eng, steps):
                self.eng, self.steps, self.n = eng, steps, 0
                self.i, self.per, self.start = None, 0, 0

            def loop(self, i, per):
                self.i, self.per, self.start = i, per, self.n

            def done(self, iterations):
                assert self.n - self.start == self.per, (self.n - self.start, self.per)
                self.n = self.start + iterations * self.per
                self.i = None

            def step(self, ins):
                ins.then_inc(self.steps, 1)
                self.n += 1

            def wait(self):
                self.eng.wait_ge(self.steps, self.n if self.i is None else self.i * self.per + self.n)

            def link(self, ins):
                self.step(ins)
                self.wait()

        NORM = {n: k for k, n in enumerate(["mix", "ffn", "out", "pre0", "post0", "pre1", "post1"])}
        STAT = {n: k for k, n in enumerate(["mix", "ffn", "out", "post0", "pre1", "post1"])}
        POOLED = {n: k for k, n in enumerate(["ffn", "out", "post0", "post1"])}
        TO_ACT = {n: k for k, n in enumerate(["mix", "ffn", "pre0", "pre1"])}

        @block.sync
        def _(sp):
            for g in range(KT // 4):
                sp.dma_start(x[:, 4 * g:4 * g + 4, :], x_in[:, 4 * g:4 * g + 4, :])\
                    .then_inc(x_loaded[g], 16)
            for c in range(2):
                sp.dma_start(raw[:, 2 * c:2 * c + 2, :], stream_in[c].rearrange("p (u n) -> p u n", u=2))\
                    .then_inc(raw_ready[c], 16)
            with sp.Fori(1, N_CHUNKS // 2) as i:
                for c in range(2):
                    sp.wait_ge(lo_ready, 4 * i - 2 + 2 * c)
                    sp.dma_start(raw[:, 2 * c:2 * c + 2, :],
                                 stream_in[2 * i + c].rearrange("p (u n) -> p u n", u=2))\
                        .then_inc(raw_ready[c], 16)
            for g in range(KT // 4):
                sp.wait_ge(x_added, KT // 2 + 2 * g + 2)
                sp.wait_ge(x_added_pool, KT // 2 + 2 * g + 2)
                sp.dma_start(out[:, 4 * g:4 * g + 4, :], x[:, 4 * g:4 * g + 4, :]).then_inc(stored, 16)
            sp.wait_ge(stored, 16 * (KT // 4))

        @block.tensor
        def _(pe):
            def unit(name, i, j):
                u, s, _ = unit_of(name, i, j)
                pe.wait_ge(lo_ready, u + 1)
                return s

            def bank(b, name, i, j):
                uses = count(1 + b, name, i, j)
                if i is not None or uses:
                    pe.wait_ge(acc_taken[b], uses)
                return acc[b]

            def tile(out, s, c, hi, lo, k, first, last):
                wc = slice(c * P, (c + 1) * P)
                nc.tensor.matmul(out, w_hi[:, s, wc], hi[:, k, :], start=first, stop=False)
                nc.tensor.matmul(out, w_hi[:, s, wc], lo[:, k, :], start=False, stop=False)
                return nc.tensor.matmul(out, w_lo[:, s, wc], hi[:, k, :], start=False, stop=last)

            def feature_tile(name, i, j, b, use, hi, lo, wait_act=None):
                o = bank(b, name, i, use)[:, 0:T]
                for n in range(2):
                    s = unit(name, i, j + n)
                    for c in range(8):
                        if wait_act is not None and c % 4 == 0:
                            pe.wait_ge(act_ready, wait_act * KT + 8 * n + c + 4)
                        last = tile(o, s, c, hi, lo, 8 * n + c, n + c == 0, 8 * n + c == KT - 1)
                    last.then_inc(unit_done, 1)

            def token_tiles(name, i, j, units, per_unit, width, hi, lo, k0=0):
                n_k = units * per_unit
                uses = count(3, name, i, 0)
                if i is not None or uses:
                    pe.wait_ge(tok_taken, 2 * uses)
                for n in range(units):
                    s = unit(name, i, j + n)
                    for c in range(per_unit):
                        k = n * per_unit + c
                        wc = slice(c * width, (c + 1) * width)
                        for t in range(2):
                            tt = slice(t * P, (t + 1) * P)
                            o = tok[t][:, 0:width]
                            nc.tensor.matmul(o, hi[:, k0 + k, tt], w_hi[:, s, wc], start=k == 0, stop=False)
                            nc.tensor.matmul(o, hi[:, k0 + k, tt], w_lo[:, s, wc], start=False, stop=False)
                            last = nc.tensor.matmul(o, lo[:, k0 + k, tt], w_hi[:, s, wc], start=False,
                                                    stop=k == n_k - 1)
                    last.then_inc(unit_done, 1)

            def norm_sum(n):
                pe.wait_ge(sq_added, KT * (POOLED[n] + 1))
                nc.tensor.matmul(att[3][:, 0:T], ones[:, :], sumsq[:, :], start=True, stop=True)\
                    .then_inc(stat_ready, 1)

            def norm_sum_all(n):
                for k in range(KT):
                    if k % 4 == 0:
                        pe.wait_ge(squares_ready, (n == "pre1") * KT // 4 + k // 4 + 1)
                    last = nc.tensor.matmul(att[3][:, 0:T], ones[:, :], squares_all[:, k, :],
                                            start=k == 0, stop=k == KT - 1)
                last.then_inc(stat_ready, 1)

            pe.wait_ge(const_ready, 4)
            norm_sum_all("mix")

            feature_tile("gates", None, 0, 0, 0, n_hi, n_lo, wait_act=0)
            def mix(i):
                feature_tile("mix", i, 0, 1, 0, n_hi, n_lo)
                feature_tile("mix", i, 2, 0, 0, n_hi, n_lo)
                token_tiles("mix", i, 4, 4, 4, M_DV, n_hi, n_lo)
                taken(pe, 1, "mix", i, 0)
                taken(pe, 0, "mix", i, 0)
                nc.tensor.matmul(att[0][:, 0:T], kT[:, 0:P], qT[:, :], start=True, stop=True)
                nc.tensor.matmul(att[0][:, T:T + P], kT[:, P:T], qT[:, P:T], start=True, stop=True)\
                    .then_inc(scores_ready, 1)
                feature_tile("mix", i, 8, 1, 1, n_hi, n_lo)
                pe.wait_ge(st_ready, 2 * i + 2)
                pe.wait_ge(tok_taken, count(3, "mix", i, 1) * 2)
                for v in range(2):
                    o = att[1][:, v * T:(v + 1) * T]
                    vv = slice(v * P, (v + 1) * P)
                    nc.tensor.matmul(o, vm[:, 0, vv], st0[:, :], start=True, stop=False)
                    nc.tensor.matmul(o[:, P:T], vm[:, 1, vv], st1[:, :], start=False, stop=True)
                nc.tensor.matmul(att[2][:, 0:T], ones[:, :], st0[:, :], start=True, stop=False)
                nc.tensor.matmul(att[2][:, P:T], ones[:, :], st1[:, :], start=False, stop=True)\
                    .then_inc(pv_ready, 1)
                feature_tile("mix", i, 10, 0, 1, n_hi, n_lo)
                feature_tile("mix", i, 12, 1, 2, n_hi, n_lo)
                feature_tile("mix", i, 14, 0, 2, n_hi, n_lo)
                pe.wait_ge(hsum_ready, i + 1)
                nc.tensor.matmul(att[3][:, 0:T], ones[:, :], h_sum[:, :], start=True, stop=True)\
                    .then_inc(hstat_ready, 1)
                feature_tile("mix", i, 16, 1, 3, n_hi, n_lo)
                feature_tile("mix", i, 18, 0, 3, n_hi, n_lo)
                feature_tile("mix", i, 20, 1, 4, n_hi, n_lo)
                feature_tile("mix", i, 22, 0, 4, n_hi, n_lo)

            pe.wait_ge(rows_ready, 1)
            for t in range(2):
                last = nc.tensor.transpose(att[2][:, 4 * t:4 * t + 4], a_row[:, t * P:(t + 1) * P],
                                           ident[0:M_HEADS, 0:M_HEADS])
            last.then_inc(rows_t_ready, 1)
            for hd in range(M_HEADS):
                if hd >= 2:
                    pe.wait_ge(bcast_taken, hd - 1)
                nc.tensor.matmul(att[hd % 2][:, :], head_row[:, hd, :],
                                 mm_row[:, :, :].rearrange("h a t -> h (a t)"),
                                 start=True, stop=True).then_inc(bcast_ready, 1)
            pe.wait_ge(bcast_taken, M_HEADS)
            with pe.Fori(0, M_HEADS) as i:
                mix(i)
            pe.wait_ge(yclo_ready, 2 * M_HEADS)
            pe.wait_ge(hmlo_ready, M_HEADS)
            with pe.Fori(0, KT // 2) as i:
                for m in range(2):
                    feature_tile("merge", i, 6 * m, 1, 2 * m, n_hi, n_lo)
                    feature_tile("merge", i, 6 * m + 2, 0, 2 * m, n_hi, n_lo)
                    for n, (hi, lo) in enumerate(((hm_hi, hm_lo), (yc_hi, yc_lo))):
                        o = bank(1 - n, "merge", i, 2 * m + 1)[:, 0:T]
                        s = unit("merge", i, 6 * m + 4 + n)
                        for c in range(8):
                            last = tile(o, s, c, hi, lo, c, c == 0, c == 7)
                        last.then_inc(unit_done, 1)
            pe.wait_ge(mglo_ready, KT)
            with pe.Fori(0, KT // 2) as i:
                for m in range(2):
                    feature_tile("wout", i, 2 * m, 1 - m, 0, mg_hi, mg_lo)
            norm_sum("ffn")
            def up(i):
                for m in range(2):
                    feature_tile("wup", i, 2 * m, 1 - m, 0, n_hi, n_lo, wait_act=1)

            with pe.Fori(0, F_TILES // 2) as pair:
                up(2 * pair)
                up(2 * pair + 1)
            up(F_TILES - 1)
            pe.wait_ge(flo_ready, F_TILES)
            with pe.Fori(0, KT // 2) as i:
                for m in range(2):
                    o = bank(1 - m, "wdown", i, 0)[:, 0:T]
                    for n in range(6):
                        s = unit("wdown", i, 6 * m + n)
                        for k in range(8 * n, min(8 * n + 8, F_TILES)):
                            last = tile(o, s, k - 8 * n, f_hi, f_lo, k, k == 0, k == F_TILES - 1)
                        last.then_inc(unit_done, 1)
            pe.wait_ge(sq_added, KT * (POOLED["out"] + 1))
            nc.tensor.matmul(att[3][:, 0:T], ones[:, :], sumsq[:, :], start=True, stop=True)
            nc.tensor.matmul(att[3][:, T:2 * T], ones[:, :], sumsq_g[:, :], start=True, stop=True)\
                .then_inc(stat_ready, 1)
            feature_tile("rank", None, 0, 1, 0, n_hi, n_lo, wait_act=2)
            taken(pe, 1, "rank", None, 0)
            pe.wait_ge(gk2_loaded, 16)
            for hd in range(G_HEADS):
                for t in range(2):
                    c = (2 * hd + t) * P
                    last = nc.tensor.matmul(att[hd][:, t * T:(t + 1) * T], gk2[:, c:c + P],
                                            rank_rows[0:G_RANK + 1, :], start=True, stop=True)
                last.then_inc(gk_ready, 1)
            with pe.Fori(0, G_HEADS) as i:
                for n in range(4):
                    feature_tile("gla", i, 2 * n, n % 2, n // 2, n_hi, n_lo)
                token_tiles("gla", i, 8, 8, 2, G_DV, n_hi, n_lo)
                pe.wait_ge(gk_taken, G_HEADS)
                pe.wait_ge(qx_ready, 4 * i + 4)
                pe.wait_ge(kk_ready, 2 * i + 2)
                for kc in range(4):
                    part = slice(CHUNK * (kc % 2), CHUNK * (kc % 2 + 1))
                    col = T * (kc // 2)
                    src = slice(CHUNK * kc, CHUNK * (kc + 1))
                    nxt = slice(CHUNK * (kc + 1), CHUNK * (kc + 2))
                    jobs = [(k_e, src, q_e, src, CHUNK * kc)]
                    if kc < 3:
                        jobs.append((k_l, src, q_e, nxt, CHUNK * (kc + 1)))
                    if kc == 0:
                        jobs.append((k_l, src, q_x, slice(0, 2 * CHUNK), 2 * CHUNK))
                    if kc == 1:
                        jobs.append((k_l, src, q_y, slice(0, CHUNK), 3 * CHUNK))
                    for keys, ks, queries, qs, at in jobs:
                        width = qs.stop - qs.start
                        for dk in range(2):
                            last = nc.tensor.matmul(att[0][part, col + at:col + at + width],
                                                    keys[:, dk, ks], queries[:, dk, qs],
                                                    start=dk == 0, stop=dk == 1)
                last.then_inc(gscores_ready, 1)
                feature_tile("gla", i, 16, 0, 2, n_hi, n_lo)
                pe.wait_ge(at_ready, 5 * i + 5)
                pe.wait_ge(tok_taken, 2 * count(3, "gla", i, 1))
                for v in range(4):
                    o = att[1 + v // 2][:, (v % 2) * T:(v % 2 + 1) * T]
                    vv = slice(v * P, (v + 1) * P)
                    nc.tensor.matmul(o, vg[:, 0, vv], a_t[:, 0, :], start=True, stop=False)
                    last = nc.tensor.matmul(o[:, P:T], vg[:, 1, vv], a_t[:, 1, P:T], start=False, stop=True)
                last.then_inc(gpv_ready, 1)
                feature_tile("gla", i, 18, 1, 2, n_hi, n_lo)
                feature_tile("gla", i, 20, 0, 3, n_hi, n_lo)
                pe.wait_ge(osum_ready, i + 1)
                nc.tensor.matmul(att[3][:, 0:T], ones[:, :], o_sum[:, :], start=True, stop=True)\
                    .then_inc(ostat_ready, 1)
                feature_tile("gla", i, 22, 1, 3, n_hi, n_lo)
            pe.wait_ge(oglo_ready, G_HEADS)
            with pe.Fori(0, KT // 2) as i:
                for m in range(2):
                    feature_tile("glaout", i, 2 * m, m, 0, og_hi, og_lo)
            norm_sum("post0")
            norm_sum_all("pre1")
            with pe.Fori(0, A_TILES) as i:
                for m in range(2):
                    feature_tile("latent", i, 2 * m, m, 0, n_hi, n_lo, wait_act=3)
            feature_tile("krope", None, 0, 0, 0, n_hi, n_lo)
            pe.wait_ge(lsq_added, 2 * A_TILES)
            nc.tensor.matmul(att[3][:, :], ones[:, :], l_sumsq[:, :, :].rearrange("p a t -> p (a t)"),
                             start=True, stop=True).then_inc(lstat_ready, 1)
            feature_tile("krope", None, 2, 1, 0, n_hi, n_lo)
            def pair_tile(i, j, b, use, k0):
                o = bank(b, "mla", i, use)
                s = unit("mla", i, j)
                for c in range(8):
                    m, k = divmod(c, A_TILES)
                    last = tile(o[:, m * T:(m + 1) * T], s, c, c_hi, c_lo, k0 + k, k == 0,
                                k == A_TILES - 1)
                return last

            def scores(i, n):
                pe.wait_ge(ptr_ready, 4 * i + max(n - 1, 0))
                for t, (at, width) in enumerate(((0, P), (P, T))):
                    tt = slice(t * P, (t + 1) * P)
                    o = att[n % 2][:, at:at + width]
                    nc.tensor.matmul(o, qn[:, n, tt], kn[:, n, 0:width], start=True, stop=False)
                    nc.tensor.matmul(o, q_rope[:, 0, tt], kr_m[:, 0, n, 0:width], start=False, stop=False)
                    last = nc.tensor.matmul(o, q_rope[:, 1, tt], kr_m[:, 1, n, 0:width],
                                            start=False, stop=True)
                last.then_inc(logits_ready, 1)

            def transposes(i, n):
                pe.wait_ge(probs_ready, 4 * i + n + 1)
                for b in range(3):
                    last = nc.tensor.transpose(att[n % 2][:, b * P:(b + 1) * P],
                                               probs[:, n % 2, b * P:(b + 1) * P], ident[:, :])
                last.then_inc(ptp_ready, 1)

            def outputs(i, n):
                pe.wait_ge(aout_ready, 4 * i + 2 * (n // 2))
                pe.wait_ge(ptr_ready, 4 * i + n + 1)
                o = att[2 + n % 2][:, 0:T]
                vv = slice(n * A_V, (n + 1) * A_V)
                nc.tensor.matmul(o, va[:, 0, vv], probs_t[:, n % 2, 0:T], start=True, stop=False)
                nc.tensor.matmul(o[:, P:T], va[:, 1, vv], probs_t[:, n % 2, T:3 * P], start=False, stop=True)\
                    .then_inc(apv_ready, 1)

            pe.wait_ge(c_ready, 2 * A_TILES)
            pe.wait_ge(krm_ready, 8)
            with pe.Fori(0, A_HEADS // 4) as i:
                for n in range(2):
                    pair_tile(i, 2 * n, 0, n, 0).then_inc(unit_done, 1)
                    pair_tile(i, 2 * n + 1, 1, n, A_TILES).then_inc(unit_done, 1)
                last = pair_tile(i, 4, 0, 2, 0)
                unit("mla", i, 5)
                last.then_inc(unit_done, 2)
                token_tiles("mla", i, 6, 2, 2, 4 * A_V, c_hi, c_lo, k0=A_TILES)
                taken(pe, 0, "mla", i, 2)
                taken(pe, 1, "mla", i, 1)
                pe.wait_ge(qrope_ready, 2 * i + 2)
                scores(i, 0)
                scores(i, 1)
                feature_tile("mla", i, 8, 1, 2, n_hi, n_lo)
                transposes(i, 0)
                transposes(i, 1)
                feature_tile("mla", i, 10, 0, 3, n_hi, n_lo)
                pe.wait_ge(tok_taken, 2 * count(3, "mla", i, 1))
                outputs(i, 0)
                outputs(i, 1)
                scores(i, 2)
                scores(i, 3)
                feature_tile("mla", i, 12, 1, 3, n_hi, n_lo)
                transposes(i, 2)
                transposes(i, 3)
                feature_tile("mla", i, 14, 0, 4, n_hi, n_lo)
                outputs(i, 2)
                outputs(i, 3)
            pe.wait_ge(molo_ready, A_HEADS)
            with pe.Fori(0, KT // 2) as i:
                for m in range(2):
                    feature_tile("mlaout", i, 2 * m, 1 - m, 0, mo_hi, mo_lo)
            norm_sum("post1")

        @block.scalar
        def _(act):
            chain = Chain(act, act_step)

            def split(name, i, j):
                u, s, use = unit_of(name, i, j + RING)
                high(u, s, use)

            def high(u, s, use):
                if s % 2 == 0:
                    act.wait_ge(raw_ready[s // 2], 16 * use + 16)
                if not isinstance(u, int) or u >= RING:
                    act.wait_ge(unit_done, u - RING + 1)
                nc.scalar.activation(w_hi[:, s, :], raw[:, s, :], ACT.Copy).then_inc(hi_ready, 1)

            def unit_is_done(name, i, j):
                act.wait_ge(unit_done, unit_of(name, i, j)[0] + 1)

            def one_square(n, i, m, source, gain=None):
                act.wait_ge(sq_added, 2 * i + max(POOLED[n] * KT + m - 1, 0))
                ins = nc.scalar.activation(square[:, m, :], source, ACT.Square)
                if gain is not None:
                    ins = nc.scalar.activation(square_g[:, m, :], source, ACT.Square, scale=gain)
                ins.then_inc(sq_ready, 1)

            def norm_std(n):
                act.wait_ge(stat_ready, STAT[n] + 1)
                if NORM[n]:
                    act.wait_ge(rstd_ready, NORM[n])
                nc.scalar.activation(std[:, :], att[3][:, 0:T], ACT.Sqrt, bias=eps, scale=1.0 / D)\
                    .then_inc(std_ready, 1)

            def four_high(n, g):
                for m in range(4):
                    act.wait_ge(normed_ready, 4 * g + TO_ACT[n] * KT + m + 1)
                    nc.scalar.activation(n_hi[:, 4 * g + m, :], normed[:, m, :], ACT.Copy)\
                        .then_inc(nhi_ready, 1)

            def norm_high(n):
                with act.Fori(0, KT // 4) as g:
                    four_high(n, g)

            act.dma_start(par[:, :], params_in).then_inc(loaded, 16)
            act.dma_start(pos_i[:, :], positions_in.to_broadcast([P, T])).then_inc(pos_loaded, 16)
            act.dma_start(v_bias[:, :, :].rearrange("p h v -> p (h v)"),
                          v_bias_in.to_broadcast([P, M_HEADS * M_DV])).then_inc(bias_loaded, 16)
            eps = eps_col[:, :]
            for g in range(KT // 4):
                act.wait_ge(x_loaded[g], 16)
                nc.scalar.activation(squares_all[:, 4 * g:4 * g + 4, :], x[:, 4 * g:4 * g + 4, :],
                                     ACT.Square).then_inc(squares_ready, 1)
            act.wait_ge(const_ready, 1)
            norm_std("mix")
            for g in range(RING):
                four_high("mix", g)
                high(g, g, 0)

            act.wait_ge(rope_red, 1)
            nc.scalar.activation(sine[:, :], red[:, 0, :], ACT.Sin).then_inc(rope_ready, 1)
            nc.scalar.activation(cosine[:, :], red[:, 1, :], ACT.Sin).then_inc(rope_ready, 1)

            unit_is_done("gates", None, 1)
            nc.scalar.activation(i_row[0:32, :], acc[0][0:32, 0:T], ACT.Identity,
                                 bias=pcols("b_gate")[0:32, :]).then_inc(row_pre, 1)
            nc.scalar.activation(f_row[32:64, :], acc[0][32:64, 0:T], ACT.Identity,
                                 bias=pcols("b_gate")[32:64, :]).then_inc(acc_taken[0], 1)
            taken(act, 0, "gates", None, 0)
            chain.link(nc.scalar.activation(f_abs[32:64, :], f_row[32:64, :], ACT.Abs))
            chain.link(nc.scalar.activation(f_exp[32:64, :], f_abs[32:64, :], ACT.Exp, scale=-1.0))
            nc.scalar.activation(f_log[32:64, :], f_exp[32:64, :], ACT.Ln, bias=1.0).then_inc(row_log, 1)
            split("gates", None, 0)
            split("gates", None, 1)
            act.wait_ge(rows_t_ready, 1)
            chain.link(nc.scalar.activation(a_col[:, :, :].rearrange("p t h -> p (t h)"),
                                            att[2][:, 0:2 * M_HEADS], ACT.Copy))
            for hd in range(M_HEADS):
                act.wait_ge(bcast_ready, hd + 1)
                rows = att[hd % 2]
                nc.scalar.activation(decay0[:, hd, :], rows[:, 0:T], ACT.Exp, scale=-1.0,
                                     bias=a_col[:, 0, hd:hd + 1]).then_inc(a_col_ready, 1)
                nc.scalar.activation(decay1[:, hd, :], rows[:, P:T], ACT.Exp, scale=-1.0,
                                     bias=a_col[:, 1, hd:hd + 1]).then_inc(a_col_ready, 1)
                nc.scalar.activation(floor[:, hd, :], rows[:, T:2 * T], ACT.Exp, scale=-1.0)\
                    .then_inc(bcast_taken, 1)
            with act.Fori(0, M_HEADS) as i:
                for j in range(24):
                    if j == 1:
                        unit_is_done("mix", i, j)
                        nc.scalar.activation(qT[:, :], acc[1][:, 0:T], ACT.Identity,
                                             bias=par_mix[:, i, 0:1]).then_inc(acc_taken[1], 1)
                    if j == 3:
                        unit_is_done("mix", i, j)
                        nc.scalar.activation(kT[:, :], acc[0][:, 0:T], ACT.Identity,
                                             bias=par_mix[:, i, 1:2]).then_inc(acc_taken[0], 1)
                    if j in (9, 11):
                        n = (j - 9) // 2
                        unit_is_done("mix", i, j)
                        if n == 0:
                            act.wait_ge(hm_ready, 2 * i)
                        nc.scalar.activation(sig_o[:, n, :], acc[1 - n][:, 0:T], ACT.Sigmoid,
                                             bias=par_mix[:, i, 2 + n:3 + n]).then_inc(acc_taken[1 - n], 1)
                    if j == 10:
                        act.wait_ge(pv_ready, i + 1)
                        nc.scalar.activation(den_abs[:, :], att[2][:, 0:T], ACT.Abs)\
                            .then_inc(den_ready, 1)
                    if j in (13, 19):
                        n = (j - 13) // 6
                        unit_is_done("mix", i, j)
                        if n == 1:
                            taken(act, 0, "mix", i, 2)
                        nc.scalar.activation(cc[:, :], acc[1 - n][:, 0:T], ACT.Identity,
                                             bias=par_mix[:, i, 4 + 3 * n:5 + 3 * n])\
                            .then_inc(acc_taken[1 - n], 1)
                    if j == 12:
                        act.wait_ge(h_ready, i + 1)
                        nc.scalar.activation(h_sq[:, :, :], h[:, :, :], ACT.Square).then_inc(hsq_ready, 1)
                    if j == 16:
                        act.wait_ge(hstat_ready, i + 1)
                        nc.scalar.activation(h_std[:, :], att[3][:, 0:T], ACT.Sqrt, bias=eps,
                                             scale=1.0 / M_DV).then_inc(hstd_ready, 1)
                    if j == 18:
                        act.wait_ge(hm_ready, 2 * i + 2)
                        nc.scalar.activation(hm_hi[:, bass.ds(2 * i, 2), :], hm[:, :, :], ACT.Copy)\
                            .then_inc(hmhi_ready, 1)
                    if j in (19, 23):
                        n = (j - 19) // 4
                        taken(act, 1 - n, "mix", i, 3 + n)
                        nc.scalar.activation(yc_hi[:, 2 * i + n, :], cz[:, :], ACT.Copy)\
                            .then_inc(ychi_ready, 1)
                    split("mix", i, j)
            with act.Fori(0, KT // 2) as i:
                for j in range(12):
                    m, jj = divmod(j, 6)
                    if jj in (1, 3):
                        n = jj // 2
                        unit_is_done("merge", i, j)
                        act.wait_ge(acc_taken[1 - n], count(2 - n, "merge", i, 2 * m))
                        nc.scalar.activation((sig_m, sig_c)[n][:, :], acc[1 - n][:, 0:T], ACT.Sigmoid,
                                             bias=par_merge[:, i, 2 * m + n:2 * m + n + 1])\
                            .then_inc(acc_taken[1 - n], 1)
                    if jj == 5:
                        act.wait_ge(merged_ready, 2 * i + m + 1)
                        nc.scalar.activation(mg_hi[:, 2 * i + m, :], merged[:, :], ACT.Copy)\
                            .then_inc(mghi_ready, 1)
                    split("merge", i, j)

            def residual_squares(name, n, per, gain=None):
                with act.Fori(0, KT // 2) as i:
                    for j in range(per):
                        if j in (per // 2 - 1, per - 1):
                            m = 2 * j // per
                            taken(act, 1 - m, name, i, 0)
                            one_square(n, i, m, x[:, 2 * i + m, :],
                                       gains(gain)[:, i, m:m + 1] if gain else None)
                        split(name, i, j)

            residual_squares("wout", "ffn", 4)
            norm_std("ffn")
            norm_high("ffn")
            with act.Fori(0, F_TILES) as i:
                for j in range(4):
                    if j in (1, 3):
                        n = j // 2
                        unit_is_done("wup", i, j)
                        if n == 0:
                            act.wait_ge(fsilu_ready, i)
                        else:
                            act.wait_ge(fact_ready, i)
                        nc.scalar.activation((f_gate, f_val)[n][:, :], acc[1 - n][:, 0:T], ACT.Identity,
                                             bias=par_ffn[:, i, 4 * n + 3:4 * n + 4],
                                             scale=par_ffn[:, i, 4 * n + 2:4 * n + 3])
                        nc.scalar.activation(f_pre[:, n, :], acc[1 - n][:, 0:T], ACT.Copy)\
                            .then_inc(acc_taken[1 - n], 1)
                    if j == 2:
                        act.wait_ge(ftap_ready, 2 * i + 1)
                        act.wait_ge(fact_ready, i)
                        nc.scalar.activation(f_silu[:, :], f_gate[:, :], ACT.Silu)\
                            .then_inc(fsilu_ready, 1)
                    split("wup", i, j)
                    if j == 3:
                        act.wait_ge(fact_ready, i + 1)
                        nc.scalar.activation(f_hi[:, i, :], f_act[:, :], ACT.Copy)\
                            .then_inc(fhi_ready, 1)
            residual_squares("wdown", "out", 12, "g_out")
            norm_std("out")
            act.wait_ge(mean_ready, 1)
            nc.scalar.activation(std[:, :], mean_g[:, :], ACT.Sqrt, bias=eps, scale=1.0 / D)\
                .then_inc(std_ready, 1)
            norm_high("pre0")
            act.dma_start(gk2[:, :], gk2_in).then_inc(gk2_loaded, 16)
            act.wait_ge(rank_ones, 1)
            unit_is_done("rank", None, 1)
            nc.scalar.activation(rank_rows[0:G_RANK, :], acc[1][0:G_RANK, 0:T], ACT.Copy)\
                .then_inc(acc_taken[1], 1)
            for hd in range(G_HEADS):
                act.wait_ge(gk_ready, hd + 1)
                chain.link(nc.scalar.activation(g_abs[:, :], att[hd][:, :], ACT.Abs))
                chain.link(nc.scalar.activation(g_exp[:, :], g_abs[:, :], ACT.Exp, scale=-1.0))
                if hd:
                    act.wait_ge(gcum_ready, hd)
                nc.scalar.activation(g_log[:, :], g_exp[:, :], ACT.Ln, bias=1.0).then_inc(glog_ready, 1)
                if hd % 2:
                    split("rank", None, hd // 2)
            act.wait_ge(gcum_ready, G_HEADS)
            with act.Fori(0, G_HEADS) as i:
                for j in range(24):
                    if j == 0:
                        act.wait_ge(qx_ready, 4 * i)
                        act.wait_ge(kk_ready, 2 * i)
                        nc.scalar.activation(e_pos[:, :, :], gcum[:, i, :, :], ACT.Exp,
                                             scale=1.0 / G_TAU).then_inc(decays_ready, 1)
                        nc.scalar.activation(e_neg[:, :, :], gcum[:, i, :, :], ACT.Exp,
                                             scale=-1.0 / G_TAU).then_inc(decays_ready, 1)
                        act.wait_ge(to_end_ready, i + 1)
                        nc.scalar.activation(e_end[:, :, :], to_end[:, :, :], ACT.Exp,
                                             scale=1.0 / G_TAU).then_inc(decays_ready, 1)
                    if j in (5, 7):
                        n = (j - 5) // 2
                        unit_is_done("gla", i, j)
                        nc.scalar.activation(k_sb[:, n, :], acc[n][:, 0:T], ACT.Copy)\
                            .then_inc(acc_taken[n], 1)
                    if j == 18:
                        act.wait_ge(gpv_ready, i + 1)
                        act.wait_ge(og_ready, i)
                        for n in range(2):
                            nc.scalar.activation(o_sb[:, 2 * n:2 * n + 2, :], att[1 + n][:, :], ACT.Copy)\
                                .then_inc(osb_ready, 1)
                        for n in range(2):
                            nc.scalar.activation(o_sq[:, 2 * n:2 * n + 2, :], att[1 + n][:, :], ACT.Square)\
                                .then_inc(osq_ready, 1)
                    if j in (17, 19, 21, 23):
                        n = (j - 17) // 2
                        unit_is_done("gla", i, j)
                        if n == 0:
                            act.wait_ge(og_ready, i)
                        nc.scalar.activation(o_sg[:, n, :], acc[n % 2][:, 0:T], ACT.Silu)\
                            .then_inc(acc_taken[n % 2], 1)
                    if j == 22:
                        act.wait_ge(ostat_ready, i + 1)
                        nc.scalar.activation(o_std[:, :], att[3][:, 0:T], ACT.Sqrt, bias=eps,
                                             scale=1.0 / G_DV).then_inc(ostd_ready, 1)
                    if j == 23:
                        act.wait_ge(og_ready, i + 1)
                        nc.scalar.activation(og_hi[:, bass.ds(4 * i, 4), :], o_norm[:, :, :], ACT.Copy)\
                            .then_inc(oghi_ready, 1)
                    split("gla", i, j)

            def mixer_output(name, n, to, flip, last_phase=False):
                def body(i, splits):
                    for j in range(4):
                        if j in (1, 3):
                            m = j // 2
                            unit_is_done(name, i, j)
                            b = 1 - m if flip else m
                            one_square(n, i, m, acc[b][:, 0:T])
                            nc.scalar.activation(to[:, 2 * i + m, :], acc[b][:, 0:T], ACT.Copy)\
                                .then_inc(acc_taken[b], 1)
                        if splits:
                            split(name, i, j)

                with act.Fori(0, KT // 2 - last_phase) as i:
                    body(i, True)
                if last_phase:
                    body(KT // 2 - 1, False)

            mixer_output("glaout", "post0", y, False)
            norm_std("post0")
            for g in range(KT // 4):
                act.wait_ge(x_added, 2 * g + 2)
                act.wait_ge(x_added_pool, 2 * g + 2)
                nc.scalar.activation(squares_all[:, 4 * g:4 * g + 4, :], x[:, 4 * g:4 * g + 4, :],
                                     ACT.Square).then_inc(squares_ready, 1)
            norm_std("pre1")
            norm_high("pre1")
            with act.Fori(0, A_TILES) as i:
                for j in range(4):
                    if j in (1, 3):
                        n = j // 2
                        unit_is_done("latent", i, j)
                        nc.scalar.activation(latent[:, n, i, :], acc[n][:, 0:T], ACT.Copy)
                        act.wait_ge(lsq_added, 2 * i)
                        nc.scalar.activation(l_square[:, n, :], acc[n][:, 0:T], ACT.Square)\
                            .then_inc(acc_taken[n], 1)
                    split("latent", i, j)
            for j in range(4):
                if j in (1, 3):
                    n = j // 2
                    unit_is_done("krope", None, j)
                    nc.scalar.activation(kr[:, n, :], acc[n][:, 0:T], ACT.Copy).then_inc(acc_taken[n], 1)
                if j == 2:
                    act.wait_ge(lstat_ready, 1)
                    nc.scalar.activation(l_std[:, :, :], att[3][:, :], ACT.Sqrt, bias=eps,
                                         scale=1.0 / A_RANK).then_inc(lstd_ready, 1)
                    for k in range(2 * A_TILES):
                        act.wait_ge(cnormed_ready, k + 1)
                        nc.scalar.activation(c_hi[:, k, :], normed[:, k % 2, :], ACT.Copy)\
                            .then_inc(chi_ready, 1)
                split("krope", None, j)
            with act.Fori(0, A_HEADS // 4) as i:
                for j in range(16):
                    if j in (0, 2):
                        n = j // 2
                        unit_is_done("mla", i, j)
                        nc.scalar.activation(qn[:, 2 * n:2 * n + 2, :], acc[0][:, :], ACT.Copy)\
                            .then_inc(acc_taken[0], 1)
                    if j == 4:
                        unit_is_done("mla", i, j)
                        act.wait_ge(qrope_ready, 2 * i)
                        nc.scalar.activation(q_r[:, :, :], acc[0][:, :], ACT.Copy)\
                            .then_inc(acc_taken[0], 1)
                    if j in (8, 12):
                        for n in range((j - 8) // 2, (j - 8) // 2 + 2):
                            act.wait_ge(neg_ready, 4 * i + n + 1)
                            for t, blocks in enumerate((slice(0, P), slice(P, 3 * P))):
                                nc.scalar.activation(probs[:, n % 2, blocks], logits[:, n % 2, blocks],
                                                     ACT.Exp, bias=neg_max[:, n % 2, t:t + 1],
                                                     accum_out=row_sum[:, n % 2, t:t + 1])\
                                    .then_inc(exp_ready, 1)
                    if j in (10, 14):
                        for n in range((j - 10) // 2, (j - 10) // 2 + 2):
                            act.wait_ge(ptp_ready, 4 * i + n + 1)
                            nc.scalar.activation(probs_t[:, n % 2, :], att[n % 2][:, 0:3 * P], ACT.Copy)\
                                .then_inc(ptr_ready, 1)
                    if j in (9, 11, 13, 15):
                        n = (j - 9) // 2
                        unit_is_done("mla", i, j)
                        if n == 0:
                            act.wait_ge(aout_ready, 4 * i)
                        b = 1 - n % 2
                        nc.scalar.activation(a_gate[:, n, :], acc[b][:, 0:T], ACT.Silu)\
                            .then_inc(acc_taken[b], 1)
                    if j in (13, 15):
                        for n in range(j - 13, j - 11):
                            act.wait_ge(aout_ready, 4 * i + n + 1)
                            nc.scalar.activation(mo_hi[:, 4 * i + n, :], a_out[:, n, :], ACT.Copy)\
                                .then_inc(mohi_ready, 1)
                    split("mla", i, j)
            mixer_output("mlaout", "post1", y2, True, last_phase=True)
            norm_std("post1")

        @block.vector
        def _(dve):
            chain = Chain(dve, dve_step)

            def split(name, i, j):
                u, s, _ = unit_of(name, i, j + RING)
                rest(u, s)

            def rest(u, s):
                dve.wait_ge(hi_ready, u + 1)
                nc.vector.tensor_tensor(w_lo[:, s, :], raw[:, s, :], w_hi[:, s, :].bitcast(fp32),
                                        ALU.subtract).then_inc(lo_ready, 1)

            def unit_is_done(name, i, j):
                dve.wait_ge(unit_done, unit_of(name, i, j)[0] + 1)

            def norm_rstd(n):
                dve.wait_ge(std_ready, NORM[n] + 1)
                nc.vector.reciprocal(rstd[:, :], std[:, :]).then_inc(rstd_ready, 1)
                dve.wait_ge(rstd_ready, NORM[n] + 1)

            def four_normed(n, g, gain, scale):
                at = TO_ACT[n] * KT
                for m in range(4):
                    dve.wait_ge(act_ready, 4 * g + max(at + m - 3, 0))
                    nc.vector.scalar_tensor_tensor(
                        out=normed[:, m, :], in0=x[:, 4 * g + m, :], scalar=gain[:, g, m:m + 1],
                        in1=scale[:, :], op0=ALU.mult, op1=ALU.mult).then_inc(normed_ready, 1)

            def norm_tiles(n, gain, scale):
                with dve.Fori(0, KT // 4) as g:
                    four_normed(n, g, gain, scale)

            dve.wait_ge(loaded, 16)
            dve.wait_ge(pos_loaded, 16)
            chain.link(nc.vector.tensor_scalar(ang[:, :], pos_i[:, :], pcols("inv_freq"), None, ALU.mult))
            chain.link(nc.vector.tensor_scalar(turns_i[:, :], ang[:, :], 0.15915494309189535, None, ALU.mult))
            chain.link(nc.vector.tensor_copy(turns[:, :], turns_i[:, :]))
            source = ang[:, :]
            for part in (6.28125, 0.0019340515136718750, 1.2556659146e-06):
                chain.link(nc.vector.scalar_tensor_tensor(out=red[:, 0, :], in0=turns[:, :], scalar=-part,
                                                          in1=source, op0=ALU.mult, op1=ALU.add))
                source = red[:, 0, :]
            chain.link(nc.vector.tensor_scalar(red[:, 1, :], red[:, 0, :], 1.5707963267948966, None, ALU.add))
            for compare, edge, turn in ((ALU.is_gt, PI, -2 * PI), (ALU.is_lt, -PI, 2 * PI)):
                chain.link(nc.vector.tensor_scalar(wrap[:, :, :], red[:, :, :], edge, turn, compare, ALU.mult))
                chain.link(nc.vector.tensor_tensor(red[:, :, :], red[:, :, :], wrap[:, :, :], ALU.add))
            nc.vector.tensor_scalar(red[:, :, :], red[:, :, :], -PI_INSIDE, PI_INSIDE, ALU.max, ALU.min)\
                .then_inc(rope_red, 1)
            nc.vector.tensor_tensor(g_both[:, :], pcols("g_out"), pcols("g_pre0"), ALU.mult)\
                .then_inc(gains_ready, 1)
            norm_rstd("mix")
            for g in range(RING):
                four_normed("mix", g, fours(pcols("g_mix")), rstd)
                rest(g, g)
            dve.wait_ge(row_log, 1)
            chain.link(nc.vector.tensor_scalar(f_min[32:64, :], f_row[32:64, :], 0.0, None, ALU.min))
            chain.link(nc.vector.tensor_tensor(logf[32:64, :], f_min[32:64, :], f_log[32:64, :],
                                               ALU.subtract))
            chain.link(nc.vector.tensor_copy(logf0[:, :], logf[32:32 + M_HEADS, :]))
            chain.link(nc.vector.memset(ones_row[:, :], 1.0))
            chain.link(nc.vector.tensor_tensor_scan(b_row[:, :], ones_row[:, :], logf0[:, :], 0.0,
                                                    ALU.mult, ALU.add))
            dve.wait_ge(row_pre, 1)
            chain.link(nc.vector.tensor_tensor(a_row[:, :], i_row[0:M_HEADS, :], b_row[:, :], ALU.subtract))
            chain.link(nc.vector.tensor_tensor_scan(mm_row[:, 0, :], a_row[:, :], a_row[:, :], 0.0,
                                                    ALU.max, ALU.max))
            nc.vector.tensor_tensor(mm_row[:, 1, :], mm_row[:, 0, :], b_row[:, :], ALU.add)\
                .then_inc(rows_ready, 1)
            split("gates", None, 0)
            split("gates", None, 1)

            dve.wait_ge(bias_loaded, 16)
            dve.wait_ge(decay_masked, 2)
            with dve.Fori(0, M_HEADS) as i:
                chain.loop(i, 10)
                for j in range(24):
                    if j == 7:
                        unit_is_done("mix", i, j)
                        for t in range(2):
                            nc.vector.tensor_tensor(vm[:, t, :], tok[t][:, 0:M_DV], v_bias[:, i, :],
                                                    ALU.add).then_inc(tok_taken, 1)
                    if j == 8:
                        dve.wait_ge(scores_ready, i + 1)
                        nc.vector.scalar_tensor_tensor(out=st0[:, :], in0=att[0][:, 0:T],
                                                       scalar=M_DQK ** -0.5, in1=decay0[:, i, :],
                                                       op0=ALU.mult, op1=ALU.mult).then_inc(st_ready, 1)
                        nc.vector.scalar_tensor_tensor(out=st1[:, :], in0=att[0][:, T:T + P],
                                                       scalar=M_DQK ** -0.5, in1=decay1[:, i, :],
                                                       op0=ALU.mult, op1=ALU.mult).then_inc(st_ready, 1)
                    if j == 10:
                        dve.wait_ge(den_ready, i + 1)
                        chain.link(nc.vector.tensor_tensor(den[:, :], den_abs[:, :], floor[:, i, :],
                                                           ALU.max))
                        chain.link(nc.vector.reciprocal(rden[:, :], den[:, :]))
                        for v in range(2):
                            ins = nc.vector.tensor_tensor(h[:, v, :], att[1][:, v * T:(v + 1) * T],
                                                          rden[:, :], ALU.mult)
                            if v == 0:
                                chain.link(ins)
                            else:
                                ins.then_inc(h_ready, 1)
                    if j in (15, 21):
                        n = (j - 15) // 6
                        unit_is_done("mix", i, j)
                        taken(dve, 1 - n, "mix", i, 2 + n)
                        nc.vector.scalar_tensor_tensor(
                            out=cu[:, :], in0=acc[n][:, 0:T], scalar=par_mix[:, i, 5 + 3 * n:6 + 3 * n],
                            in1=cc[:, :], op0=ALU.add, op1=ALU.mult).then_inc(acc_taken[n], 1)
                        taken(dve, n, "mix", i, 2 + 2 * n)
                        chain.link(nc.vector.tensor_scalar(cy[:, :], cu[:, :],
                                                           par_conv[:, i, 3 * n + 2:3 * n + 3], None,
                                                           ALU.mult))
                        for back, w in ((1, 1), (2, 0)):
                            chain.link(nc.vector.scalar_tensor_tensor(
                                out=cy[:, back:T], in0=cu[:, 0:T - back],
                                scalar=par_conv[:, i, 3 * n + w:3 * n + w + 1], in1=cy[:, back:T],
                                op0=ALU.mult, op1=ALU.add))
                    if j == 17 or j == 23:
                        n = (j - 17) // 6
                        unit_is_done("mix", i, j)
                        dve.wait_ge(yclo_ready, 2 * i + n)
                        nc.vector.scalar_tensor_tensor(
                            out=cz[:, :], in0=acc[1 - n][:, 0:T],
                            scalar=par_mix[:, i, 6 + 3 * n:7 + 3 * n],
                            in1=cy[:, :], op0=ALU.add, op1=ALU.mult).then_inc(acc_taken[1 - n], 1)
                    if j == 17:
                        dve.wait_ge(hstd_ready, i + 1)
                        chain.link(nc.vector.reciprocal(h_rstd[:, :], h_std[:, :]))
                        dve.wait_ge(hmlo_ready, i)
                        taken(dve, 0, "mix", i, 1)
                        for v in range(2):
                            nc.vector.scalar_tensor_tensor(
                                out=h_norm[:, v, :], in0=h[:, v, :], scalar=par_head[:, i, v:v + 1],
                                in1=h_rstd[:, :], op0=ALU.mult, op1=ALU.mult).then_inc(h_normed, 1)
                        for v in range(2):
                            dve.wait_ge(h_normed, 2 * i + v + 1)
                            nc.vector.tensor_tensor(hm[:, v, :], h_norm[:, v, :], sig_o[:, v, :],
                                                    ALU.mult).then_inc(hm_ready, 1)
                    split("mix", i, j)
                chain.done(M_HEADS)
            with dve.Fori(0, KT // 2) as i:
                for j in range(12):
                    m, jj = divmod(j, 6)
                    if jj in (4, 5):
                        n = jj - 4
                        unit_is_done("merge", i, j)
                        taken(dve, 1 - n, "merge", i, 2 * m)
                        dve.wait_ge(merged_ready, 2 * i + m)
                        nc.vector.tensor_tensor((part_m, part_c)[n][:, :], acc[1 - n][:, 0:T],
                                                (sig_m, sig_c)[n][:, :], ALU.mult)\
                            .then_inc(acc_taken[1 - n], 1)
                    split("merge", i, j)

            def residual(name, per):
                with dve.Fori(0, KT // 2) as i:
                    for j in range(per):
                        if j in (per // 2 - 1, per - 1):
                            m = 2 * j // per
                            unit_is_done(name, i, j)
                            nc.vector.tensor_tensor(x[:, 2 * i + m, :], acc[1 - m][:, 0:T],
                                                    x[:, 2 * i + m, :], ALU.add)\
                                .then_inc(acc_taken[1 - m], 1)
                        split(name, i, j)

            residual("wout", 4)
            norm_rstd("ffn")
            norm_tiles("ffn", fours(pcols("g_ffn")), rstd)
            with dve.Fori(0, F_TILES) as i:
                chain.loop(i, 2)
                for j in range(4):
                    if j in (1, 3):
                        n = j // 2
                        u = (f_gate, f_val)[n]
                        taken(dve, 1 - n, "wup", i, 0)
                        src = f_pre[:, n, :]
                        chain.link(nc.vector.scalar_tensor_tensor(
                            out=u[:, 1:T], in0=src[:, 0:T - 1],
                            scalar=par_ffn[:, i, 4 * n + 1:4 * n + 2], in1=u[:, 1:T],
                            op0=ALU.mult, op1=ALU.add))
                        nc.vector.scalar_tensor_tensor(
                            out=u[:, 2:T], in0=src[:, 0:T - 2],
                            scalar=par_ffn[:, i, 4 * n:4 * n + 1], in1=u[:, 2:T],
                            op0=ALU.mult, op1=ALU.add).then_inc(ftap_ready, 1)
                    if j == 3:
                        dve.wait_ge(fsilu_ready, i + 1)
                        dve.wait_ge(ftap_ready, 2 * i + 2)
                        dve.wait_ge(flo_ready, i)
                        nc.vector.tensor_tensor(f_act[:, :], f_silu[:, :], f_val[:, :], ALU.mult)\
                            .then_inc(fact_ready, 1)
                    split("wup", i, j)
                chain.done(F_TILES)
            residual("wdown", 12)
            norm_rstd("out")
            chain.link(nc.vector.tensor_tensor(mean_part[:, :], att[3][:, T:2 * T], rstd[:, :], ALU.mult))
            nc.vector.tensor_tensor(mean_g[:, :], mean_part[:, :], rstd[:, :], ALU.mult)\
                .then_inc(mean_ready, 1)
            dve.wait_ge(std_ready, NORM["pre0"] + 1)
            chain.link(nc.vector.reciprocal(mean_part[:, :], std[:, :]))
            nc.vector.tensor_tensor(rstd_both[:, :], mean_part[:, :], rstd[:, :], ALU.mult)\
                .then_inc(rstd_ready, 1)
            dve.wait_ge(rstd_ready, NORM["pre0"] + 1)
            dve.wait_ge(gains_ready, 1)
            norm_tiles("pre0", fours(g_both[:, :]), rstd_both)
            with dve.Fori(0, KT // 4) as g:
                for m in range(4):
                    nc.vector.scalar_tensor_tensor(
                        out=x[:, 4 * g + m, :], in0=x[:, 4 * g + m, :], scalar=fours(pcols("g_out"))[:, g, m:m + 1],
                        in1=rstd[:, :], op0=ALU.mult, op1=ALU.mult).then_inc(x_normed, 1)
            dve.wait_ge(restart_ready, 1)
            for hd in range(G_HEADS):
                dve.wait_ge(glog_ready, hd + 1)
                nc.vector.tensor_scalar(g_min[:, :], att[hd][:, :], 0.0, None, ALU.min)\
                    .then_inc(gk_taken, 1)
                dve.wait_ge(gk_taken, hd + 1)
                chain.link(nc.vector.tensor_tensor(log_a[:, :], g_min[:, :], g_log[:, :], ALU.subtract))
                nc.vector.tensor_tensor_scan(gcum[:, hd, :, :].rearrange("p a t -> p (a t)"),
                                             restart[:, :, :].rearrange("p a t -> p (a t)"),
                                             log_a[:, :], 0.0, ALU.mult, ALU.add).then_inc(gcum_ready, 1)
                if hd % 2:
                    split("rank", None, hd // 2)
            dve.wait_ge(gcum_ready, G_HEADS)
            dve.wait_ge(at_init, 2)
            with dve.Fori(0, G_HEADS) as i:
                chain.loop(i, 7)
                for j in range(24):
                    if j == 0:
                        dve.wait_ge(decays_ready, 3 * i)
                        b = gcum[:, i, :, :].rearrange("p a (c t) -> p (a c) t", t=CHUNK)
                        nc.vector.tensor_tensor(
                            to_end[:, :, :].rearrange("p a (c t) -> p (a c) t", t=CHUNK),
                            b[:, :, CHUNK - 1:CHUNK].to_broadcast([P, 2 * T // CHUNK, CHUNK]), b,
                            ALU.subtract).then_inc(to_end_ready, 1)
                    if j in (1, 3):
                        n = j // 2
                        unit_is_done("gla", i, j)
                        dve.wait_ge(decays_ready, 3 * i + 1)
                        nc.vector.scalar_tensor_tensor(out=q_e[:, n, :], in0=acc[n][:, 0:T],
                                                       scalar=G_DK ** -0.5, in1=e_pos[:, n, :],
                                                       op0=ALU.mult, op1=ALU.mult)\
                            .then_inc(acc_taken[n], 1)
                    if j == 3:
                        taken(dve, 0, "gla", i, 0)
                        taken(dve, 1, "gla", i, 0)
                        over1, over2 = 2 * CHUNK - 1, 3 * CHUNK - 1
                        for n in range(2):
                            chain.step(nc.vector.tensor_scalar(
                                q_y[:, n, :], q_e[:, n, 3 * CHUNK:T], e_pos[:, n, over2:over2 + 1],
                                None, ALU.mult))
                        chain.wait()
                        for n in range(2):
                            nc.vector.tensor_scalar(
                                q_x[:, n, 0:CHUNK], q_e[:, n, 2 * CHUNK:3 * CHUNK],
                                e_pos[:, n, over1:over1 + 1], None, ALU.mult).then_inc(qx_ready, 1)
                            nc.vector.tensor_scalar(
                                q_x[:, n, CHUNK:2 * CHUNK], q_y[:, n, :],
                                e_pos[:, n, over1:over1 + 1], None, ALU.mult).then_inc(qx_ready, 1)
                    if j == 15:
                        unit_is_done("gla", i, j)
                        for t in range(2):
                            nc.vector.tensor_copy(vg[:, t, :], tok[t][:, :]).then_inc(tok_taken, 1)
                    if j == 16:
                        dve.wait_ge(gscores_ready, i + 1)
                        nc.vector.tensor_copy(a_t[:, 0, P:T], att[0][:, P:T]).then_inc(at_ready, 1)
                        for s in range(2):
                            for p, lo, hi in ((CHUNK, 0, CHUNK), (P, CHUNK, P)):
                                at = s * P
                                nc.vector.copy_predicated(
                                    a_t[0:p, s, at + lo:at + hi], kept[0:p, lo:hi].bitcast(i32),
                                    att[0][0:p, s * T + at + lo:s * T + at + hi]).then_inc(at_ready, 1)
                    if j == 23:
                        dve.wait_ge(ostd_ready, i + 1)
                        chain.link(nc.vector.reciprocal(o_rstd[:, :], o_std[:, :]))
                        dve.wait_ge(oglo_ready, i)
                        dve.wait_ge(osb_ready, 2 * i + 2)
                        for v in range(4):
                            chain.step(nc.vector.scalar_tensor_tensor(
                                out=o_norm[:, v, :], in0=o_sb[:, v, :], scalar=pcols("g_gla")[:, v:v + 1],
                                in1=o_rstd[:, :], op0=ALU.mult, op1=ALU.mult))
                        chain.wait()
                        taken(dve, 0, "gla", i, 3)
                        taken(dve, 1, "gla", i, 3)
                        nc.vector.tensor_tensor(o_norm[:, :, :], o_norm[:, :, :], o_sg[:, :, :],
                                                ALU.mult).then_inc(og_ready, 1)
                    split("gla", i, j)
                chain.done(G_HEADS)

            def add_normed(n, gain, source, k):
                norm_rstd(n)
                half = k * KT // 2
                with dve.Fori(0, KT // 4) as g:
                    for m in range(4):
                        dve.wait_ge((x_added_pool, x_added)[m // 2], 2 * g + max(half + m % 2 - 1, 0))
                        nc.vector.scalar_tensor_tensor(
                            out=normed[:, m, :], in0=source[:, 4 * g + m, :],
                            scalar=fours(pcols(gain))[:, g, m:m + 1],
                            in1=rstd[:, :], op0=ALU.mult, op1=ALU.mult).then_inc(scaled_ready, 1)
                    for m in (2, 3):
                        dve.wait_ge(scaled_ready, 4 * g + (k * KT + m + 1))
                        nc.vector.tensor_tensor(x[:, 4 * g + m, :], x[:, 4 * g + m, :], normed[:, m, :],
                                                ALU.add).then_inc(x_added, 1)

            with dve.Fori(0, KT // 2) as i:
                for j in range(4):
                    split("glaout", i, j)
            dve.wait_ge(x_normed, KT)
            add_normed("post0", "g_post0", y, 0)
            norm_rstd("pre1")
            norm_tiles("pre1", fours(pcols("g_pre1")), rstd)
            with dve.Fori(0, A_TILES) as i:
                for j in range(4):
                    split("latent", i, j)
            for j in range(4):
                if j == 2:
                    dve.wait_ge(lstd_ready, 1)
                    chain.link(nc.vector.reciprocal(l_rstd[:, :, :], l_std[:, :, :]))
                    for k in range(2 * A_TILES):
                        if k < 2:
                            dve.wait_ge(act_ready, 4 * KT)
                        else:
                            dve.wait_ge(c_ready, k - 1)
                        n = k // A_TILES
                        nc.vector.scalar_tensor_tensor(
                            out=normed[:, k % 2, :], in0=latent[:, n, k % A_TILES, :],
                            scalar=pcols("g_latent")[:, k:k + 1], in1=l_rstd[:, n, :],
                            op0=ALU.mult, op1=ALU.mult).then_inc(cnormed_ready, 1)
                split("krope", None, j)
            taken(dve, 0, "krope", None, 0)
            taken(dve, 1, "krope", None, 0)
            dve.wait_ge(rope_ready, 2)
            dve.wait_ge(krm_zero, 1)
            for n, (part, angle) in enumerate(((0, cosine), (1, sine), (1, cosine), (0, sine))):
                chain.step(nc.vector.tensor_tensor(rope_t[:, n, :], kr[:, part, :], angle[:, :], ALU.mult))
            chain.wait()
            for n in range(4):
                rows = slice(HALF * n, HALF * (n + 1))
                nc.vector.tensor_tensor(kr_m[rows, 0, n, :], rope_t[rows, 0, :], rope_t[rows, 1, :],
                                        ALU.subtract).then_inc(krm_ready, 1)
                nc.vector.tensor_tensor(kr_m[rows, 1, n, :], rope_t[rows, 2, :], rope_t[rows, 3, :],
                                        ALU.add).then_inc(krm_ready, 1)
            dve.wait_ge(krm_ready, 8)
            dve.wait_ge(causal_ready, 3)
            with dve.Fori(0, A_HEADS // 4) as i:
                chain.loop(i, 2 + 4 * 2)
                for j in range(16):
                    if j in (1, 3):
                        n = j // 2
                        unit_is_done("mla", i, j)
                        nc.vector.tensor_copy(kn[:, 2 * n:2 * n + 2, :], acc[1][:, :])\
                            .then_inc(acc_taken[1], 1)
                    if j == 5:
                        taken(dve, 0, "mla", i, 2)
                        chain.step(nc.vector.tensor_tensor(rope_t[:, 0, :], q_r[:, 0, :], cosine[:, :],
                                                           ALU.mult))
                        chain.step(nc.vector.tensor_tensor(rope_t[:, 1, :], q_r[:, 1, :], sine[:, :],
                                                           ALU.mult))
                        chain.wait()
                        nc.vector.tensor_tensor(q_rope[:, 0, :], rope_t[:, 0, :], rope_t[:, 1, :],
                                                ALU.subtract).then_inc(qrope_ready, 1)
                    if j == 7:
                        unit_is_done("mla", i, j)
                        for t in range(2):
                            nc.vector.tensor_copy(va[:, t, :], tok[t][:, :]).then_inc(tok_taken, 1)
                    if j in (8, 12):
                        first = (j - 8) // 2
                        for n in (first, first + 1):
                            dve.wait_ge(logits_ready, 4 * i + n + 1)
                            dve.wait_ge(exp_ready, 8 * i + max(2 * (n - 1), 0))
                            chain.link(nc.vector.scalar_tensor_tensor(
                                out=logits[:, n % 2, :], in0=att[n % 2][:, 0:3 * P],
                                scalar=(A_NOPE + A_ROPE) ** -0.5, in1=causal[:, :],
                                op0=ALU.mult, op1=ALU.add))
                            nc.vector.reduce_max(row_max[:, n % 2, 0:1], logits[:, n % 2, 0:P], AX)
                            chain.link(nc.vector.reduce_max(row_max[:, n % 2, 1:2],
                                                            logits[:, n % 2, P:3 * P], AX))
                            nc.vector.tensor_scalar(neg_max[:, n % 2, :], row_max[:, n % 2, :], -1.0,
                                                    None, ALU.mult).then_inc(neg_ready, 1)
                        for n in (first, first + 1):
                            dve.wait_ge(exp_ready, 8 * i + 2 * n + 2)
                            nc.vector.reciprocal(row_inv[:, n % 2, :], row_sum[:, n % 2, :])\
                                .then_inc(inv_ready, 1)
                    if j in (12, 15):
                        for n in range(2 * (j // 15), 2 * (j // 15) + 2):
                            dve.wait_ge(apv_ready, 4 * i + n + 1)
                            taken(dve, 1 - n % 2, "mla", i, (2, 3, 3, 4)[n])
                            dve.wait_ge(molo_ready, 4 * i)
                            nc.vector.tensor_tensor(a_out[:, n, :], att[2 + n % 2][:, 0:T],
                                                    a_gate[:, n, :], ALU.mult).then_inc(aout_ready, 1)
                    split("mla", i, j)
                chain.done(A_HEADS // 4)
            with dve.Fori(0, KT // 2 - 1) as i:
                for j in range(4):
                    split("mlaout", i, j)
            add_normed("post1", "g_post1", y2, 1)

        @block.gpsimd
        def _(pool):
            chain = Chain(pool, pool_step)
            gp = nc.gpsimd

            def add_squares(n, with_gain=False):
                k = POOLED[n]
                pool.wait_ge(stat_ready, STAT[n])
                if with_gain:
                    chain.link(gp.memset(sumsq_g[:, :], 0.0))
                chain.link(gp.memset(sumsq[:, :], 0.0))
                with pool.Fori(0, KT // 2) as i:
                    for m in range(2):
                        pool.wait_ge(sq_ready, 2 * i + (k * KT + m + 1))
                        pool.wait_ge(sq_added, 2 * i + (k * KT + m))
                        ins = gp.tensor_tensor(sumsq[:, :], sumsq[:, :], square[:, m, :], ALU.add)
                        if with_gain:
                            ins = gp.tensor_tensor(sumsq_g[:, :], sumsq_g[:, :], square_g[:, m, :], ALU.add)
                        ins.then_inc(sq_added, 1)

            def norm_low(n):
                at = TO_ACT[n] * KT
                with pool.Fori(0, KT // 4) as g:
                    for m in range(4):
                        pool.wait_ge(nhi_ready, 4 * g + (at + m + 1))
                        gp.tensor_tensor(n_lo[:, 4 * g + m, :], normed[:, m, :],
                                         n_hi[:, 4 * g + m, :].bitcast(fp32), ALU.subtract)\
                            .then_inc(act_ready, 1)

            def add_scaled(k):
                with pool.Fori(0, KT // 4) as g:
                    for m in range(2):
                        pool.wait_ge(scaled_ready, 4 * g + (k * KT + m + 1))
                        gp.tensor_tensor(x[:, 4 * g + m, :], x[:, 4 * g + m, :], normed[:, m, :], ALU.add)\
                            .then_inc(x_added_pool, 1)

            gp.memset(eps_col[:, :], EPS).then_inc(const_ready, 1)
            chain.step(gp.memset(ident[:, :], 0.0))
            chain.step(gp.memset(head_row[:, :, :], 0.0))
            gp.memset(ones[:, :], 1.0).then_inc(const_ready, 1)
            chain.wait()
            gp.affine_select(out=ident[:, :], in_=ident[:, :], compare_op=ALU.not_equal, fill=1.0, base=0,
                             pattern=[[-1, P]], channel_multiplier=1).then_inc(const_ready, 1)
            gp.affine_select(out=head_row[:, :, :], in_=head_row[:, :, :], compare_op=ALU.not_equal, fill=1.0,
                             base=0, pattern=[[-1, M_HEADS], [0, P]], channel_multiplier=1)\
                .then_inc(const_ready, 1)
            norm_low("mix")
            pool.wait_ge(a_col_ready, 2 * M_HEADS)
            for d in (decay0[:, :, 0:P], decay1[:, :, :]):
                gp.affine_select(out=d, in_=d, compare_op=ALU.is_ge, fill=0.0, base=0,
                                 pattern=[[0, M_HEADS], [1, P]], channel_multiplier=-1)\
                    .then_inc(decay_masked, 1)
            with pool.Fori(0, M_HEADS) as i:
                pool.wait_ge(hsq_ready, i + 1)
                gp.tensor_tensor(h_sum[:, :], h_sq[:, 0, :], h_sq[:, 1, :], ALU.add).then_inc(hsum_ready, 1)
                pool.wait_ge(hmhi_ready, i + 1)
                gp.tensor_tensor(hm_lo[:, bass.ds(2 * i, 2), :], hm[:, :, :],
                                 hm_hi[:, bass.ds(2 * i, 2), :].bitcast(fp32), ALU.subtract)\
                    .then_inc(hmlo_ready, 1)
                for n in range(2):
                    pool.wait_ge(ychi_ready, 2 * i + n + 1)
                    gp.tensor_tensor(yc_lo[:, 2 * i + n, :], cz[:, :],
                                     yc_hi[:, 2 * i + n, :].bitcast(fp32), ALU.subtract)\
                        .then_inc(yclo_ready, 1)
            with pool.Fori(0, KT // 2) as i:
                for m in range(2):
                    taken(pool, 1, "merge", i, 2 * m + 1)
                    taken(pool, 0, "merge", i, 2 * m + 1)
                    pool.wait_ge(mglo_ready, 2 * i + m)
                    gp.tensor_tensor(merged[:, :], part_m[:, :], part_c[:, :], ALU.add)\
                        .then_inc(merged_ready, 1)
                    pool.wait_ge(mghi_ready, 2 * i + m + 1)
                    gp.tensor_tensor(mg_lo[:, 2 * i + m, :], merged[:, :],
                                     mg_hi[:, 2 * i + m, :].bitcast(fp32), ALU.subtract)\
                        .then_inc(mglo_ready, 1)
            add_squares("ffn")
            norm_low("ffn")
            with pool.Fori(0, F_TILES) as i:
                pool.wait_ge(fhi_ready, i + 1)
                gp.tensor_tensor(f_lo[:, i, :], f_act[:, :], f_hi[:, i, :].bitcast(fp32), ALU.subtract)\
                    .then_inc(flo_ready, 1)
            add_squares("out", with_gain=True)
            norm_low("pre0")
            gp.memset(rank_rows[:, :], 1.0).then_inc(rank_ones, 1)
            chain.step(gp.memset(restart[:, :, :], 1.0))
            chain.step(gp.memset(kept[:, :], 1.0))
            gp.memset(a_t[:, :, :], 0.0).then_inc(at_init, 1)
            chain.wait()
            gp.affine_select(out=kept[:, :], in_=kept[:, :], compare_op=ALU.is_ge, fill=0.0, base=0,
                             pattern=[[1, P]], channel_multiplier=-1).then_inc(at_init, 1)
            gp.memset(restart[:, :, :].rearrange("p a (c t) -> p (a c) t", t=CHUNK)[:, :, 0:1], 0.0)\
                .then_inc(restart_ready, 1)
            with pool.Fori(0, G_HEADS) as i:
                taken(pool, 0, "gla", i, 1)
                taken(pool, 1, "gla", i, 1)
                pool.wait_ge(decays_ready, 3 * i + 3)
                gp.tensor_tensor(k_e[:, :, :], k_sb[:, :, :], e_neg[:, :, :], ALU.mult).then_inc(kk_ready, 1)
                gp.tensor_tensor(k_l[:, :, :], k_sb[:, :, :], e_end[:, :, :], ALU.mult).then_inc(kk_ready, 1)
                pool.wait_ge(osq_ready, 2 * i + 2)
                chain.loop(i, 1)
                chain.link(gp.tensor_tensor(o_sum2[:, :, :], o_sq[:, 0:2, :], o_sq[:, 2:4, :], ALU.add))
                gp.tensor_tensor(o_sum[:, :], o_sum2[:, 0, :], o_sum2[:, 1, :], ALU.add)\
                    .then_inc(osum_ready, 1)
                pool.wait_ge(oghi_ready, i + 1)
                gp.tensor_tensor(og_lo[:, bass.ds(4 * i, 4), :], o_norm[:, :, :],
                                 og_hi[:, bass.ds(4 * i, 4), :].bitcast(fp32), ALU.subtract)\
                    .then_inc(oglo_ready, 1)
                chain.done(G_HEADS)
            add_squares("post0")
            pool.wait_ge(x_normed, KT)
            add_scaled(0)
            norm_low("pre1")
            chain.link(gp.memset(l_sumsq[:, :, :], 0.0))
            chain.step(gp.memset(causal[:, :], 0.0))
            gp.memset(kr_m[:, :, :, :], 0.0).then_inc(krm_zero, 1)
            chain.wait()
            for b in (0, 2):
                d = causal[:, b * P:(b + 1) * P]
                gp.affine_select(out=d, in_=d, compare_op=ALU.is_ge, fill=-1e30, base=0,
                                 pattern=[[-1, P]], channel_multiplier=1).then_inc(causal_ready, 1)
            gp.memset(row_max[:, :, :], 0.0).then_inc(causal_ready, 1)
            with pool.Fori(0, A_TILES) as i:
                for n in range(2):
                    taken(pool, n, "latent", i, 0)
                    pool.wait_ge(lsq_added, 2 * i + n)
                    gp.tensor_tensor(l_sumsq[:, n, :], l_sumsq[:, n, :], l_square[:, n, :], ALU.add)\
                        .then_inc(lsq_added, 1)
            for k in range(2 * A_TILES):
                pool.wait_ge(chi_ready, k + 1)
                gp.tensor_tensor(c_lo[:, k, :], normed[:, k % 2, :], c_hi[:, k, :].bitcast(fp32),
                                 ALU.subtract).then_inc(c_ready, 1)
            pool.wait_ge(krm_ready, 8)
            with pool.Fori(0, A_HEADS // 4) as i:
                chain.loop(i, 2 + 4)
                taken(pool, 0, "mla", i, 2)
                chain.step(gp.tensor_tensor(rope_t[:, 2, :], q_r[:, 1, :], cosine[:, :], ALU.mult))
                chain.step(gp.tensor_tensor(rope_t[:, 3, :], q_r[:, 0, :], sine[:, :], ALU.mult))
                chain.wait()
                gp.tensor_tensor(q_rope[:, 1, :], rope_t[:, 2, :], rope_t[:, 3, :], ALU.add)\
                    .then_inc(qrope_ready, 1)
                for pair in range(2):
                    for n in (2 * pair, 2 * pair + 1):
                        pool.wait_ge(inv_ready, 4 * i + n + 1)
                        chain.step(gp.tensor_tensor(
                            probs[:, n % 2, 0:P], probs[:, n % 2, 0:P],
                            row_inv[:, n % 2, 0:1].to_broadcast([P, P]), ALU.mult))
                        gp.tensor_tensor(
                            probs[:, n % 2, P:3 * P], probs[:, n % 2, P:3 * P],
                            row_inv[:, n % 2, 1:2].to_broadcast([P, 2 * P]), ALU.mult)\
                            .then_inc(probs_ready, 1)
                    for n in (2 * pair, 2 * pair + 1):
                        pool.wait_ge(mohi_ready, 4 * i + n + 1)
                        gp.tensor_tensor(mo_lo[:, 4 * i + n, :], a_out[:, n, :],
                                         mo_hi[:, 4 * i + n, :].bitcast(fp32), ALU.subtract)\
                            .then_inc(molo_ready, 1)
                chain.done(A_HEADS // 4)
            add_squares("post1")
            add_scaled(1)


def kernel(**inputs):
    import concourse.bacc as _bacc
    import numpy as np
    from concourse.bass_utils import run_bass_kernel_spmd as _run

    arrays = lay_out({k: np.asarray(v) for k, v in inputs.items()})
    nc = _bacc.Bacc("TRN2", target_bir_lowering=False, num_devices=1)
    ins = {n: nc.dram_tensor(n, v.shape, mybir.dt.from_np(v.dtype), kind="ExternalInput").ap()
           for n, v in arrays.items()}
    out = nc.dram_tensor("out", (P, KT, T), mybir.dt.float32, kind="ExternalOutput").ap()
    program(nc, out=out, **ins)
    got = _run(nc, [arrays], core_ids=[0]).results[0]["out"]
    return np.ascontiguousarray(got.transpose(2, 1, 0).reshape(1, T, D))


def lay_out(a):
    import numpy as np

    splits = (M_HEADS * M_DQK, M_HEADS * M_DQK, M_HEADS * M_DV, M_HEADS * M_DV, M_HEADS, M_HEADS,
              C_TILES * P, C_TILES * P, C_TILES * P, D, D)
    offs = [sum(splits[:n]) for n in range(len(splits))]
    cols = {n: slice(o, o + w) for n, o, w in zip("q k v o i f cb cc ch gm gc".split(), offs, splits)}
    w_in = {n: a["w_in"][:, s] for n, s in cols.items()}
    b_in = {n: a["b_in"][s] for n, s in cols.items()}

    chunks = np.zeros((N_CHUNKS, P, 2 * UNIT), np.float32)
    at = [0, 0]

    def put(w, width=P):
        k, n = w.shape
        for c in range(0, n, width):
            for r in range(0, k, P):
                block = w[r:r + P, c:c + width]
                chunks[at[0], 0:block.shape[0], at[1]:at[1] + block.shape[1]] = block
                at[1] += width
                if at[1] == 2 * UNIT:
                    at[0], at[1] = at[0] + 1, 0

    def end():
        if at[1]:
            at[0], at[1] = at[0] + 1, 0

    def tile_of(w, m):
        return w[:, m * P:(m + 1) * P]

    gates = np.zeros((D, P), np.float32)
    gates[:, 0:M_HEADS] = w_in["i"]
    gates[:, 32:32 + M_HEADS] = w_in["f"]
    put(gates)
    for h in range(M_HEADS):
        put(tile_of(w_in["q"], h))
        put(tile_of(w_in["k"], h))
        put(w_in["v"][:, h * M_DV:(h + 1) * M_DV], M_DV)
        for n in range(2):
            put(tile_of(w_in["o"], 2 * h + n))
        for n in range(2):
            for part in ("cc", "ch", "cb"):
                put(tile_of(w_in[part], 2 * h + n))
    for m in range(KT):
        put(tile_of(w_in["gm"], m))
        put(tile_of(w_in["gc"], m))
        put(tile_of(a["w_branch_m"], m))
        put(tile_of(a["w_branch_c"], m))
    put(a["w_out"])
    for f in range(F_TILES):
        put(tile_of(a["w_up"], f))
        put(tile_of(a["w_up"], F_TILES + f))
    for m in range(KT):
        put(tile_of(a["w_down"], m))
        end()
    gla = a["l0_gla_w_in_2"]
    qk, vv = G_HEADS * G_DK, G_HEADS * G_DV
    ranks = np.zeros((D, P), np.float32)
    ranks[:, 0:G_RANK] = gla[:, 2 * qk + 2 * vv:]
    put(ranks)
    for h in range(G_HEADS):
        put(gla[:, h * G_DK:(h + 1) * G_DK])
        put(gla[:, qk + h * G_DK:qk + (h + 1) * G_DK])
        put(gla[:, 2 * qk + h * G_DV:2 * qk + (h + 1) * G_DV], G_DV)
        put(gla[:, 2 * qk + vv + h * G_DV:2 * qk + vv + (h + 1) * G_DV])
    put(a["l0_gla_w_out_2"])
    mla = a["l1_mla_w_in_2"]
    for m in range(A_TILES):
        put(tile_of(mla, m))
        put(tile_of(mla, A_TILES + m))
    k_rope = mla[:, 2 * A_RANK:2 * A_RANK + A_ROPE]
    for half in range(2):
        put(np.concatenate([k_rope[:, half * HALF:(half + 1) * HALF]] * 4, axis=1))
    w_q = a["l1_mla_w_qb_2"].reshape(A_RANK, A_HEADS, A_NOPE + A_ROPE)
    w_kv = a["l1_mla_w_kvb_2"].reshape(A_RANK, A_HEADS, A_NOPE + A_V)
    for g in range(0, A_HEADS, 4):
        for n in (0, 2):
            for w in (w_q, w_kv):
                put(w[:, g + n, 0:A_NOPE])
                put(w[:, g + n + 1, 0:A_NOPE])
        for half in range(2):
            r = A_NOPE + half * HALF
            put(np.ascontiguousarray(w_q[:, g:g + 4, r:r + HALF]).reshape(A_RANK, 4 * HALF))
        end()
        put(np.ascontiguousarray(w_kv[:, g:g + 4, A_NOPE:]).reshape(A_RANK, 4 * A_V), 4 * A_V)
        for n in range(4):
            put(tile_of(mla[:, 2 * A_RANK + A_ROPE:], g + n))
    put(a["l1_mla_w_out_2"])
    assert at == [N_CHUNKS, 0], at

    def col(v):
        return v.reshape(-1, P).T

    b_gate = np.zeros((P, 1), np.float32)
    b_gate[0:M_HEADS, 0] = b_in["i"]
    b_gate[32:32 + M_HEADS, 0] = b_in["f"]
    b_mix = []
    for h in range(M_HEADS):
        b_mix += [col(b_in["q"])[:, h], col(b_in["k"])[:, h]]
        b_mix += [col(b_in["o"])[:, 2 * h + n] for n in range(2)]
        b_mix += [col(b_in[part])[:, 2 * h + n] for n in range(2) for part in ("cc", "ch", "cb")]
    b_merge = [col(b_in[part])[:, m] for m in range(KT) for part in ("gm", "gc")]
    conv = a["conv_w"].reshape(3, C_TILES, P).transpose(2, 1, 0).reshape(P, -1)
    ffn = np.concatenate([a["ffn_conv_w"], a["ffn_conv_b"][None]]).reshape(4, 2, F_TILES, P)
    ffn = ffn.transpose(3, 2, 1, 0).reshape(P, -1)
    freq = np.float32(10000.0) ** (-np.arange(0, A_ROPE, 2, dtype=np.float32) / np.float32(A_ROPE))
    params = {
        "g_mix": col(a["norm_mix_g"]), "g_ffn": col(a["norm_ffn_g"]), "g_out": col(a["norm_out_g"]),
        "g_pre0": col(a["l0_pre_norm_2"]), "g_post0": col(a["l0_post_norm_2"]),
        "g_pre1": col(a["l1_pre_norm_2"]), "g_post1": col(a["l1_post_norm_2"]),
        "b_gate": b_gate, "b_mix": np.stack(b_mix, 1), "b_merge": np.stack(b_merge, 1),
        "g_head": col(a["mlstm_head_g"]), "w_conv": conv, "w_ffn": ffn, "g_gla": col(a["l0_gla_g_onorm_2"]),
        "g_latent": np.concatenate([col(a["l1_mla_g_qa_2"]), col(a["l1_mla_g_kva_2"])], 1),
        "inv_freq": np.tile(freq.astype(np.float32), 4)[:, None],
    }
    for n, k in PARAMS:
        assert params[n].shape == (P, k), (n, params[n].shape)
    return {
        "x_in": np.ascontiguousarray(a["x"][0].T.reshape(KT, P, T).transpose(1, 0, 2)),
        "stream_in": chunks,
        "params_in": np.concatenate([params[n] for n, _ in PARAMS], 1),
        "v_bias_in": np.ascontiguousarray(b_in["v"])[None],
        "gk2_in": np.concatenate([a["l0_gla_w_gk2_2"], a["l0_gla_b_gk_2"][None]]),
        "positions_in": np.ascontiguousarray(a["positions_2"]),
    }
```

```python
from contextlib import ExitStack

import concourse.bass as bass
from concourse import mybir

P = 128
T = 256
D = 2048
KT = D // P
CHUNK = 64
PI = 3.14159265358979
PI_INSIDE = 3.1415925
EPS = 1e-6
M_HEADS, M_DV, M_DQK = 4, 256, 128
C_TILES = 1024 // P
D_FF = 5504
F_TILES = D_FF // P
G_HEADS, G_DK, G_DV, G_RANK, G_TAU = 4, 256, 512, 16, 16.0
A_HEADS, A_RANK, A_NOPE, A_ROPE, A_V = 16, 512, 128, 64, 128
A_TILES = A_RANK // P
HALF = A_ROPE // 2
UNIT = 1024
RING = 4
FREE = 1

PHASES = [
    ("gates", 1, 2, 1, 0, 0),
    ("mix", M_HEADS, 24, 5, 5, 1),
    ("merge", KT // 2, 12, 4, 4, 0),
    ("wout", KT // 2, 4, 1, 1, 0),
    ("wup", F_TILES, 4, 1, 1, 0),
    ("wdown", KT // 2, 12, 1, 1, 0),
    ("rank", 1, 2, 0, 1, 0),
    ("gla", G_HEADS, 24, 4, 4, 1),
    ("glaout", KT // 2, 4, 1, 1, 0),
    ("latent", 1, 16, 4, 4, 0),
    ("krope", 1, 4, 1, 1, 0),
    ("mla", A_HEADS // 4, 16, 5, 4, 1),
    ("mlaout", KT // 2, 4, 1, 1, 0),
]
N_CHUNKS = sum(n * units for _, n, units, *_ in PHASES) // 2

PARAMS = [
    ("g_mix", KT), ("g_ffn", KT), ("g_out", KT), ("g_pre0", KT), ("g_post0", KT), ("g_pre1", KT),
    ("g_post1", KT), ("b_gate", 1), ("b_mix", M_HEADS * 10), ("b_merge", 2 * KT), ("g_head", 8),
    ("w_conv", 3 * C_TILES), ("w_ffn", 8 * F_TILES), ("g_gla", G_DV // P), ("g_latent", 8),
    ("inv_freq", 1),
]
N_PARAMS = sum(n for _, n in PARAMS)


def program(nc, x_in, stream_in, params_in, v_bias_in, gk2_in, positions_in, out):
    fp32, fp32r, i32 = mybir.dt.float32, mybir.dt.float32r, mybir.dt.int32
    ALU = mybir.AluOpType
    ACT = mybir.ActivationFunctionType
    AX = mybir.AxisListType.X

    base, total = {}, [0, 0, 0, 0]
    for name, n, *per in PHASES:
        base[name] = (list(total), per)
        total = [t + n * k for t, k in zip(total, per)]

    def count(which, name, i, j):
        start, per = base[name]
        k = start[which] + j
        return k if i is None else i * per[which] + k

    def unit_of(name, i, j):
        start, per = base[name]
        k = start[0] + j
        if i is None:
            return k, k % RING, k // RING
        assert per[0] % RING == 0
        return i * per[0] + k, k % RING, i * (per[0] // RING) + k // RING

    ctx = ExitStack()
    with ctx:
        def sb(name, shape, dt=fp32):
            return ctx.enter_context(nc.sbuf_tensor(name, shape, dt))

        def sem(name):
            return ctx.enter_context(nc.semaphore(name))

        free_from_start = []

        def used_sem(name):
            free_from_start.append(sem(name))
            return free_from_start[-1]

        x = sb("x", [P, KT, T])
        raw = sb("raw", [P, RING, UNIT])
        w_hi = sb("w_hi", [P, RING, UNIT], fp32r)
        w_lo = sb("w_lo", [P, RING, UNIT], fp32r)
        n_hi = sb("n_hi", [P, KT, T], fp32r)
        n_lo = sb("n_lo", [P, KT, T], fp32r)
        par = sb("par", [P, N_PARAMS])
        normed = sb("normed", [P, 4, T])
        square = sb("square", [P, 2, T])
        sumsq = sb("sumsq", [P, T])
        std = sb("std", [P, T])
        rstd = sb("rstd", [P, T])
        g_both = sb("g_both", [P, KT])
        ones = sb("ones", [P, P])
        ident = sb("ident", [P, P])
        cosine = sb("cosine", [P, T])
        sine = sb("sine", [P, T])
        eps_col = sb("eps_col", [P, 1])

        arena_start = -(-nc.sbuf_base // 64) * 64
        arena_end = nc.sbuf_usable_end

        class Arena:
            def __init__(self, at):
                self.at = at

            def place(self, name, shape, dt=fp32):
                n = 4
                for s in shape[1:]:
                    n *= s
                t = nc.alloc_sbuf_tensor_at(name, shape, dt, offset=self.at)
                self.at += -(-n // 32) * 32
                assert self.at <= arena_end, (name, self.at - arena_end)
                return t

        a = Arena(arena_start)
        yc_hi = a.place("yc_hi", [P, C_TILES, T], fp32r)
        yc_lo = a.place("yc_lo", [P, C_TILES, T], fp32r)
        hm_hi = a.place("hm_hi", [P, C_TILES, T], fp32r)
        hm_lo = a.place("hm_lo", [P, C_TILES, T], fp32r)
        sig_m = a.place("sig_m", [P, T])
        sig_c = a.place("sig_c", [P, T])
        part_m = a.place("part_m", [P, T])
        part_c = a.place("part_c", [P, T])
        merged = a.place("merged", [P, T])
        mixer_temps = a.at
        mg_hi = a.place("mg_hi", [P, KT, T], fp32r)
        mg_lo = a.place("mg_lo", [P, KT, T], fp32r)
        a = Arena(mixer_temps)
        decay0 = a.place("decay0", [P, M_HEADS, T])
        decay1 = a.place("decay1", [P, M_HEADS, P])
        floor = a.place("floor", [P, M_HEADS, T])
        v_bias = a.place("v_bias", [P, M_HEADS, M_DV])
        qT = a.place("qT", [P, T])
        kT = a.place("kT", [P, T])
        vm = a.place("vm", [P, 2, M_DV])
        sig_o = a.place("sig_o", [P, 2, T])
        st0 = a.place("st0", [P, T])
        st1 = a.place("st1", [P, P])
        den_abs = a.place("den_abs", [P, T])
        den = a.place("den", [P, T])
        rden = a.place("rden", [P, T])
        h = a.place("h", [P, 2, T])
        h_sq = a.place("h_sq", [P, 2, T])
        h_sum = a.place("h_sum", [P, T])
        h_std = a.place("h_std", [P, T])
        h_rstd = a.place("h_rstd", [P, T])
        h_norm = a.place("h_norm", [P, 2, T])
        hm = a.place("hm", [P, 2, T])
        cc = a.place("cc", [P, T])
        cu = a.place("cu", [P, T])
        cy = a.place("cy", [P, T])
        cz = a.place("cz", [P, T])
        i_row = a.place("i_row", [64, T])
        f_row = a.place("f_row", [64, T])
        f_abs = a.place("f_abs", [64, T])
        f_exp = a.place("f_exp", [64, T])
        f_log = a.place("f_log", [64, T])
        f_min = a.place("f_min", [64, T])
        logf = a.place("logf", [64, T])
        logf0 = a.place("logf0", [M_HEADS, T])
        ones_row = a.place("ones_row", [M_HEADS, T])
        b_row = a.place("b_row", [M_HEADS, T])
        a_row = a.place("a_row", [M_HEADS, T])
        mm_row = a.place("mm_row", [M_HEADS, 2, T])
        a_col = a.place("a_col", [P, 2, M_HEADS])
        head_row = a.place("head_row", [M_HEADS, M_HEADS, P])

        squares_all = Arena(arena_start).place("squares_all", [P, KT, T])

        a = Arena(arena_start)
        f_hi = a.place("f_hi", [P, F_TILES, T], fp32r)
        f_lo = a.place("f_lo", [P, F_TILES, T], fp32r)
        f_pre = a.place("f_pre", [P, 2, T])
        f_gate = a.place("f_gate", [P, T])
        f_val = a.place("f_val", [P, T])
        f_silu = a.place("f_silu", [P, T])
        f_act = a.place("f_act", [P, T])
        square_g = a.place("square_g", [P, 2, T])
        sumsq_g = a.place("sumsq_g", [P, T])
        mean_g = Arena(a.at).place("mean_g", [P, T])
        a = Arena(a.at - 3 * 4 * T)
        mean_part = a.place("mean_part", [P, T])
        rstd_both = a.place("rstd_both", [P, T])

        a = Arena(arena_start)
        og_hi = a.place("og_hi", [P, KT, T], fp32r)
        og_lo = a.place("og_lo", [P, KT, T], fp32r)
        y_at = a.at
        y = a.place("y", [P, KT, T])
        restart = a.place("restart", [P, 2, T])
        gcum = a.place("gcum", [P, G_HEADS, 2, T])
        g_log = Arena(a.at).place("g_log", [P, G_HEADS, 2 * T])
        to_end = a.place("to_end", [P, 2, T])
        e_pos = a.place("e_pos", [P, 2, T])
        e_neg = a.place("e_neg", [P, 2, T])
        e_end = a.place("e_end", [P, 2, T])
        q_e = a.place("q_e", [P, 2, T])
        q_x = a.place("q_x", [P, 2, 2 * CHUNK])
        q_y = a.place("q_y", [P, 2, CHUNK])
        k_sb = a.place("k_sb", [P, 2, T])
        k_e = a.place("k_e", [P, 2, T])
        k_l = a.place("k_l", [P, 2, T])
        a_t = a.place("a_t", [P, 2, T])
        kept = a.place("kept", [P, P])
        vg = a.place("vg", [P, 2, G_DV])
        o_sb = a.place("o_sb", [P, 4, T])
        o_sq = a.place("o_sq", [P, 4, T])
        a = Arena(y_at)
        log_a = a.place("log_a", [P, G_HEADS, 2 * T])
        rank_rows = a.place("rank_rows", [32, T])
        gk2 = a.place("gk2", [G_RANK + 1, G_HEADS * G_DK])
        a = Arena(y_at)
        o_sg = a.place("o_sg", [P, 4, T])
        o_sum2 = a.place("o_sum2", [P, 2, T])
        o_sum = a.place("o_sum", [P, T])
        o_std = a.place("o_std", [P, T])
        o_rstd = a.place("o_rstd", [P, T])
        o_norm = a.place("o_norm", [P, 4, T])

        a = Arena(arena_start)
        mo_hi = a.place("mo_hi", [P, KT, T], fp32r)
        mo_lo = a.place("mo_lo", [P, KT, T], fp32r)
        y2_at = a.at
        y2 = a.place("y2", [P, KT, T])
        c_hi = a.place("c_hi", [P, 2 * A_TILES, T], fp32r)
        c_lo = a.place("c_lo", [P, 2 * A_TILES, T], fp32r)
        kr_m = a.place("kr_m", [P, 2, 4, T])
        causal = a.place("causal", [P, 3 * P])
        rope_t = a.place("rope_t", [P, 4, T])
        kn = a.place("kn", [P, 4, T])
        qn = a.place("qn", [P, 4, T])
        probs_t = a.place("probs_t", [P, 2, 3 * P])
        kr = Arena(a.at).place("kr", [P, 2, T])
        a_gate = a.place("a_gate", [P, 4, T])
        a_out = a.place("a_out", [P, 4, T])
        row_max = a.place("row_max", [P, 2, 2])
        neg_max = a.place("neg_max", [P, 2, 2])
        row_sum = a.place("row_sum", [P, 2, 2])
        row_inv = a.place("row_inv", [P, 2, 2])
        a = Arena(y2_at)
        latent = a.place("latent", [P, 2 * A_TILES, T])
        l_square = a.place("l_square", [P, 2, T])
        l_sumsq = a.place("l_sumsq", [P, 2, T])
        l_std = a.place("l_std", [P, 2, T])
        l_rstd = a.place("l_rstd", [P, 2, T])
        a = Arena(y2_at)
        q_r = a.place("q_r", [P, 2, T])
        q_rope = a.place("q_rope", [P, 2, T])
        va = a.place("va", [P, 2, 4 * A_V])
        logits = a.place("logits", [P, 2, 3 * P])
        probs = a.place("probs", [P, 2, 3 * P])

        a = Arena(arena_start + 4 * 2 * C_TILES * T)
        pos_i = a.place("pos_i", [P, T], i32)
        ang = a.place("ang", [P, T])
        turns = a.place("turns", [P, T])
        turns_i = a.place("turns_i", [P, T], i32)
        red = a.place("red", [P, 2, T])
        wrap = a.place("wrap", [P, 2, T])

        def pcols(name):
            at = 0
            for n, k in PARAMS:
                if n == name:
                    return par[:, at:at + k]
                at += k

        par_mix = pcols("b_mix").rearrange("p (h c) -> p h c", h=M_HEADS)
        par_conv = pcols("w_conv").rearrange("p (h c) -> p h c", h=M_HEADS)
        par_head = pcols("g_head").rearrange("p (h c) -> p h c", h=M_HEADS)
        par_merge = pcols("b_merge").rearrange("p (m c) -> p m c", c=4)
        par_ffn = pcols("w_ffn").rearrange("p (f c) -> p f c", c=8)

        def gains(name):
            return pcols(name).rearrange("p (i m) -> p i m", m=2)

        def fours(columns):
            return columns.rearrange("p (g m) -> p g m", m=4)

        def pb(name):
            return ctx.enter_context(nc.psum_tensor(name, [P, 512], fp32))

        acc = [pb("acc0"), pb("acc1")]
        tok = [pb("tok0"), pb("tok1")]
        att = [pb(f"att{i}") for i in range(4)]

        loaded = sem("loaded")
        x_loaded = [sem(f"x_loaded{g}") for g in range(KT // 4)]
        gains_ready = sem("gains_ready")
        squares_ready = sem("squares_ready")
        bias_loaded = sem("bias_loaded")
        pos_loaded = sem("pos_loaded")
        gk2_loaded = sem("gk2_loaded")
        raw_ready = [sem("raw_ready0"), sem("raw_ready1")]
        hi_ready = sem("hi_ready")
        lo_ready = sem("lo_ready")
        unit_done = sem("unit_done")
        acc_taken = [used_sem("acc_taken0"), used_sem("acc_taken1")]
        tok_taken = used_sem("tok_taken")
        const_ready = sem("const_ready")
        sq_ready = sem("sq_ready")
        sq_added = used_sem("sq_added")
        stat_ready = sem("stat_ready")
        std_ready = sem("std_ready")
        rstd_ready = sem("rstd_ready")
        normed_ready = sem("normed_ready")
        nhi_ready = sem("nhi_ready")
        act_ready = sem("act_ready")
        act_ready_dve = sem("act_ready_dve")
        scaled_ready = sem("scaled_ready")
        x_normed = sem("x_normed")
        mean_ready = sem("mean_ready")
        x_added = used_sem("x_added")
        x_added_pool = used_sem("x_added_pool")
        stored = sem("stored")
        dve_step = sem("dve_step")
        act_step = sem("act_step")
        pool_step = sem("pool_step")
        rows_ready = sem("rows_ready")
        rows_t_ready = sem("rows_t_ready")
        row_pre = sem("row_pre")
        row_log = sem("row_log")
        a_col_ready = sem("a_col_ready")
        bcast_ready = sem("bcast_ready")
        bcast_taken = sem("bcast_taken")
        decay_masked = sem("decay_masked")
        scores_ready = sem("scores_ready")
        st_ready = sem("st_ready")
        pv_ready = sem("pv_ready")
        den_ready = sem("den_ready")
        h_ready = sem("h_ready")
        hsq_ready = sem("hsq_ready")
        hsum_ready = sem("hsum_ready")
        hstat_ready = sem("hstat_ready")
        hstd_ready = sem("hstd_ready")
        hm_ready = used_sem("hm_ready")
        hmhi_ready = sem("hmhi_ready")
        hmlo_ready = used_sem("hmlo_ready")
        h_normed = sem("h_normed")
        ychi_ready = sem("ychi_ready")
        yclo_ready = used_sem("yclo_ready")
        merged_ready = used_sem("merged_ready")
        mghi_ready = sem("mghi_ready")
        mglo_ready = used_sem("mglo_ready")
        ftap_ready = sem("ftap_ready")
        fsilu_ready = used_sem("fsilu_ready")
        fact_ready = used_sem("fact_ready")
        fhi_ready = sem("fhi_ready")
        flo_ready = used_sem("flo_ready")
        rope_ready = sem("rope_ready")
        rope_red = sem("rope_red")
        gk_ready = sem("gk_ready")
        gk_taken = sem("gk_taken")
        glog_ready = sem("glog_ready")
        gcum_ready = sem("gcum_ready")
        restart_ready = sem("restart_ready")
        rank_ones = sem("rank_ones")
        at_init = sem("at_init")
        qx_ready = used_sem("qx_ready")
        kk_ready = used_sem("kk_ready")
        decays_ready = used_sem("decays_ready")
        to_end_ready = sem("to_end_ready")
        gscores_ready = sem("gscores_ready")
        at_ready = sem("at_ready")
        gpv_ready = sem("gpv_ready")
        osb_ready = sem("osb_ready")
        osq_ready = sem("osq_ready")
        osum_ready = sem("osum_ready")
        ostat_ready = sem("ostat_ready")
        ostd_ready = sem("ostd_ready")
        og_ready = used_sem("og_ready")
        oghi_ready = sem("oghi_ready")
        oglo_ready = used_sem("oglo_ready")
        lsq_added = sem("lsq_added")
        lstat_ready = sem("lstat_ready")
        lstd_ready = sem("lstd_ready")
        cnormed_ready = sem("cnormed_ready")
        chi_ready = sem("chi_ready")
        c_ready = sem("c_ready")
        krm_zero = sem("krm_zero")
        krm_ready = sem("krm_ready")
        causal_ready = sem("causal_ready")
        qrope_ready = used_sem("qrope_ready")
        logits_ready = sem("logits_ready")
        neg_ready = sem("neg_ready")
        exp_ready = used_sem("exp_ready")
        inv_ready = sem("inv_ready")
        probs_ready = sem("probs_ready")
        ptp_ready = sem("ptp_ready")
        ptr_ready = used_sem("ptr_ready")
        apv_ready = sem("apv_ready")
        aout_ready = used_sem("aout_ready")
        mohi_ready = sem("mohi_ready")
        molo_ready = used_sem("molo_ready")

        block = ctx.enter_context(nc.Block())

        def taken(eng, b, name, i, j):
            eng.wait_ge(acc_taken[b], FREE + count(1 + b, name, i, j + 1))

        class Chain:

            def __init__(self, eng, steps):
                self.eng, self.steps, self.n = eng, steps, 0
                self.i, self.per, self.start = None, 0, 0

            def loop(self, i, per):
                self.i, self.per, self.start = i, per, self.n

            def done(self, iterations):
                assert self.n - self.start == self.per, (self.n - self.start, self.per)
                self.n = self.start + iterations * self.per
                self.i = None

            def step(self, ins):
                ins.then_inc(self.steps, 1)
                self.n += 1

            def wait(self):
                self.eng.wait_ge(self.steps, self.n if self.i is None else self.i * self.per + self.n)

            def link(self, ins):
                self.step(ins)
                self.wait()

        NORM = {n: k for k, n in enumerate(["mix", "ffn", "out", "pre0", "post0", "pre1", "post1"])}
        STAT = {n: k for k, n in enumerate(["mix", "ffn", "out", "post0", "pre1", "post1"])}
        POOLED = {n: k for k, n in enumerate(["ffn", "out", "post0", "post1"])}
        TO_ACT = {n: k for k, n in enumerate(["mix", "ffn", "pre0", "pre1"])}

        @block.sync
        def _(sp):
            for g in range(KT // 4):
                sp.dma_start(x[:, 4 * g:4 * g + 4, :], x_in[:, 4 * g:4 * g + 4, :])\
                    .then_inc(x_loaded[g], 16)
            for c in range(2):
                sp.dma_start(raw[:, 2 * c:2 * c + 2, :], stream_in[c].rearrange("p (u n) -> p u n", u=2))\
                    .then_inc(raw_ready[c], 16)
            with sp.Fori(1, N_CHUNKS // 2) as i:
                for c in range(2):
                    sp.wait_ge(lo_ready, 4 * i - 2 + 2 * c)
                    sp.dma_start(raw[:, 2 * c:2 * c + 2, :],
                                 stream_in[2 * i + c].rearrange("p (u n) -> p u n", u=2))\
                        .then_inc(raw_ready[c], 16)
            for g in range(KT // 4):
                sp.wait_ge(x_added, FREE + KT // 2 + 2 * g + 2)
                sp.wait_ge(x_added_pool, FREE + KT // 2 + 2 * g + 2)
                sp.dma_start(out[:, 4 * g:4 * g + 4, :], x[:, 4 * g:4 * g + 4, :]).then_inc(stored, 16)
            sp.wait_ge(stored, 16 * (KT // 4))

        @block.tensor
        def _(pe):
            def unit(name, i, j):
                u, s, _ = unit_of(name, i, j)
                pe.wait_ge(lo_ready, u + 1)
                return s

            def bank(b, name, i, j):
                uses = count(1 + b, name, i, j)
                if i is not None or uses:
                    pe.wait_ge(acc_taken[b], FREE + uses)
                return acc[b]

            def tile(out, s, c, hi, lo, k, first, last):
                wc = slice(c * P, (c + 1) * P)
                nc.tensor.matmul(out, w_hi[:, s, wc], hi[:, k, :], start=first, stop=False)
                nc.tensor.matmul(out, w_hi[:, s, wc], lo[:, k, :], start=False, stop=False)
                return nc.tensor.matmul(out, w_lo[:, s, wc], hi[:, k, :], start=False, stop=last)

            def feature_tile(name, i, j, b, use, hi, lo, wait_act=None, ready=None):
                o = bank(b, name, i, use)[:, 0:T]
                for n in range(2):
                    s = unit(name, i, j + n)
                    for c in range(8):
                        if wait_act is not None and c % 4 == 0:
                            four = wait_act * KT // 4 + 2 * n + c // 4 + 1
                            pe.wait_ge(act_ready, 3 * four)
                            pe.wait_ge(act_ready_dve, four)
                        if ready is not None and c % 4 == 0:
                            pe.wait_ge(ready[0], FREE + (8 * n + c + 4) // ready[1])
                        last = tile(o, s, c, hi, lo, 8 * n + c, n + c == 0, 8 * n + c == KT - 1)
                    last.then_inc(unit_done, 1)

            def token_tiles(name, i, j, units, per_unit, width, hi, lo, k0=0):
                n_k = units * per_unit
                uses = count(3, name, i, 0)
                if i is not None or uses:
                    pe.wait_ge(tok_taken, FREE + 2 * uses)
                for n in range(units):
                    s = unit(name, i, j + n)
                    for c in range(per_unit):
                        k = n * per_unit + c
                        wc = slice(c * width, (c + 1) * width)
                        for t in range(2):
                            tt = slice(t * P, (t + 1) * P)
                            o = tok[t][:, 0:width]
                            nc.tensor.matmul(o, hi[:, k0 + k, tt], w_hi[:, s, wc], start=k == 0, stop=False)
                            nc.tensor.matmul(o, hi[:, k0 + k, tt], w_lo[:, s, wc], start=False, stop=False)
                            last = nc.tensor.matmul(o, lo[:, k0 + k, tt], w_hi[:, s, wc], start=False,
                                                    stop=k == n_k - 1)
                    last.then_inc(unit_done, 1)

            def norm_sum(n):
                pe.wait_ge(sq_added, FREE + KT * (POOLED[n] + 1))
                nc.tensor.matmul(att[3][:, 0:T], ones[:, :], sumsq[:, :], start=True, stop=True)\
                    .then_inc(stat_ready, 1)

            def norm_sum_all(n):
                for k in range(KT):
                    if k % 4 == 0:
                        pe.wait_ge(squares_ready, (n == "pre1") * KT // 4 + k // 4 + 1)
                    last = nc.tensor.matmul(att[3][:, 0:T], ones[:, :], squares_all[:, k, :],
                                            start=k == 0, stop=k == KT - 1)
                last.then_inc(stat_ready, 1)

            pe.wait_ge(const_ready, 4)
            norm_sum_all("mix")

            feature_tile("gates", None, 0, 0, 0, n_hi, n_lo, wait_act=0)
            def mix(i):
                feature_tile("mix", i, 0, 1, 0, n_hi, n_lo)
                feature_tile("mix", i, 2, 0, 0, n_hi, n_lo)
                token_tiles("mix", i, 4, 4, 4, M_DV, n_hi, n_lo)
                taken(pe, 1, "mix", i, 0)
                taken(pe, 0, "mix", i, 0)
                nc.tensor.matmul(att[0][:, 0:T], kT[:, 0:P], qT[:, :], start=True, stop=True)
                nc.tensor.matmul(att[0][:, T:T + P], kT[:, P:T], qT[:, P:T], start=True, stop=True)\
                    .then_inc(scores_ready, 1)
                feature_tile("mix", i, 8, 1, 1, n_hi, n_lo)
                pe.wait_ge(st_ready, 2 * i + 2)
                pe.wait_ge(tok_taken, FREE + count(3, "mix", i, 1) * 2)
                for v in range(2):
                    o = att[1][:, v * T:(v + 1) * T]
                    vv = slice(v * P, (v + 1) * P)
                    nc.tensor.matmul(o, vm[:, 0, vv], st0[:, :], start=True, stop=False)
                    nc.tensor.matmul(o[:, P:T], vm[:, 1, vv], st1[:, :], start=False, stop=True)
                nc.tensor.matmul(att[2][:, 0:T], ones[:, :], st0[:, :], start=True, stop=False)
                nc.tensor.matmul(att[2][:, P:T], ones[:, :], st1[:, :], start=False, stop=True)\
                    .then_inc(pv_ready, 1)
                feature_tile("mix", i, 10, 0, 1, n_hi, n_lo)
                feature_tile("mix", i, 12, 1, 2, n_hi, n_lo)
                feature_tile("mix", i, 14, 0, 2, n_hi, n_lo)
                pe.wait_ge(hsum_ready, i + 1)
                nc.tensor.matmul(att[3][:, 0:T], ones[:, :], h_sum[:, :], start=True, stop=True)\
                    .then_inc(hstat_ready, 1)
                feature_tile("mix", i, 16, 1, 3, n_hi, n_lo)
                feature_tile("mix", i, 18, 0, 3, n_hi, n_lo)
                feature_tile("mix", i, 20, 1, 4, n_hi, n_lo)
                feature_tile("mix", i, 22, 0, 4, n_hi, n_lo)

            pe.wait_ge(rows_ready, 1)
            for t in range(2):
                last = nc.tensor.transpose(att[2][:, 4 * t:4 * t + 4], a_row[:, t * P:(t + 1) * P],
                                           ident[0:M_HEADS, 0:M_HEADS])
            last.then_inc(rows_t_ready, 1)
            for hd in range(M_HEADS):
                if hd >= 2:
                    pe.wait_ge(bcast_taken, hd - 1)
                nc.tensor.matmul(att[hd % 2][:, :], head_row[:, hd, :],
                                 mm_row[:, :, :].rearrange("h a t -> h (a t)"),
                                 start=True, stop=True).then_inc(bcast_ready, 1)
            pe.wait_ge(bcast_taken, M_HEADS)
            with pe.Fori(0, M_HEADS) as i:
                mix(i)
            with pe.Fori(0, KT // 2) as i:
                for m in range(2):
                    feature_tile("merge", i, 6 * m, 1, 2 * m, n_hi, n_lo)
                    feature_tile("merge", i, 6 * m + 2, 0, 2 * m, n_hi, n_lo)
                    for n, (hi, lo) in enumerate(((hm_hi, hm_lo), (yc_hi, yc_lo))):
                        if n == 0:
                            pe.wait_ge(hmlo_ready, FREE + M_HEADS)
                        else:
                            pe.wait_ge(yclo_ready, FREE + 2 * M_HEADS)
                        o = bank(1 - n, "merge", i, 2 * m + 1)[:, 0:T]
                        s = unit("merge", i, 6 * m + 4 + n)
                        for c in range(8):
                            last = tile(o, s, c, hi, lo, c, c == 0, c == 7)
                        last.then_inc(unit_done, 1)
            with pe.Fori(0, KT // 2) as i:
                for m in range(2):
                    feature_tile("wout", i, 2 * m, 1 - m, 0, mg_hi, mg_lo, ready=(mglo_ready, 1))
            norm_sum("ffn")
            def up(i):
                for m in range(2):
                    feature_tile("wup", i, 2 * m, 1 - m, 0, n_hi, n_lo, wait_act=1)

            with pe.Fori(0, F_TILES // 2) as pair:
                up(2 * pair)
                up(2 * pair + 1)
            up(F_TILES - 1)
            with pe.Fori(0, KT // 2) as i:
                for m in range(2):
                    o = bank(1 - m, "wdown", i, 0)[:, 0:T]
                    for n in range(6):
                        s = unit("wdown", i, 6 * m + n)
                        pe.wait_ge(flo_ready, FREE + min(8 * n + 8, F_TILES))
                        for k in range(8 * n, min(8 * n + 8, F_TILES)):
                            last = tile(o, s, k - 8 * n, f_hi, f_lo, k, k == 0, k == F_TILES - 1)
                        last.then_inc(unit_done, 1)
            pe.wait_ge(sq_added, FREE + KT * (POOLED["out"] + 1))
            nc.tensor.matmul(att[3][:, 0:T], ones[:, :], sumsq[:, :], start=True, stop=True)
            nc.tensor.matmul(att[3][:, T:2 * T], ones[:, :], sumsq_g[:, :], start=True, stop=True)\
                .then_inc(stat_ready, 1)
            feature_tile("rank", None, 0, 1, 0, n_hi, n_lo, wait_act=2)
            taken(pe, 1, "rank", None, 0)
            pe.wait_ge(gk2_loaded, 16)
            for hd in range(G_HEADS):
                for t in range(2):
                    c = (2 * hd + t) * P
                    last = nc.tensor.matmul(att[hd][:, t * T:(t + 1) * T], gk2[:, c:c + P],
                                            rank_rows[0:G_RANK + 1, :], start=True, stop=True)
                last.then_inc(gk_ready, 1)
            with pe.Fori(0, G_HEADS) as i:
                for n in range(4):
                    feature_tile("gla", i, 2 * n, n % 2, n // 2, n_hi, n_lo)
                token_tiles("gla", i, 8, 8, 2, G_DV, n_hi, n_lo)
                pe.wait_ge(gk_taken, G_HEADS)
                pe.wait_ge(qx_ready, FREE + 4 * i + 4)
                pe.wait_ge(kk_ready, FREE + 2 * i + 2)
                for kc in range(4):
                    part = slice(CHUNK * (kc % 2), CHUNK * (kc % 2 + 1))
                    col = T * (kc // 2)
                    src = slice(CHUNK * kc, CHUNK * (kc + 1))
                    nxt = slice(CHUNK * (kc + 1), CHUNK * (kc + 2))
                    jobs = [(k_e, src, q_e, src, CHUNK * kc)]
                    if kc < 3:
                        jobs.append((k_l, src, q_e, nxt, CHUNK * (kc + 1)))
                    if kc == 0:
                        jobs.append((k_l, src, q_x, slice(0, 2 * CHUNK), 2 * CHUNK))
                    if kc == 1:
                        jobs.append((k_l, src, q_y, slice(0, CHUNK), 3 * CHUNK))
                    for keys, ks, queries, qs, at in jobs:
                        width = qs.stop - qs.start
                        for dk in range(2):
                            last = nc.tensor.matmul(att[0][part, col + at:col + at + width],
                                                    keys[:, dk, ks], queries[:, dk, qs],
                                                    start=dk == 0, stop=dk == 1)
                last.then_inc(gscores_ready, 1)
                feature_tile("gla", i, 16, 0, 2, n_hi, n_lo)
                pe.wait_ge(at_ready, 5 * i + 5)
                pe.wait_ge(tok_taken, FREE + 2 * count(3, "gla", i, 1))
                for v in range(4):
                    o = att[1 + v // 2][:, (v % 2) * T:(v % 2 + 1) * T]
                    vv = slice(v * P, (v + 1) * P)
                    nc.tensor.matmul(o, vg[:, 0, vv], a_t[:, 0, :], start=True, stop=False)
                    last = nc.tensor.matmul(o[:, P:T], vg[:, 1, vv], a_t[:, 1, P:T], start=False, stop=True)
                last.then_inc(gpv_ready, 1)
                feature_tile("gla", i, 18, 1, 2, n_hi, n_lo)
                feature_tile("gla", i, 20, 0, 3, n_hi, n_lo)
                pe.wait_ge(osum_ready, i + 1)
                nc.tensor.matmul(att[3][:, 0:T], ones[:, :], o_sum[:, :], start=True, stop=True)\
                    .then_inc(ostat_ready, 1)
                feature_tile("gla", i, 22, 1, 3, n_hi, n_lo)
            with pe.Fori(0, KT // 2) as i:
                for m in range(2):
                    feature_tile("glaout", i, 2 * m, m, 0, og_hi, og_lo, ready=(oglo_ready, 4))
            norm_sum("post0")
            norm_sum_all("pre1")
            def latent_sum(n):
                pe.wait_ge(lsq_added, A_TILES * (n + 1))
                if n:
                    pe.wait_ge(lstd_ready, 1)
                nc.tensor.matmul(att[3][:, 0:T], ones[:, :], l_sumsq[:, n, :], start=True, stop=True)\
                    .then_inc(lstat_ready, 1)

            for k in range(2 * A_TILES):
                feature_tile("latent", None, 2 * k, k % 2, k // 2, n_hi, n_lo, wait_act=3)
                if k == A_TILES:
                    latent_sum(0)
            feature_tile("krope", None, 0, 0, 0, n_hi, n_lo)
            latent_sum(1)
            feature_tile("krope", None, 2, 1, 0, n_hi, n_lo)
            def pair_tile(i, j, b, use, k0):
                pe.wait_ge(c_ready, k0 + A_TILES)
                o = bank(b, "mla", i, use)
                s = unit("mla", i, j)
                for c in range(8):
                    m, k = divmod(c, A_TILES)
                    last = tile(o[:, m * T:(m + 1) * T], s, c, c_hi, c_lo, k0 + k, k == 0,
                                k == A_TILES - 1)
                return last

            def scores(i, n):
                pe.wait_ge(ptr_ready, FREE + 4 * i + max(n - 1, 0))
                for t, (at, width) in enumerate(((0, P), (P, T))):
                    tt = slice(t * P, (t + 1) * P)
                    o = att[n % 2][:, at:at + width]
                    nc.tensor.matmul(o, qn[:, n, tt], kn[:, n, 0:width], start=True, stop=False)
                    nc.tensor.matmul(o, q_rope[:, 0, tt], kr_m[:, 0, n, 0:width], start=False, stop=False)
                    last = nc.tensor.matmul(o, q_rope[:, 1, tt], kr_m[:, 1, n, 0:width],
                                            start=False, stop=True)
                last.then_inc(logits_ready, 1)

            def transposes(i, n):
                pe.wait_ge(probs_ready, 4 * i + n + 1)
                for b in range(3):
                    last = nc.tensor.transpose(att[n % 2][:, b * P:(b + 1) * P],
                                               probs[:, n % 2, b * P:(b + 1) * P], ident[:, :])
                last.then_inc(ptp_ready, 1)

            def outputs(i, n):
                pe.wait_ge(aout_ready, FREE + 4 * i + 2 * (n // 2))
                pe.wait_ge(ptr_ready, FREE + 4 * i + n + 1)
                o = att[2 + n % 2][:, 0:T]
                vv = slice(n * A_V, (n + 1) * A_V)
                nc.tensor.matmul(o, va[:, 0, vv], probs_t[:, n % 2, 0:T], start=True, stop=False)
                nc.tensor.matmul(o[:, P:T], va[:, 1, vv], probs_t[:, n % 2, T:3 * P], start=False, stop=True)\
                    .then_inc(apv_ready, 1)

            with pe.Fori(0, A_HEADS // 4) as i:
                for n in range(2):
                    pair_tile(i, 2 * n, 0, n, 0).then_inc(unit_done, 1)
                    pair_tile(i, 2 * n + 1, 1, n, A_TILES).then_inc(unit_done, 1)
                last = pair_tile(i, 4, 0, 2, 0)
                unit("mla", i, 5)
                last.then_inc(unit_done, 2)
                token_tiles("mla", i, 6, 2, 2, 4 * A_V, c_hi, c_lo, k0=A_TILES)
                taken(pe, 0, "mla", i, 2)
                taken(pe, 1, "mla", i, 1)
                pe.wait_ge(qrope_ready, FREE + 2 * i + 2)
                pe.wait_ge(krm_ready, 8)
                scores(i, 0)
                scores(i, 1)
                feature_tile("mla", i, 8, 1, 2, n_hi, n_lo)
                transposes(i, 0)
                transposes(i, 1)
                feature_tile("mla", i, 10, 0, 3, n_hi, n_lo)
                pe.wait_ge(tok_taken, FREE + 2 * count(3, "mla", i, 1))
                outputs(i, 0)
                outputs(i, 1)
                scores(i, 2)
                scores(i, 3)
                feature_tile("mla", i, 12, 1, 3, n_hi, n_lo)
                transposes(i, 2)
                transposes(i, 3)
                feature_tile("mla", i, 14, 0, 4, n_hi, n_lo)
                outputs(i, 2)
                outputs(i, 3)
            with pe.Fori(0, KT // 2) as i:
                for m in range(2):
                    feature_tile("mlaout", i, 2 * m, 1 - m, 0, mo_hi, mo_lo, ready=(molo_ready, 1))
            norm_sum("post1")

        @block.scalar
        def _(act):
            chain = Chain(act, act_step)

            def split(name, i, j):
                u, s, use = unit_of(name, i, j + RING)
                high(u, s, use)

            def high(u, s, use):
                if s % 2 == 0:
                    act.wait_ge(raw_ready[s // 2], 16 * use + 16)
                if not isinstance(u, int) or u >= RING:
                    act.wait_ge(unit_done, u - RING + 1)
                nc.scalar.activation(w_hi[:, s, :], raw[:, s, :], ACT.Copy).then_inc(hi_ready, 1)

            def unit_is_done(name, i, j):
                act.wait_ge(unit_done, unit_of(name, i, j)[0] + 1)

            def one_square(n, i, m, source, gain=None):
                act.wait_ge(sq_added, FREE + 2 * i + max(POOLED[n] * KT + m - 1, 0))
                ins = nc.scalar.activation(square[:, m, :], source, ACT.Square)
                if gain is not None:
                    ins = nc.scalar.activation(square_g[:, m, :], source, ACT.Square, scale=gain)
                ins.then_inc(sq_ready, 1)

            def norm_std(n):
                act.wait_ge(stat_ready, STAT[n] + 1)
                if NORM[n]:
                    act.wait_ge(rstd_ready, NORM[n])
                nc.scalar.activation(std[:, :], att[3][:, 0:T], ACT.Sqrt, bias=eps, scale=1.0 / D)\
                    .then_inc(std_ready, 1)

            def four_high(n, g):
                for m in range(4):
                    act.wait_ge(normed_ready, 4 * g + TO_ACT[n] * KT + m + 1)
                    nc.scalar.activation(n_hi[:, 4 * g + m, :], normed[:, m, :], ACT.Copy)\
                        .then_inc(nhi_ready, 1)

            def norm_high(n):
                with act.Fori(0, KT // 4) as g:
                    four_high(n, g)

            act.dma_start(par[:, :], params_in).then_inc(loaded, 16)
            act.dma_start(pos_i[:, :], positions_in.to_broadcast([P, T])).then_inc(pos_loaded, 16)
            act.dma_start(v_bias[:, :, :].rearrange("p h v -> p (h v)"),
                          v_bias_in.to_broadcast([P, M_HEADS * M_DV])).then_inc(bias_loaded, 16)
            eps = eps_col[:, :]
            for g in range(KT // 4):
                act.wait_ge(x_loaded[g], 16)
                nc.scalar.activation(squares_all[:, 4 * g:4 * g + 4, :], x[:, 4 * g:4 * g + 4, :],
                                     ACT.Square).then_inc(squares_ready, 1)
            act.wait_ge(const_ready, 1)
            norm_std("mix")
            for g in range(RING):
                four_high("mix", g)
                high(g, g, 0)

            act.wait_ge(rope_red, 1)
            nc.scalar.activation(sine[:, :], red[:, 0, :], ACT.Sin).then_inc(rope_ready, 1)
            nc.scalar.activation(cosine[:, :], red[:, 1, :], ACT.Sin).then_inc(rope_ready, 1)

            unit_is_done("gates", None, 1)
            nc.scalar.activation(i_row[0:32, :], acc[0][0:32, 0:T], ACT.Identity,
                                 bias=pcols("b_gate")[0:32, :]).then_inc(row_pre, 1)
            nc.scalar.activation(f_row[32:64, :], acc[0][32:64, 0:T], ACT.Identity,
                                 bias=pcols("b_gate")[32:64, :]).then_inc(acc_taken[0], 1)
            taken(act, 0, "gates", None, 0)
            chain.link(nc.scalar.activation(f_abs[32:64, :], f_row[32:64, :], ACT.Abs))
            chain.link(nc.scalar.activation(f_exp[32:64, :], f_abs[32:64, :], ACT.Exp, scale=-1.0))
            nc.scalar.activation(f_log[32:64, :], f_exp[32:64, :], ACT.Ln, bias=1.0).then_inc(row_log, 1)
            split("gates", None, 0)
            split("gates", None, 1)
            act.wait_ge(rows_t_ready, 1)
            chain.link(nc.scalar.activation(a_col[:, :, :].rearrange("p t h -> p (t h)"),
                                            att[2][:, 0:2 * M_HEADS], ACT.Copy))
            for hd in range(M_HEADS):
                act.wait_ge(bcast_ready, hd + 1)
                rows = att[hd % 2]
                nc.scalar.activation(decay0[:, hd, :], rows[:, 0:T], ACT.Exp, scale=-1.0,
                                     bias=a_col[:, 0, hd:hd + 1]).then_inc(a_col_ready, 1)
                nc.scalar.activation(decay1[:, hd, :], rows[:, P:T], ACT.Exp, scale=-1.0,
                                     bias=a_col[:, 1, hd:hd + 1]).then_inc(a_col_ready, 1)
                nc.scalar.activation(floor[:, hd, :], rows[:, T:2 * T], ACT.Exp, scale=-1.0)\
                    .then_inc(bcast_taken, 1)
            with act.Fori(0, M_HEADS) as i:
                for j in range(24):
                    if j == 1:
                        unit_is_done("mix", i, j)
                        nc.scalar.activation(qT[:, :], acc[1][:, 0:T], ACT.Identity,
                                             bias=par_mix[:, i, 0:1]).then_inc(acc_taken[1], 1)
                    if j == 3:
                        unit_is_done("mix", i, j)
                        nc.scalar.activation(kT[:, :], acc[0][:, 0:T], ACT.Identity,
                                             bias=par_mix[:, i, 1:2]).then_inc(acc_taken[0], 1)
                    if j in (9, 11):
                        n = (j - 9) // 2
                        unit_is_done("mix", i, j)
                        if n == 0:
                            act.wait_ge(hm_ready, FREE + 2 * i)
                        nc.scalar.activation(sig_o[:, n, :], acc[1 - n][:, 0:T], ACT.Sigmoid,
                                             bias=par_mix[:, i, 2 + n:3 + n]).then_inc(acc_taken[1 - n], 1)
                    if j == 10:
                        act.wait_ge(pv_ready, i + 1)
                        nc.scalar.activation(den_abs[:, :], att[2][:, 0:T], ACT.Abs)\
                            .then_inc(den_ready, 1)
                    if j in (13, 19):
                        n = (j - 13) // 6
                        unit_is_done("mix", i, j)
                        if n == 1:
                            taken(act, 0, "mix", i, 2)
                        nc.scalar.activation(cc[:, :], acc[1 - n][:, 0:T], ACT.Identity,
                                             bias=par_mix[:, i, 4 + 3 * n:5 + 3 * n])\
                            .then_inc(acc_taken[1 - n], 1)
                    if j == 12:
                        act.wait_ge(h_ready, i + 1)
                        nc.scalar.activation(h_sq[:, :, :], h[:, :, :], ACT.Square).then_inc(hsq_ready, 1)
                    if j == 16:
                        act.wait_ge(hstat_ready, i + 1)
                        nc.scalar.activation(h_std[:, :], att[3][:, 0:T], ACT.Sqrt, bias=eps,
                                             scale=1.0 / M_DV).then_inc(hstd_ready, 1)
                    if j == 18:
                        act.wait_ge(hm_ready, FREE + 2 * i + 2)
                        nc.scalar.activation(hm_hi[:, bass.ds(2 * i, 2), :], hm[:, :, :], ACT.Copy)\
                            .then_inc(hmhi_ready, 1)
                    if j in (19, 23):
                        n = (j - 19) // 4
                        taken(act, 1 - n, "mix", i, 3 + n)
                        nc.scalar.activation(yc_hi[:, 2 * i + n, :], cz[:, :], ACT.Copy)\
                            .then_inc(ychi_ready, 1)
                    split("mix", i, j)
            with act.Fori(0, KT // 2) as i:
                for j in range(12):
                    m, jj = divmod(j, 6)
                    if jj in (1, 3):
                        n = jj // 2
                        unit_is_done("merge", i, j)
                        act.wait_ge(acc_taken[1 - n], FREE + count(2 - n, "merge", i, 2 * m))
                        nc.scalar.activation((sig_m, sig_c)[n][:, :], acc[1 - n][:, 0:T], ACT.Sigmoid,
                                             bias=par_merge[:, i, 2 * m + n:2 * m + n + 1])\
                            .then_inc(acc_taken[1 - n], 1)
                    if jj == 5:
                        act.wait_ge(merged_ready, FREE + 2 * i + m + 1)
                        nc.scalar.activation(mg_hi[:, 2 * i + m, :], merged[:, :], ACT.Copy)\
                            .then_inc(mghi_ready, 1)
                    split("merge", i, j)

            def residual_squares(name, n, per, gain=None):
                with act.Fori(0, KT // 2) as i:
                    for j in range(per):
                        if j in (per // 2 - 1, per - 1):
                            m = 2 * j // per
                            taken(act, 1 - m, name, i, 0)
                            one_square(n, i, m, x[:, 2 * i + m, :],
                                       gains(gain)[:, i, m:m + 1] if gain else None)
                        split(name, i, j)

            residual_squares("wout", "ffn", 4)
            norm_std("ffn")
            norm_high("ffn")
            def up(i):
                for j in range(4):
                    if j in (1, 3):
                        n = j // 2
                        unit_is_done("wup", i, j)
                        if n == 0:
                            act.wait_ge(fsilu_ready, FREE + i)
                        else:
                            act.wait_ge(fact_ready, FREE + i)
                        nc.scalar.activation((f_gate, f_val)[n][:, :], acc[1 - n][:, 0:T], ACT.Identity,
                                             bias=par_ffn[:, i, 4 * n + 3:4 * n + 4],
                                             scale=par_ffn[:, i, 4 * n + 2:4 * n + 3])
                        nc.scalar.activation(f_pre[:, n, :], acc[1 - n][:, 0:T], ACT.Copy)\
                            .then_inc(acc_taken[1 - n], 1)
                    if j == 2:
                        act.wait_ge(ftap_ready, 2 * i + 1)
                        act.wait_ge(fact_ready, FREE + i)
                        nc.scalar.activation(f_silu[:, :], f_gate[:, :], ACT.Silu)\
                            .then_inc(fsilu_ready, 1)
                    split("wup", i, j)
                    if j == 3:
                        act.wait_ge(fact_ready, FREE + i + 1)
                        nc.scalar.activation(f_hi[:, i, :], f_act[:, :], ACT.Copy)\
                            .then_inc(fhi_ready, 1)

            with act.Fori(0, F_TILES // 2) as pair:
                up(2 * pair)
                up(2 * pair + 1)
            up(F_TILES - 1)
            residual_squares("wdown", "out", 12, "g_out")
            norm_std("out")
            act.wait_ge(mean_ready, 1)
            nc.scalar.activation(std[:, :], mean_g[:, :], ACT.Sqrt, bias=eps, scale=1.0 / D)\
                .then_inc(std_ready, 1)
            norm_high("pre0")
            act.dma_start(gk2[:, :], gk2_in).then_inc(gk2_loaded, 16)
            act.wait_ge(rank_ones, 1)
            unit_is_done("rank", None, 1)
            nc.scalar.activation(rank_rows[0:G_RANK, :], acc[1][0:G_RANK, 0:T], ACT.Copy)\
                .then_inc(acc_taken[1], 1)
            split("rank", None, 0)
            split("rank", None, 1)
            for hd in range(G_HEADS):
                act.wait_ge(gk_ready, hd + 1)
                chain.step(nc.scalar.activation(g_log[:, hd, :], att[hd][:, :], ACT.Abs))
            chain.wait()
            for hd in range(G_HEADS):
                chain.step(nc.scalar.activation(g_log[:, hd, :], g_log[:, hd, :], ACT.Exp, scale=-1.0))
            chain.wait()
            for hd in range(G_HEADS):
                nc.scalar.activation(g_log[:, hd, :], g_log[:, hd, :], ACT.Ln, bias=1.0)\
                    .then_inc(glog_ready, 1)
            with act.Fori(0, G_HEADS) as i:
                for j in range(24):
                    if j == 0:
                        act.wait_ge(gcum_ready, G_HEADS)
                        act.wait_ge(qx_ready, FREE + 4 * i)
                        act.wait_ge(kk_ready, FREE + 2 * i)
                        nc.scalar.activation(e_pos[:, :, :], gcum[:, i, :, :], ACT.Exp,
                                             scale=1.0 / G_TAU).then_inc(decays_ready, 1)
                        nc.scalar.activation(e_neg[:, :, :], gcum[:, i, :, :], ACT.Exp,
                                             scale=-1.0 / G_TAU).then_inc(decays_ready, 1)
                        act.wait_ge(to_end_ready, i + 1)
                        nc.scalar.activation(e_end[:, :, :], to_end[:, :, :], ACT.Exp,
                                             scale=1.0 / G_TAU).then_inc(decays_ready, 1)
                    if j in (5, 7):
                        n = (j - 5) // 2
                        unit_is_done("gla", i, j)
                        nc.scalar.activation(k_sb[:, n, :], acc[n][:, 0:T], ACT.Copy)\
                            .then_inc(acc_taken[n], 1)
                    if j == 18:
                        act.wait_ge(gpv_ready, i + 1)
                        act.wait_ge(og_ready, FREE + i)
                        for n in range(2):
                            nc.scalar.activation(o_sb[:, 2 * n:2 * n + 2, :], att[1 + n][:, :], ACT.Copy)\
                                .then_inc(osb_ready, 1)
                        for n in range(2):
                            nc.scalar.activation(o_sq[:, 2 * n:2 * n + 2, :], att[1 + n][:, :], ACT.Square)\
                                .then_inc(osq_ready, 1)
                    if j in (17, 19, 21, 23):
                        n = (j - 17) // 2
                        unit_is_done("gla", i, j)
                        if n == 0:
                            act.wait_ge(og_ready, FREE + i)
                        nc.scalar.activation(o_sg[:, n, :], acc[n % 2][:, 0:T], ACT.Silu)\
                            .then_inc(acc_taken[n % 2], 1)
                    if j == 22:
                        act.wait_ge(ostat_ready, i + 1)
                        nc.scalar.activation(o_std[:, :], att[3][:, 0:T], ACT.Sqrt, bias=eps,
                                             scale=1.0 / G_DV).then_inc(ostd_ready, 1)
                    if j == 23:
                        act.wait_ge(og_ready, FREE + i + 1)
                        nc.scalar.activation(og_hi[:, bass.ds(4 * i, 4), :], o_norm[:, :, :], ACT.Copy)\
                            .then_inc(oghi_ready, 1)
                    split("gla", i, j)

            def mixer_output(name, n, to, flip, last_phase=False):
                def body(i, splits):
                    for j in range(4):
                        if j in (1, 3):
                            m = j // 2
                            unit_is_done(name, i, j)
                            b = 1 - m if flip else m
                            one_square(n, i, m, acc[b][:, 0:T])
                            nc.scalar.activation(to[:, 2 * i + m, :], acc[b][:, 0:T], ACT.Copy)\
                                .then_inc(acc_taken[b], 1)
                        if splits:
                            split(name, i, j)

                with act.Fori(0, KT // 2 - last_phase) as i:
                    body(i, True)
                if last_phase:
                    body(KT // 2 - 1, False)

            mixer_output("glaout", "post0", y, False)
            norm_std("post0")
            for g in range(KT // 4):
                act.wait_ge(x_added, FREE + 2 * g + 2)
                act.wait_ge(x_added_pool, FREE + 2 * g + 2)
                nc.scalar.activation(squares_all[:, 4 * g:4 * g + 4, :], x[:, 4 * g:4 * g + 4, :],
                                     ACT.Square).then_inc(squares_ready, 1)
            norm_std("pre1")
            norm_high("pre1")
            def latent_std(n):
                act.wait_ge(lstat_ready, n + 1)
                nc.scalar.activation(l_std[:, n, :], att[3][:, 0:T], ACT.Sqrt, bias=eps,
                                     scale=1.0 / A_RANK).then_inc(lstd_ready, 1)

            def latent_high(n):
                for k in range(A_TILES * n, A_TILES * (n + 1)):
                    act.wait_ge(cnormed_ready, k + 1)
                    nc.scalar.activation(c_hi[:, k, :], normed[:, k % 4, :], ACT.Copy)\
                        .then_inc(chi_ready, 1)

            for j in range(16):
                if j % 2:
                    k = j // 2
                    unit_is_done("latent", None, j)
                    nc.scalar.activation(latent[:, k, :], acc[k % 2][:, 0:T], ACT.Copy)
                    if k >= 2:
                        act.wait_ge(lsq_added, k - 1)
                    nc.scalar.activation(l_square[:, k % 2, :], acc[k % 2][:, 0:T], ACT.Square)\
                        .then_inc(acc_taken[k % 2], 1)
                split("latent", None, j)
                if j == 2 * A_TILES + 1:
                    latent_std(0)
                if j == 2 * A_TILES + 3:
                    latent_high(0)
            for j in range(4):
                if j in (1, 3):
                    n = j // 2
                    unit_is_done("krope", None, j)
                    nc.scalar.activation(kr[:, n, :], acc[n][:, 0:T], ACT.Copy).then_inc(acc_taken[n], 1)
                split("krope", None, j)
                if j == 1:
                    latent_std(1)
                    latent_high(1)
            with act.Fori(0, A_HEADS // 4) as i:
                for j in range(16):
                    if j in (0, 2):
                        n = j // 2
                        unit_is_done("mla", i, j)
                        nc.scalar.activation(qn[:, 2 * n:2 * n + 2, :], acc[0][:, :], ACT.Copy)\
                            .then_inc(acc_taken[0], 1)
                    if j == 4:
                        unit_is_done("mla", i, j)
                        act.wait_ge(qrope_ready, FREE + 2 * i)
                        nc.scalar.activation(q_r[:, :, :], acc[0][:, :], ACT.Copy)\
                            .then_inc(acc_taken[0], 1)
                    if j in (8, 12):
                        for n in range((j - 8) // 2, (j - 8) // 2 + 2):
                            act.wait_ge(neg_ready, 4 * i + n + 1)
                            for t, blocks in enumerate((slice(0, P), slice(P, 3 * P))):
                                nc.scalar.activation(probs[:, n % 2, blocks], logits[:, n % 2, blocks],
                                                     ACT.Exp, bias=neg_max[:, n % 2, t:t + 1],
                                                     accum_out=row_sum[:, n % 2, t:t + 1])\
                                    .then_inc(exp_ready, 1)
                    if j in (10, 14):
                        for n in range((j - 10) // 2, (j - 10) // 2 + 2):
                            act.wait_ge(ptp_ready, 4 * i + n + 1)
                            nc.scalar.activation(probs_t[:, n % 2, :], att[n % 2][:, 0:3 * P], ACT.Copy)\
                                .then_inc(ptr_ready, 1)
                    if j in (9, 11, 13, 15):
                        n = (j - 9) // 2
                        unit_is_done("mla", i, j)
                        if n == 0:
                            act.wait_ge(aout_ready, FREE + 4 * i)
                        b = 1 - n % 2
                        nc.scalar.activation(a_gate[:, n, :], acc[b][:, 0:T], ACT.Silu)\
                            .then_inc(acc_taken[b], 1)
                    if j in (13, 15):
                        for n in range(j - 13, j - 11):
                            act.wait_ge(aout_ready, FREE + 4 * i + n + 1)
                            nc.scalar.activation(mo_hi[:, 4 * i + n, :], a_out[:, n, :], ACT.Copy)\
                                .then_inc(mohi_ready, 1)
                    split("mla", i, j)
            mixer_output("mlaout", "post1", y2, True, last_phase=True)
            norm_std("post1")

        @block.vector
        def _(dve):
            chain = Chain(dve, dve_step)

            def split(name, i, j):
                u, s, _ = unit_of(name, i, j + RING)
                rest(u, s)

            def rest(u, s):
                dve.wait_ge(hi_ready, u + 1)
                nc.vector.tensor_tensor(w_lo[:, s, :], raw[:, s, :], w_hi[:, s, :].bitcast(fp32),
                                        ALU.subtract).then_inc(lo_ready, 1)

            def unit_is_done(name, i, j):
                dve.wait_ge(unit_done, unit_of(name, i, j)[0] + 1)

            def norm_rstd(n):
                dve.wait_ge(std_ready, NORM[n] + 1)
                nc.vector.reciprocal(rstd[:, :], std[:, :]).then_inc(rstd_ready, 1)
                dve.wait_ge(rstd_ready, NORM[n] + 1)

            def four_normed(n, g, gain, scale):
                at = TO_ACT[n] * KT // 4
                for m in range(4):
                    if isinstance(g, int) and g + at == 0:
                        pass
                    elif m == 0:
                        dve.wait_ge(act_ready_dve, g + at)
                    else:
                        dve.wait_ge(act_ready, 3 * g + max(3 * at + m - 3, 0))
                    nc.vector.scalar_tensor_tensor(
                        out=normed[:, m, :], in0=x[:, 4 * g + m, :], scalar=gain[:, g, m:m + 1],
                        in1=scale[:, :], op0=ALU.mult, op1=ALU.mult).then_inc(normed_ready, 1)
                dve.wait_ge(nhi_ready, 4 * (g + at) + 1)
                nc.vector.tensor_tensor(n_lo[:, 4 * g, :], normed[:, 0, :], n_hi[:, 4 * g, :].bitcast(fp32),
                                        ALU.subtract).then_inc(act_ready_dve, 1)

            def norm_tiles(n, gain, scale):
                with dve.Fori(0, KT // 4) as g:
                    four_normed(n, g, gain, scale)

            dve.wait_ge(loaded, 16)
            dve.wait_ge(pos_loaded, 16)
            chain.link(nc.vector.tensor_scalar(ang[:, :], pos_i[:, :], pcols("inv_freq"), None, ALU.mult))
            chain.link(nc.vector.tensor_scalar(turns_i[:, :], ang[:, :], 0.15915494309189535, None, ALU.mult))
            chain.link(nc.vector.tensor_copy(turns[:, :], turns_i[:, :]))
            source = ang[:, :]
            for part in (6.28125, 0.0019340515136718750, 1.2556659146e-06):
                chain.link(nc.vector.scalar_tensor_tensor(out=red[:, 0, :], in0=turns[:, :], scalar=-part,
                                                          in1=source, op0=ALU.mult, op1=ALU.add))
                source = red[:, 0, :]
            chain.link(nc.vector.tensor_scalar(red[:, 1, :], red[:, 0, :], 1.5707963267948966, None, ALU.add))
            for compare, edge, turn in ((ALU.is_gt, PI, -2 * PI), (ALU.is_lt, -PI, 2 * PI)):
                chain.link(nc.vector.tensor_scalar(wrap[:, :, :], red[:, :, :], edge, turn, compare, ALU.mult))
                chain.link(nc.vector.tensor_tensor(red[:, :, :], red[:, :, :], wrap[:, :, :], ALU.add))
            nc.vector.tensor_scalar(red[:, :, :], red[:, :, :], -PI_INSIDE, PI_INSIDE, ALU.max, ALU.min)\
                .then_inc(rope_red, 1)
            nc.vector.tensor_tensor(g_both[:, :], pcols("g_out"), pcols("g_pre0"), ALU.mult)\
                .then_inc(gains_ready, 1)
            norm_rstd("mix")
            for g in range(RING):
                four_normed("mix", g, fours(pcols("g_mix")), rstd)
                rest(g, g)
            dve.wait_ge(row_log, 1)
            chain.link(nc.vector.tensor_scalar(f_min[32:64, :], f_row[32:64, :], 0.0, None, ALU.min))
            chain.link(nc.vector.tensor_tensor(logf[32:64, :], f_min[32:64, :], f_log[32:64, :],
                                               ALU.subtract))
            chain.link(nc.vector.tensor_copy(logf0[:, :], logf[32:32 + M_HEADS, :]))
            chain.link(nc.vector.memset(ones_row[:, :], 1.0))
            chain.link(nc.vector.tensor_tensor_scan(b_row[:, :], ones_row[:, :], logf0[:, :], 0.0,
                                                    ALU.mult, ALU.add))
            dve.wait_ge(row_pre, 1)
            chain.link(nc.vector.tensor_tensor(a_row[:, :], i_row[0:M_HEADS, :], b_row[:, :], ALU.subtract))
            chain.link(nc.vector.tensor_tensor_scan(mm_row[:, 0, :], a_row[:, :], a_row[:, :], 0.0,
                                                    ALU.max, ALU.max))
            nc.vector.tensor_tensor(mm_row[:, 1, :], mm_row[:, 0, :], b_row[:, :], ALU.add)\
                .then_inc(rows_ready, 1)
            split("gates", None, 0)
            split("gates", None, 1)

            dve.wait_ge(bias_loaded, 16)
            dve.wait_ge(decay_masked, 2)
            with dve.Fori(0, M_HEADS) as i:
                chain.loop(i, 10)
                for j in range(24):
                    if j == 7:
                        unit_is_done("mix", i, j)
                        for t in range(2):
                            nc.vector.tensor_tensor(vm[:, t, :], tok[t][:, 0:M_DV], v_bias[:, i, :],
                                                    ALU.add).then_inc(tok_taken, 1)
                    if j == 8:
                        dve.wait_ge(scores_ready, i + 1)
                        nc.vector.scalar_tensor_tensor(out=st0[:, :], in0=att[0][:, 0:T],
                                                       scalar=M_DQK ** -0.5, in1=decay0[:, i, :],
                                                       op0=ALU.mult, op1=ALU.mult).then_inc(st_ready, 1)
                        nc.vector.scalar_tensor_tensor(out=st1[:, :], in0=att[0][:, T:T + P],
                                                       scalar=M_DQK ** -0.5, in1=decay1[:, i, :],
                                                       op0=ALU.mult, op1=ALU.mult).then_inc(st_ready, 1)
                    if j == 10:
                        dve.wait_ge(den_ready, i + 1)
                        chain.link(nc.vector.tensor_tensor(den[:, :], den_abs[:, :], floor[:, i, :],
                                                           ALU.max))
                        chain.link(nc.vector.reciprocal(rden[:, :], den[:, :]))
                        for v in range(2):
                            ins = nc.vector.tensor_tensor(h[:, v, :], att[1][:, v * T:(v + 1) * T],
                                                          rden[:, :], ALU.mult)
                            if v == 0:
                                chain.link(ins)
                            else:
                                ins.then_inc(h_ready, 1)
                    if j in (15, 21):
                        n = (j - 15) // 6
                        unit_is_done("mix", i, j)
                        taken(dve, 1 - n, "mix", i, 2 + n)
                        nc.vector.scalar_tensor_tensor(
                            out=cu[:, :], in0=acc[n][:, 0:T], scalar=par_mix[:, i, 5 + 3 * n:6 + 3 * n],
                            in1=cc[:, :], op0=ALU.add, op1=ALU.mult).then_inc(acc_taken[n], 1)
                        taken(dve, n, "mix", i, 2 + 2 * n)
                        chain.link(nc.vector.tensor_scalar(cy[:, :], cu[:, :],
                                                           par_conv[:, i, 3 * n + 2:3 * n + 3], None,
                                                           ALU.mult))
                        for back, w in ((1, 1), (2, 0)):
                            chain.link(nc.vector.scalar_tensor_tensor(
                                out=cy[:, back:T], in0=cu[:, 0:T - back],
                                scalar=par_conv[:, i, 3 * n + w:3 * n + w + 1], in1=cy[:, back:T],
                                op0=ALU.mult, op1=ALU.add))
                    if j == 17 or j == 23:
                        n = (j - 17) // 6
                        unit_is_done("mix", i, j)
                        dve.wait_ge(yclo_ready, FREE + 2 * i + n)
                        nc.vector.scalar_tensor_tensor(
                            out=cz[:, :], in0=acc[1 - n][:, 0:T],
                            scalar=par_mix[:, i, 6 + 3 * n:7 + 3 * n],
                            in1=cy[:, :], op0=ALU.add, op1=ALU.mult).then_inc(acc_taken[1 - n], 1)
                    if j == 17:
                        dve.wait_ge(hstd_ready, i + 1)
                        chain.link(nc.vector.reciprocal(h_rstd[:, :], h_std[:, :]))
                        dve.wait_ge(hmlo_ready, FREE + i)
                        taken(dve, 0, "mix", i, 1)
                        for v in range(2):
                            nc.vector.scalar_tensor_tensor(
                                out=h_norm[:, v, :], in0=h[:, v, :], scalar=par_head[:, i, v:v + 1],
                                in1=h_rstd[:, :], op0=ALU.mult, op1=ALU.mult).then_inc(h_normed, 1)
                        for v in range(2):
                            dve.wait_ge(h_normed, 2 * i + v + 1)
                            nc.vector.tensor_tensor(hm[:, v, :], h_norm[:, v, :], sig_o[:, v, :],
                                                    ALU.mult).then_inc(hm_ready, 1)
                    split("mix", i, j)
                chain.done(M_HEADS)
            with dve.Fori(0, KT // 2) as i:
                for j in range(12):
                    m, jj = divmod(j, 6)
                    if jj in (4, 5):
                        n = jj - 4
                        unit_is_done("merge", i, j)
                        taken(dve, 1 - n, "merge", i, 2 * m)
                        dve.wait_ge(merged_ready, FREE + 2 * i + m)
                        nc.vector.tensor_tensor((part_m, part_c)[n][:, :], acc[1 - n][:, 0:T],
                                                (sig_m, sig_c)[n][:, :], ALU.mult)\
                            .then_inc(acc_taken[1 - n], 1)
                    split("merge", i, j)

            def residual(name, per):
                with dve.Fori(0, KT // 2) as i:
                    for j in range(per):
                        if j in (per // 2 - 1, per - 1):
                            m = 2 * j // per
                            unit_is_done(name, i, j)
                            nc.vector.tensor_tensor(x[:, 2 * i + m, :], acc[1 - m][:, 0:T],
                                                    x[:, 2 * i + m, :], ALU.add)\
                                .then_inc(acc_taken[1 - m], 1)
                        split(name, i, j)

            residual("wout", 4)
            norm_rstd("ffn")
            norm_tiles("ffn", fours(pcols("g_ffn")), rstd)
            def up(i):
                for j in range(4):
                    if j in (1, 3):
                        n = j // 2
                        u = (f_gate, f_val)[n]
                        taken(dve, 1 - n, "wup", i, 0)
                        src = f_pre[:, n, :]
                        chain.link(nc.vector.scalar_tensor_tensor(
                            out=u[:, 1:T], in0=src[:, 0:T - 1],
                            scalar=par_ffn[:, i, 4 * n + 1:4 * n + 2], in1=u[:, 1:T],
                            op0=ALU.mult, op1=ALU.add))
                        nc.vector.scalar_tensor_tensor(
                            out=u[:, 2:T], in0=src[:, 0:T - 2],
                            scalar=par_ffn[:, i, 4 * n:4 * n + 1], in1=u[:, 2:T],
                            op0=ALU.mult, op1=ALU.add).then_inc(ftap_ready, 1)
                    if j == 3:
                        dve.wait_ge(fsilu_ready, FREE + i + 1)
                        dve.wait_ge(ftap_ready, 2 * i + 2)
                        dve.wait_ge(flo_ready, FREE + i)
                        nc.vector.tensor_tensor(f_act[:, :], f_silu[:, :], f_val[:, :], ALU.mult)\
                            .then_inc(fact_ready, 1)
                    split("wup", i, j)

            with dve.Fori(0, F_TILES // 2) as pair:
                chain.loop(pair, 4)
                up(2 * pair)
                up(2 * pair + 1)
                chain.done(F_TILES // 2)
            up(F_TILES - 1)
            residual("wdown", 12)
            norm_rstd("out")
            chain.link(nc.vector.tensor_tensor(mean_part[:, :], att[3][:, T:2 * T], rstd[:, :], ALU.mult))
            nc.vector.tensor_tensor(mean_g[:, :], mean_part[:, :], rstd[:, :], ALU.mult)\
                .then_inc(mean_ready, 1)
            dve.wait_ge(std_ready, NORM["pre0"] + 1)
            chain.link(nc.vector.reciprocal(mean_part[:, :], std[:, :]))
            nc.vector.tensor_tensor(rstd_both[:, :], mean_part[:, :], rstd[:, :], ALU.mult)\
                .then_inc(rstd_ready, 1)
            dve.wait_ge(rstd_ready, NORM["pre0"] + 1)
            dve.wait_ge(gains_ready, 1)
            norm_tiles("pre0", fours(g_both[:, :]), rstd_both)
            with dve.Fori(0, KT // 4) as g:
                for m in range(4):
                    nc.vector.scalar_tensor_tensor(
                        out=x[:, 4 * g + m, :], in0=x[:, 4 * g + m, :], scalar=fours(pcols("g_out"))[:, g, m:m + 1],
                        in1=rstd[:, :], op0=ALU.mult, op1=ALU.mult).then_inc(x_normed, 1)
            split("rank", None, 0)
            split("rank", None, 1)
            dve.wait_ge(restart_ready, 1)
            for hd in range(G_HEADS):
                dve.wait_ge(glog_ready, hd + 1)
                nc.vector.scalar_tensor_tensor(out=log_a[:, hd, :], in0=att[hd][:, :], scalar=0.0,
                                               in1=g_log[:, hd, :], op0=ALU.min, op1=ALU.subtract)\
                    .then_inc(gk_taken, 1)
                dve.wait_ge(gk_taken, hd + 1)
                nc.vector.tensor_tensor_scan(gcum[:, hd, :, :].rearrange("p a t -> p (a t)"),
                                             restart[:, :, :].rearrange("p a t -> p (a t)"),
                                             log_a[:, hd, :], 0.0, ALU.mult, ALU.add).then_inc(gcum_ready, 1)
            dve.wait_ge(gcum_ready, G_HEADS)
            dve.wait_ge(at_init, 2)
            with dve.Fori(0, G_HEADS) as i:
                chain.loop(i, 7)
                for j in range(24):
                    if j == 0:
                        dve.wait_ge(decays_ready, FREE + 3 * i)
                        b = gcum[:, i, :, :].rearrange("p a (c t) -> p (a c) t", t=CHUNK)
                        nc.vector.tensor_tensor(
                            to_end[:, :, :].rearrange("p a (c t) -> p (a c) t", t=CHUNK),
                            b[:, :, CHUNK - 1:CHUNK].to_broadcast([P, 2 * T // CHUNK, CHUNK]), b,
                            ALU.subtract).then_inc(to_end_ready, 1)
                    if j in (1, 3):
                        n = j // 2
                        unit_is_done("gla", i, j)
                        dve.wait_ge(decays_ready, FREE + 3 * i + 1)
                        nc.vector.scalar_tensor_tensor(out=q_e[:, n, :], in0=acc[n][:, 0:T],
                                                       scalar=G_DK ** -0.5, in1=e_pos[:, n, :],
                                                       op0=ALU.mult, op1=ALU.mult)\
                            .then_inc(acc_taken[n], 1)
                    if j == 3:
                        taken(dve, 0, "gla", i, 0)
                        taken(dve, 1, "gla", i, 0)
                        over1, over2 = 2 * CHUNK - 1, 3 * CHUNK - 1
                        for n in range(2):
                            chain.step(nc.vector.tensor_scalar(
                                q_y[:, n, :], q_e[:, n, 3 * CHUNK:T], e_pos[:, n, over2:over2 + 1],
                                None, ALU.mult))
                        chain.wait()
                        for n in range(2):
                            nc.vector.tensor_scalar(
                                q_x[:, n, 0:CHUNK], q_e[:, n, 2 * CHUNK:3 * CHUNK],
                                e_pos[:, n, over1:over1 + 1], None, ALU.mult).then_inc(qx_ready, 1)
                            nc.vector.tensor_scalar(
                                q_x[:, n, CHUNK:2 * CHUNK], q_y[:, n, :],
                                e_pos[:, n, over1:over1 + 1], None, ALU.mult).then_inc(qx_ready, 1)
                    if j == 15:
                        unit_is_done("gla", i, j)
                        for t in range(2):
                            nc.vector.tensor_copy(vg[:, t, :], tok[t][:, :]).then_inc(tok_taken, 1)
                    if j == 16:
                        dve.wait_ge(gscores_ready, i + 1)
                        nc.vector.tensor_copy(a_t[:, 0, P:T], att[0][:, P:T]).then_inc(at_ready, 1)
                        for s in range(2):
                            for p, lo, hi in ((CHUNK, 0, CHUNK), (P, CHUNK, P)):
                                at = s * P
                                nc.vector.copy_predicated(
                                    a_t[0:p, s, at + lo:at + hi], kept[0:p, lo:hi].bitcast(i32),
                                    att[0][0:p, s * T + at + lo:s * T + at + hi]).then_inc(at_ready, 1)
                    if j == 23:
                        dve.wait_ge(ostd_ready, i + 1)
                        chain.link(nc.vector.reciprocal(o_rstd[:, :], o_std[:, :]))
                        dve.wait_ge(oglo_ready, FREE + i)
                        dve.wait_ge(osb_ready, 2 * i + 2)
                        for v in range(4):
                            chain.step(nc.vector.scalar_tensor_tensor(
                                out=o_norm[:, v, :], in0=o_sb[:, v, :], scalar=pcols("g_gla")[:, v:v + 1],
                                in1=o_rstd[:, :], op0=ALU.mult, op1=ALU.mult))
                        chain.wait()
                        taken(dve, 0, "gla", i, 3)
                        taken(dve, 1, "gla", i, 3)
                        nc.vector.tensor_tensor(o_norm[:, :, :], o_norm[:, :, :], o_sg[:, :, :],
                                                ALU.mult).then_inc(og_ready, 1)
                    split("gla", i, j)
                chain.done(G_HEADS)

            def add_normed(n, gain, source, k):
                norm_rstd(n)
                half = k * KT // 2
                with dve.Fori(0, KT // 4) as g:
                    for m in range(4):
                        dve.wait_ge((x_added_pool, x_added)[m // 2], FREE + 2 * g + max(half + m % 2 - 1, 0))
                        nc.vector.scalar_tensor_tensor(
                            out=normed[:, m, :], in0=source[:, 4 * g + m, :],
                            scalar=fours(pcols(gain))[:, g, m:m + 1],
                            in1=rstd[:, :], op0=ALU.mult, op1=ALU.mult).then_inc(scaled_ready, 1)
                    for m in (2, 3):
                        dve.wait_ge(scaled_ready, 4 * g + (k * KT + m + 1))
                        nc.vector.tensor_tensor(x[:, 4 * g + m, :], x[:, 4 * g + m, :], normed[:, m, :],
                                                ALU.add).then_inc(x_added, 1)

            with dve.Fori(0, KT // 2) as i:
                for j in range(4):
                    split("glaout", i, j)
            dve.wait_ge(x_normed, KT)
            add_normed("post0", "g_post0", y, 0)
            norm_rstd("pre1")
            norm_tiles("pre1", fours(pcols("g_pre1")), rstd)
            def latent_normed(n):
                dve.wait_ge(lstd_ready, n + 1)
                chain.link(nc.vector.reciprocal(l_rstd[:, n, :], l_std[:, n, :]))
                for k in range(A_TILES * n, A_TILES * (n + 1)):
                    if k < 4:
                        dve.wait_ge(act_ready, 3 * KT)
                        dve.wait_ge(act_ready_dve, KT)
                    else:
                        dve.wait_ge(c_ready, k - 3)
                    nc.vector.scalar_tensor_tensor(
                        out=normed[:, k % 4, :], in0=latent[:, k, :],
                        scalar=pcols("g_latent")[:, k:k + 1], in1=l_rstd[:, n, :],
                        op0=ALU.mult, op1=ALU.mult).then_inc(cnormed_ready, 1)

            for j in range(16):
                split("latent", None, j)
                if j == 2 * A_TILES + 1:
                    latent_normed(0)
            for j in range(4):
                split("krope", None, j)
                if j == 1:
                    latent_normed(1)
            taken(dve, 0, "krope", None, 0)
            taken(dve, 1, "krope", None, 0)
            dve.wait_ge(rope_ready, 2)
            dve.wait_ge(krm_zero, 1)
            for n, (part, angle) in enumerate(((0, cosine), (1, sine), (1, cosine), (0, sine))):
                chain.step(nc.vector.tensor_tensor(rope_t[:, n, :], kr[:, part, :], angle[:, :], ALU.mult))
            chain.wait()
            for n in range(4):
                rows = slice(HALF * n, HALF * (n + 1))
                nc.vector.tensor_tensor(kr_m[rows, 0, n, :], rope_t[rows, 0, :], rope_t[rows, 1, :],
                                        ALU.subtract).then_inc(krm_ready, 1)
                nc.vector.tensor_tensor(kr_m[rows, 1, n, :], rope_t[rows, 2, :], rope_t[rows, 3, :],
                                        ALU.add).then_inc(krm_ready, 1)
            dve.wait_ge(krm_ready, 8)
            dve.wait_ge(causal_ready, 3)
            with dve.Fori(0, A_HEADS // 4) as i:
                chain.loop(i, 2 + 4 * 2)
                for j in range(16):
                    if j in (1, 3):
                        n = j // 2
                        unit_is_done("mla", i, j)
                        nc.vector.tensor_copy(kn[:, 2 * n:2 * n + 2, :], acc[1][:, :])\
                            .then_inc(acc_taken[1], 1)
                    if j == 5:
                        taken(dve, 0, "mla", i, 2)
                        chain.step(nc.vector.tensor_tensor(rope_t[:, 0, :], q_r[:, 0, :], cosine[:, :],
                                                           ALU.mult))
                        chain.step(nc.vector.tensor_tensor(rope_t[:, 1, :], q_r[:, 1, :], sine[:, :],
                                                           ALU.mult))
                        chain.wait()
                        nc.vector.tensor_tensor(q_rope[:, 0, :], rope_t[:, 0, :], rope_t[:, 1, :],
                                                ALU.subtract).then_inc(qrope_ready, 1)
                    if j == 7:
                        unit_is_done("mla", i, j)
                        for t in range(2):
                            nc.vector.tensor_copy(va[:, t, :], tok[t][:, :]).then_inc(tok_taken, 1)
                    if j in (8, 12):
                        first = (j - 8) // 2
                        for n in (first, first + 1):
                            dve.wait_ge(logits_ready, 4 * i + n + 1)
                            dve.wait_ge(exp_ready, FREE + 8 * i + max(2 * (n - 1), 0))
                            chain.link(nc.vector.scalar_tensor_tensor(
                                out=logits[:, n % 2, :], in0=att[n % 2][:, 0:3 * P],
                                scalar=(A_NOPE + A_ROPE) ** -0.5, in1=causal[:, :],
                                op0=ALU.mult, op1=ALU.add))
                            nc.vector.reduce_max(row_max[:, n % 2, 0:1], logits[:, n % 2, 0:P], AX)
                            chain.link(nc.vector.reduce_max(row_max[:, n % 2, 1:2],
                                                            logits[:, n % 2, P:3 * P], AX))
                            nc.vector.tensor_scalar(neg_max[:, n % 2, :], row_max[:, n % 2, :], -1.0,
                                                    None, ALU.mult).then_inc(neg_ready, 1)
                        for n in (first, first + 1):
                            dve.wait_ge(exp_ready, FREE + 8 * i + 2 * n + 2)
                            nc.vector.reciprocal(row_inv[:, n % 2, :], row_sum[:, n % 2, :])\
                                .then_inc(inv_ready, 1)
                    if j in (12, 15):
                        for n in range(2 * (j // 15), 2 * (j // 15) + 2):
                            dve.wait_ge(apv_ready, 4 * i + n + 1)
                            taken(dve, 1 - n % 2, "mla", i, (2, 3, 3, 4)[n])
                            dve.wait_ge(molo_ready, FREE + 4 * i)
                            nc.vector.tensor_tensor(a_out[:, n, :], att[2 + n % 2][:, 0:T],
                                                    a_gate[:, n, :], ALU.mult).then_inc(aout_ready, 1)
                    split("mla", i, j)
                chain.done(A_HEADS // 4)
            with dve.Fori(0, KT // 2 - 1) as i:
                for j in range(4):
                    split("mlaout", i, j)
            add_normed("post1", "g_post1", y2, 1)

        @block.gpsimd
        def _(pool):
            chain = Chain(pool, pool_step)
            gp = nc.gpsimd

            def add_squares(n, with_gain=False):
                k = POOLED[n]
                pool.wait_ge(stat_ready, STAT[n])
                if with_gain:
                    chain.link(gp.memset(sumsq_g[:, :], 0.0))
                chain.link(gp.memset(sumsq[:, :], 0.0))
                with pool.Fori(0, KT // 2) as i:
                    for m in range(2):
                        pool.wait_ge(sq_ready, 2 * i + (k * KT + m + 1))
                        pool.wait_ge(sq_added, FREE + 2 * i + (k * KT + m))
                        ins = gp.tensor_tensor(sumsq[:, :], sumsq[:, :], square[:, m, :], ALU.add)
                        if with_gain:
                            ins = gp.tensor_tensor(sumsq_g[:, :], sumsq_g[:, :], square_g[:, m, :], ALU.add)
                        ins.then_inc(sq_added, 1)

            def norm_low(n):
                at = TO_ACT[n] * KT
                with pool.Fori(0, KT // 4) as g:
                    for m in (1, 2, 3):
                        pool.wait_ge(nhi_ready, 4 * g + (at + m + 1))
                        gp.tensor_tensor(n_lo[:, 4 * g + m, :], normed[:, m, :],
                                         n_hi[:, 4 * g + m, :].bitcast(fp32), ALU.subtract)\
                            .then_inc(act_ready, 1)

            def add_scaled(k):
                with pool.Fori(0, KT // 4) as g:
                    for m in range(2):
                        pool.wait_ge(scaled_ready, 4 * g + (k * KT + m + 1))
                        gp.tensor_tensor(x[:, 4 * g + m, :], x[:, 4 * g + m, :], normed[:, m, :], ALU.add)\
                            .then_inc(x_added_pool, 1)

            for signal in free_from_start:
                pool.sem_inc(signal, FREE)
            gp.memset(eps_col[:, :], EPS).then_inc(const_ready, 1)
            chain.step(gp.memset(ident[:, :], 0.0))
            chain.step(gp.memset(head_row[:, :, :], 0.0))
            gp.memset(ones[:, :], 1.0).then_inc(const_ready, 1)
            chain.wait()
            gp.affine_select(out=ident[:, :], in_=ident[:, :], compare_op=ALU.not_equal, fill=1.0, base=0,
                             pattern=[[-1, P]], channel_multiplier=1).then_inc(const_ready, 1)
            gp.affine_select(out=head_row[:, :, :], in_=head_row[:, :, :], compare_op=ALU.not_equal, fill=1.0,
                             base=0, pattern=[[-1, M_HEADS], [0, P]], channel_multiplier=1)\
                .then_inc(const_ready, 1)
            norm_low("mix")
            pool.wait_ge(a_col_ready, 2 * M_HEADS)
            for d in (decay0[:, :, 0:P], decay1[:, :, :]):
                gp.affine_select(out=d, in_=d, compare_op=ALU.is_ge, fill=0.0, base=0,
                                 pattern=[[0, M_HEADS], [1, P]], channel_multiplier=-1)\
                    .then_inc(decay_masked, 1)
            with pool.Fori(0, M_HEADS) as i:
                pool.wait_ge(hsq_ready, i + 1)
                gp.tensor_tensor(h_sum[:, :], h_sq[:, 0, :], h_sq[:, 1, :], ALU.add).then_inc(hsum_ready, 1)
                pool.wait_ge(hmhi_ready, i + 1)
                gp.tensor_tensor(hm_lo[:, bass.ds(2 * i, 2), :], hm[:, :, :],
                                 hm_hi[:, bass.ds(2 * i, 2), :].bitcast(fp32), ALU.subtract)\
                    .then_inc(hmlo_ready, 1)
                for n in range(2):
                    pool.wait_ge(ychi_ready, 2 * i + n + 1)
                    gp.tensor_tensor(yc_lo[:, 2 * i + n, :], cz[:, :],
                                     yc_hi[:, 2 * i + n, :].bitcast(fp32), ALU.subtract)\
                        .then_inc(yclo_ready, 1)
            with pool.Fori(0, KT // 2) as i:
                for m in range(2):
                    taken(pool, 1, "merge", i, 2 * m + 1)
                    taken(pool, 0, "merge", i, 2 * m + 1)
                    pool.wait_ge(mglo_ready, FREE + 2 * i + m)
                    gp.tensor_tensor(merged[:, :], part_m[:, :], part_c[:, :], ALU.add)\
                        .then_inc(merged_ready, 1)
                    pool.wait_ge(mghi_ready, 2 * i + m + 1)
                    gp.tensor_tensor(mg_lo[:, 2 * i + m, :], merged[:, :],
                                     mg_hi[:, 2 * i + m, :].bitcast(fp32), ALU.subtract)\
                        .then_inc(mglo_ready, 1)
            add_squares("ffn")
            norm_low("ffn")
            with pool.Fori(0, F_TILES) as i:
                pool.wait_ge(fhi_ready, i + 1)
                gp.tensor_tensor(f_lo[:, i, :], f_act[:, :], f_hi[:, i, :].bitcast(fp32), ALU.subtract)\
                    .then_inc(flo_ready, 1)
            add_squares("out", with_gain=True)
            norm_low("pre0")
            gp.memset(rank_rows[:, :], 1.0).then_inc(rank_ones, 1)
            chain.step(gp.memset(restart[:, :, :], 1.0))
            chain.step(gp.memset(kept[:, :], 1.0))
            gp.memset(a_t[:, :, :], 0.0).then_inc(at_init, 1)
            chain.wait()
            gp.affine_select(out=kept[:, :], in_=kept[:, :], compare_op=ALU.is_ge, fill=0.0, base=0,
                             pattern=[[1, P]], channel_multiplier=-1).then_inc(at_init, 1)
            gp.memset(restart[:, :, :].rearrange("p a (c t) -> p (a c) t", t=CHUNK)[:, :, 0:1], 0.0)\
                .then_inc(restart_ready, 1)
            with pool.Fori(0, G_HEADS) as i:
                taken(pool, 0, "gla", i, 1)
                taken(pool, 1, "gla", i, 1)
                pool.wait_ge(decays_ready, FREE + 3 * i + 3)
                gp.tensor_tensor(k_e[:, :, :], k_sb[:, :, :], e_neg[:, :, :], ALU.mult).then_inc(kk_ready, 1)
                gp.tensor_tensor(k_l[:, :, :], k_sb[:, :, :], e_end[:, :, :], ALU.mult).then_inc(kk_ready, 1)
                pool.wait_ge(osq_ready, 2 * i + 2)
                chain.loop(i, 1)
                chain.link(gp.tensor_tensor(o_sum2[:, :, :], o_sq[:, 0:2, :], o_sq[:, 2:4, :], ALU.add))
                gp.tensor_tensor(o_sum[:, :], o_sum2[:, 0, :], o_sum2[:, 1, :], ALU.add)\
                    .then_inc(osum_ready, 1)
                pool.wait_ge(oghi_ready, i + 1)
                gp.tensor_tensor(og_lo[:, bass.ds(4 * i, 4), :], o_norm[:, :, :],
                                 og_hi[:, bass.ds(4 * i, 4), :].bitcast(fp32), ALU.subtract)\
                    .then_inc(oglo_ready, 1)
                chain.done(G_HEADS)
            add_squares("post0")
            pool.wait_ge(x_normed, KT)
            add_scaled(0)
            norm_low("pre1")
            def latent_low(n):
                for k in range(A_TILES * n, A_TILES * (n + 1)):
                    pool.wait_ge(chi_ready, k + 1)
                    gp.tensor_tensor(c_lo[:, k, :], normed[:, k % 4, :], c_hi[:, k, :].bitcast(fp32),
                                     ALU.subtract).then_inc(c_ready, 1)

            chain.link(gp.memset(l_sumsq[:, :, :], 0.0))
            chain.step(gp.memset(causal[:, :], 0.0))
            gp.memset(kr_m[:, :, :, :], 0.0).then_inc(krm_zero, 1)
            chain.wait()
            for b in (0, 2):
                d = causal[:, b * P:(b + 1) * P]
                gp.affine_select(out=d, in_=d, compare_op=ALU.is_ge, fill=-1e30, base=0,
                                 pattern=[[-1, P]], channel_multiplier=1).then_inc(causal_ready, 1)
            gp.memset(row_max[:, :, :], 0.0).then_inc(causal_ready, 1)
            for k in range(2 * A_TILES):
                taken(pool, k % 2, "latent", None, k // 2)
                if k:
                    pool.wait_ge(lsq_added, k)
                n = k // A_TILES
                gp.tensor_tensor(l_sumsq[:, n, :], l_sumsq[:, n, :], l_square[:, k % 2, :], ALU.add)\
                    .then_inc(lsq_added, 1)
                if k == A_TILES + 1:
                    latent_low(0)
            latent_low(1)
            pool.wait_ge(krm_ready, 8)
            with pool.Fori(0, A_HEADS // 4) as i:
                chain.loop(i, 2 + 4)
                taken(pool, 0, "mla", i, 2)
                chain.step(gp.tensor_tensor(rope_t[:, 2, :], q_r[:, 1, :], cosine[:, :], ALU.mult))
                chain.step(gp.tensor_tensor(rope_t[:, 3, :], q_r[:, 0, :], sine[:, :], ALU.mult))
                chain.wait()
                gp.tensor_tensor(q_rope[:, 1, :], rope_t[:, 2, :], rope_t[:, 3, :], ALU.add)\
                    .then_inc(qrope_ready, 1)
                for n in range(4):
                    pool.wait_ge(inv_ready, 4 * i + n + 1)
                    chain.step(gp.tensor_tensor(
                        probs[:, n % 2, 0:P], probs[:, n % 2, 0:P],
                        row_inv[:, n % 2, 0:1].to_broadcast([P, P]), ALU.mult))
                    gp.tensor_tensor(
                        probs[:, n % 2, P:3 * P], probs[:, n % 2, P:3 * P],
                        row_inv[:, n % 2, 1:2].to_broadcast([P, 2 * P]), ALU.mult)\
                        .then_inc(probs_ready, 1)
                for n in range(4):
                    pool.wait_ge(mohi_ready, 4 * i + n + 1)
                    gp.tensor_tensor(mo_lo[:, 4 * i + n, :], a_out[:, n, :],
                                     mo_hi[:, 4 * i + n, :].bitcast(fp32), ALU.subtract)\
                        .then_inc(molo_ready, 1)
                chain.done(A_HEADS // 4)
            add_squares("post1")
            add_scaled(1)


def kernel(**inputs):
    import concourse.bacc as _bacc
    import numpy as np
    from concourse.bass_utils import run_bass_kernel_spmd as _run

    arrays = lay_out({k: np.asarray(v) for k, v in inputs.items()})
    nc = _bacc.Bacc("TRN2", target_bir_lowering=False, num_devices=1)
    ins = {n: nc.dram_tensor(n, v.shape, mybir.dt.from_np(v.dtype), kind="ExternalInput").ap()
           for n, v in arrays.items()}
    out = nc.dram_tensor("out", (P, KT, T), mybir.dt.float32, kind="ExternalOutput").ap()
    program(nc, out=out, **ins)
    got = _run(nc, [arrays], core_ids=[0]).results[0]["out"]
    return np.ascontiguousarray(got.transpose(2, 1, 0).reshape(1, T, D))


def lay_out(a):
    import numpy as np

    splits = (M_HEADS * M_DQK, M_HEADS * M_DQK, M_HEADS * M_DV, M_HEADS * M_DV, M_HEADS, M_HEADS,
              C_TILES * P, C_TILES * P, C_TILES * P, D, D)
    offs = [sum(splits[:n]) for n in range(len(splits))]
    cols = {n: slice(o, o + w) for n, o, w in zip("q k v o i f cb cc ch gm gc".split(), offs, splits)}
    w_in = {n: a["w_in"][:, s] for n, s in cols.items()}
    b_in = {n: a["b_in"][s] for n, s in cols.items()}

    chunks = np.zeros((N_CHUNKS, P, 2 * UNIT), np.float32)
    at = [0, 0]

    def put(w, width=P):
        k, n = w.shape
        for c in range(0, n, width):
            for r in range(0, k, P):
                block = w[r:r + P, c:c + width]
                chunks[at[0], 0:block.shape[0], at[1]:at[1] + block.shape[1]] = block
                at[1] += width
                if at[1] == 2 * UNIT:
                    at[0], at[1] = at[0] + 1, 0

    def end():
        if at[1]:
            at[0], at[1] = at[0] + 1, 0

    def tile_of(w, m):
        return w[:, m * P:(m + 1) * P]

    gates = np.zeros((D, P), np.float32)
    gates[:, 0:M_HEADS] = w_in["i"]
    gates[:, 32:32 + M_HEADS] = w_in["f"]
    put(gates)
    for h in range(M_HEADS):
        put(tile_of(w_in["q"], h))
        put(tile_of(w_in["k"], h))
        put(w_in["v"][:, h * M_DV:(h + 1) * M_DV], M_DV)
        for n in range(2):
            put(tile_of(w_in["o"], 2 * h + n))
        for n in range(2):
            for part in ("cc", "ch", "cb"):
                put(tile_of(w_in[part], 2 * h + n))
    for m in range(KT):
        put(tile_of(w_in["gm"], m))
        put(tile_of(w_in["gc"], m))
        put(tile_of(a["w_branch_m"], m))
        put(tile_of(a["w_branch_c"], m))
    put(a["w_out"])
    for f in range(F_TILES):
        put(tile_of(a["w_up"], f))
        put(tile_of(a["w_up"], F_TILES + f))
    for m in range(KT):
        put(tile_of(a["w_down"], m))
        end()
    gla = a["l0_gla_w_in_2"]
    qk, vv = G_HEADS * G_DK, G_HEADS * G_DV
    ranks = np.zeros((D, P), np.float32)
    ranks[:, 0:G_RANK] = gla[:, 2 * qk + 2 * vv:]
    put(ranks)
    for h in range(G_HEADS):
        put(gla[:, h * G_DK:(h + 1) * G_DK])
        put(gla[:, qk + h * G_DK:qk + (h + 1) * G_DK])
        put(gla[:, 2 * qk + h * G_DV:2 * qk + (h + 1) * G_DV], G_DV)
        put(gla[:, 2 * qk + vv + h * G_DV:2 * qk + vv + (h + 1) * G_DV])
    put(a["l0_gla_w_out_2"])
    mla = a["l1_mla_w_in_2"]
    put(mla[:, 0:2 * A_RANK])
    k_rope = mla[:, 2 * A_RANK:2 * A_RANK + A_ROPE]
    for half in range(2):
        put(np.concatenate([k_rope[:, half * HALF:(half + 1) * HALF]] * 4, axis=1))
    w_q = a["l1_mla_w_qb_2"].reshape(A_RANK, A_HEADS, A_NOPE + A_ROPE)
    w_kv = a["l1_mla_w_kvb_2"].reshape(A_RANK, A_HEADS, A_NOPE + A_V)
    for g in range(0, A_HEADS, 4):
        for n in (0, 2):
            for w in (w_q, w_kv):
                put(w[:, g + n, 0:A_NOPE])
                put(w[:, g + n + 1, 0:A_NOPE])
        for half in range(2):
            r = A_NOPE + half * HALF
            put(np.ascontiguousarray(w_q[:, g:g + 4, r:r + HALF]).reshape(A_RANK, 4 * HALF))
        end()
        put(np.ascontiguousarray(w_kv[:, g:g + 4, A_NOPE:]).reshape(A_RANK, 4 * A_V), 4 * A_V)
        for n in range(4):
            put(tile_of(mla[:, 2 * A_RANK + A_ROPE:], g + n))
    put(a["l1_mla_w_out_2"])
    assert at == [N_CHUNKS, 0], at

    def col(v):
        return v.reshape(-1, P).T

    b_gate = np.zeros((P, 1), np.float32)
    b_gate[0:M_HEADS, 0] = b_in["i"]
    b_gate[32:32 + M_HEADS, 0] = b_in["f"]
    b_mix = []
    for h in range(M_HEADS):
        b_mix += [col(b_in["q"])[:, h], col(b_in["k"])[:, h]]
        b_mix += [col(b_in["o"])[:, 2 * h + n] for n in range(2)]
        b_mix += [col(b_in[part])[:, 2 * h + n] for n in range(2) for part in ("cc", "ch", "cb")]
    b_merge = [col(b_in[part])[:, m] for m in range(KT) for part in ("gm", "gc")]
    conv = a["conv_w"].reshape(3, C_TILES, P).transpose(2, 1, 0).reshape(P, -1)
    ffn = np.concatenate([a["ffn_conv_w"], a["ffn_conv_b"][None]]).reshape(4, 2, F_TILES, P)
    ffn = ffn.transpose(3, 2, 1, 0).reshape(P, -1)
    freq = np.float32(10000.0) ** (-np.arange(0, A_ROPE, 2, dtype=np.float32) / np.float32(A_ROPE))
    params = {
        "g_mix": col(a["norm_mix_g"]), "g_ffn": col(a["norm_ffn_g"]), "g_out": col(a["norm_out_g"]),
        "g_pre0": col(a["l0_pre_norm_2"]), "g_post0": col(a["l0_post_norm_2"]),
        "g_pre1": col(a["l1_pre_norm_2"]), "g_post1": col(a["l1_post_norm_2"]),
        "b_gate": b_gate, "b_mix": np.stack(b_mix, 1), "b_merge": np.stack(b_merge, 1),
        "g_head": col(a["mlstm_head_g"]), "w_conv": conv, "w_ffn": ffn, "g_gla": col(a["l0_gla_g_onorm_2"]),
        "g_latent": np.concatenate([col(a["l1_mla_g_qa_2"]), col(a["l1_mla_g_kva_2"])], 1),
        "inv_freq": np.tile(freq.astype(np.float32), 4)[:, None],
    }
    for n, k in PARAMS:
        assert params[n].shape == (P, k), (n, params[n].shape)
    return {
        "x_in": np.ascontiguousarray(a["x"][0].T.reshape(KT, P, T).transpose(1, 0, 2)),
        "stream_in": chunks,
        "params_in": np.concatenate([params[n] for n, _ in PARAMS], 1),
        "v_bias_in": np.ascontiguousarray(b_in["v"])[None],
        "gk2_in": np.concatenate([a["l0_gla_w_gk2_2"], a["l0_gla_b_gk_2"][None]]),
        "positions_in": np.ascontiguousarray(a["positions_2"]),
    }
```

```python
from contextlib import ExitStack

import concourse.bass as bass
from concourse import mybir

P = 128
T = 256
D = 2048
KT = D // P
CHUNK = 64
PI = 3.14159265358979
PI_INSIDE = 3.1415925
EPS = 1e-6
M_HEADS, M_DV, M_DQK = 4, 256, 128
C_TILES = 1024 // P
D_FF = 5504
F_TILES = D_FF // P
G_HEADS, G_DK, G_DV, G_RANK, G_TAU = 4, 256, 512, 16, 16.0
A_HEADS, A_RANK, A_NOPE, A_ROPE, A_V = 16, 512, 128, 64, 128
A_TILES = A_RANK // P
HALF = A_ROPE // 2
UNIT = 1024
RING = 4
FREE = 1

PHASES = [
    ("gates", 1, 2, 1, 0, 0),
    ("mix", M_HEADS, 24, 5, 5, 1),
    ("merge", KT // 2, 12, 4, 4, 0),
    ("wout", KT // 2, 4, 1, 1, 0),
    ("wup", F_TILES, 4, 1, 1, 0),
    ("wdown", KT // 2, 12, 1, 1, 0),
    ("rank", 1, 2, 0, 1, 0),
    ("gla", G_HEADS, 24, 4, 4, 1),
    ("glaout", KT // 2, 4, 1, 1, 0),
    ("latent", 1, 16, 4, 4, 0),
    ("krope", 1, 4, 1, 1, 0),
    ("mla", A_HEADS // 4, 16, 5, 4, 1),
    ("mlaout", KT // 2, 4, 1, 1, 0),
]
N_CHUNKS = sum(n * units for _, n, units, *_ in PHASES) // 2

PARAMS = [
    ("g_mix", KT), ("g_ffn", KT), ("g_out", KT), ("g_pre0", KT), ("g_post0", KT), ("g_pre1", KT),
    ("g_post1", KT), ("b_gate", 1), ("b_mix", M_HEADS * 10), ("b_merge", 2 * KT), ("g_head", 8),
    ("w_conv", 3 * C_TILES), ("w_ffn", 8 * F_TILES), ("g_gla", G_DV // P), ("g_latent", 8),
    ("inv_freq", 1),
]
N_PARAMS = sum(n for _, n in PARAMS)


def program(nc, x_in, stream_in, params_in, v_bias_in, gk2_in, positions_in, out):
    fp32, fp32r, i32 = mybir.dt.float32, mybir.dt.float32r, mybir.dt.int32
    ALU = mybir.AluOpType
    ACT = mybir.ActivationFunctionType
    AX = mybir.AxisListType.X

    base, total = {}, [0, 0, 0, 0]
    for name, n, *per in PHASES:
        base[name] = (list(total), per)
        total = [t + n * k for t, k in zip(total, per)]

    def count(which, name, i, j):
        start, per = base[name]
        k = start[which] + j
        return k if i is None else i * per[which] + k

    def unit_of(name, i, j):
        start, per = base[name]
        k = start[0] + j
        if i is None:
            return k, k % RING, k // RING
        assert per[0] % RING == 0
        return i * per[0] + k, k % RING, i * (per[0] // RING) + k // RING

    ctx = ExitStack()
    with ctx:
        def sb(name, shape, dt=fp32):
            return ctx.enter_context(nc.sbuf_tensor(name, shape, dt))

        def sem(name):
            return ctx.enter_context(nc.semaphore(name))

        free_from_start = []

        def used_sem(name):
            free_from_start.append(sem(name))
            return free_from_start[-1]

        x = sb("x", [P, KT, T])
        raw = sb("raw", [P, RING, UNIT])
        w_hi = sb("w_hi", [P, RING, UNIT], fp32r)
        w_lo = sb("w_lo", [P, RING, UNIT], fp32r)
        n_hi = sb("n_hi", [P, KT, T], fp32r)
        n_lo = sb("n_lo", [P, KT, T], fp32r)
        par = sb("par", [P, N_PARAMS])
        normed = sb("normed", [P, 4, T])
        square = sb("square", [P, 2, T])
        sumsq = sb("sumsq", [P, T])
        std = sb("std", [P, T])
        rstd = sb("rstd", [P, T])
        g_both = sb("g_both", [P, KT])
        ones = sb("ones", [P, P])
        ident = sb("ident", [P, P])
        cosine = sb("cosine", [P, T])
        sine = sb("sine", [P, T])
        eps_col = sb("eps_col", [P, 1])
        eps_eps_col = sb("eps_eps_col", [P, 1])

        arena_start = -(-nc.sbuf_base // 64) * 64
        arena_end = nc.sbuf_usable_end

        class Arena:
            def __init__(self, at):
                self.at = at

            def place(self, name, shape, dt=fp32):
                n = 4
                for s in shape[1:]:
                    n *= s
                t = nc.alloc_sbuf_tensor_at(name, shape, dt, offset=self.at)
                self.at += -(-n // 32) * 32
                assert self.at <= arena_end, (name, self.at - arena_end)
                return t

        a = Arena(arena_start)
        yc_hi = a.place("yc_hi", [P, C_TILES, T], fp32r)
        yc_lo = a.place("yc_lo", [P, C_TILES, T], fp32r)
        hm_hi = a.place("hm_hi", [P, C_TILES, T], fp32r)
        hm_lo = a.place("hm_lo", [P, C_TILES, T], fp32r)
        sig_m = a.place("sig_m", [P, T])
        sig_c = a.place("sig_c", [P, T])
        part_m = a.place("part_m", [P, T])
        part_c = a.place("part_c", [P, T])
        merged = a.place("merged", [P, T])
        mixer_temps = a.at
        mg_hi = a.place("mg_hi", [P, KT, T], fp32r)
        mg_lo = a.place("mg_lo", [P, KT, T], fp32r)
        a = Arena(mixer_temps)
        decay = a.place("decay", [P, 3, P])
        weighted = a.place("weighted", [P, 3, P])
        floor = a.place("floor", [P, T])
        future = a.place("future", [P, P])
        zeros = a.place("zeros", [P, P])
        v_bias = a.place("v_bias", [P, M_HEADS, M_DV])
        qT = a.place("qT", [P, T])
        kT = a.place("kT", [P, T])
        vm = a.place("vm", [P, 2, M_DV])
        sig_o = a.place("sig_o", [P, 2, T])
        den_abs = a.place("den_abs", [P, T])
        den = a.place("den", [P, T])
        rden = a.place("rden", [P, T])
        h = a.place("h", [P, 2, T])
        h_sq = a.place("h_sq", [P, 2, T])
        h_sum = a.place("h_sum", [P, T])
        h_std = a.place("h_std", [P, T])
        h_rstd = a.place("h_rstd", [P, T])
        h_norm = a.place("h_norm", [P, 2, T])
        hm = a.place("hm", [P, 2, T])
        cc = a.place("cc", [P, T])
        cu = a.place("cu", [P, T])
        cy = a.place("cy", [P, T])
        cz = a.place("cz", [P, T])
        i_row = a.place("i_row", [64, T])
        f_row = a.place("f_row", [64, T])
        f_abs = a.place("f_abs", [64, T])
        f_exp = a.place("f_exp", [64, T])
        f_log = a.place("f_log", [64, T])
        f_min = a.place("f_min", [64, T])
        logf = a.place("logf", [64, T])
        logf0 = a.place("logf0", [M_HEADS, T])
        ones_row = a.place("ones_row", [M_HEADS, T])
        b_row = a.place("b_row", [M_HEADS, T])
        a_row = a.place("a_row", [M_HEADS, T])
        mm_row = a.place("mm_row", [M_HEADS, 2, T])
        a_col = a.place("a_col", [P, 2])
        mm_own = a.place("mm_own", [M_HEADS, M_HEADS, 2 * T])

        squares_all = Arena(arena_start).place("squares_all", [P, KT, T])

        a = Arena(arena_start)
        f_hi = a.place("f_hi", [P, F_TILES, T], fp32r)
        f_lo = a.place("f_lo", [P, F_TILES, T], fp32r)
        f_pre = a.place("f_pre", [P, 2, T])
        f_gate = a.place("f_gate", [P, T])
        f_val = a.place("f_val", [P, T])
        f_silu = a.place("f_silu", [P, T])
        f_act = a.place("f_act", [P, T])
        square_g = a.place("square_g", [P, 2, T])
        sumsq_g = a.place("sumsq_g", [P, T])
        eps_tile = a.place("eps_tile", [P, P])


        a = Arena(arena_start)
        og_hi = a.place("og_hi", [P, KT, T], fp32r)
        og_lo = a.place("og_lo", [P, KT, T], fp32r)
        y_at = a.at
        y = a.place("y", [P, KT, T])
        restart = a.place("restart", [P, 2, T])
        gcum = a.place("gcum", [P, G_HEADS, 2, T])
        g_log = Arena(a.at).place("g_log", [P, G_HEADS, 2 * T])
        to_end = a.place("to_end", [P, 2, T])
        e_pos = a.place("e_pos", [P, 2, T])
        e_neg = a.place("e_neg", [P, 2, T])
        e_end = a.place("e_end", [P, 2, T])
        q_e = a.place("q_e", [P, 2, T])
        q_x = a.place("q_x", [P, 2, 2 * CHUNK])
        q_y = a.place("q_y", [P, 2, CHUNK])
        k_sb = a.place("k_sb", [P, 2, T])
        k_e = a.place("k_e", [P, 2, T])
        k_l = a.place("k_l", [P, 2, T])
        a_t = a.place("a_t", [P, 2, T])
        kept = a.place("kept", [P, P])
        q_sb = a.place("q_sb", [P, 2, T])
        vg = a.place("vg", [P, 2, G_DV])
        o_sb = a.place("o_sb", [P, 4, T])
        o_sq = a.place("o_sq", [P, 4, T])
        a = Arena(y_at)
        log_a = a.place("log_a", [P, G_HEADS, 2 * T])
        rank_rows = a.place("rank_rows", [32, T])
        a = Arena((arena_end - 4 * T) // 32 * 32)
        out_rstd = a.place("out_rstd", [P, T])
        a = Arena(y_at + 4 * G_HEADS * 2 * T + 4 * T)
        gk2 = a.place("gk2", [G_RANK + 1, G_HEADS * G_DK])
        a = Arena(y_at)
        o_sg = a.place("o_sg", [P, 4, T])
        o_sum2 = a.place("o_sum2", [P, 2, T])
        o_sum = a.place("o_sum", [P, T])
        o_std = a.place("o_std", [P, T])
        o_rstd = a.place("o_rstd", [P, T])
        o_norm = a.place("o_norm", [P, 4, T])

        a = Arena(arena_start)
        mo_hi = a.place("mo_hi", [P, KT, T], fp32r)
        mo_lo = a.place("mo_lo", [P, KT, T], fp32r)
        y2_at = a.at
        y2 = a.place("y2", [P, KT, T])
        c_hi = a.place("c_hi", [P, 2 * A_TILES, T], fp32r)
        c_lo = a.place("c_lo", [P, 2 * A_TILES, T], fp32r)
        kr_m = a.place("kr_m", [P, 2, T])
        causal = a.place("causal", [P, 3 * P])
        rope_t = a.place("rope_t", [P, 4, T])
        kn = a.place("kn", [P, 4, T])
        qn = a.place("qn", [P, 4, T])
        probs_t = a.place("probs_t", [P, 2, 3 * P])
        kr = Arena(a.at).place("kr", [P, 2, T])
        a_gate = a.place("a_gate", [P, 4, T])
        a_out = a.place("a_out", [P, 4, T])
        row_max = a.place("row_max", [P, 2, 2])
        neg_max = a.place("neg_max", [P, 2, 2])
        row_sum = a.place("row_sum", [P, 2, 2])
        row_inv = a.place("row_inv", [P, 2, 2])
        a = Arena(y2_at)
        latent = a.place("latent", [P, 2 * A_TILES, T])
        l_square = a.place("l_square", [P, 2, T])
        l_sumsq = a.place("l_sumsq", [P, 2, T])
        l_std = a.place("l_std", [P, 2, T])
        l_rstd = a.place("l_rstd", [P, 2, T])
        a = Arena(y2_at)
        q_r = a.place("q_r", [P, 2, T])
        q_rope = a.place("q_rope", [P, 2, T])
        va = a.place("va", [P, 2, 4 * A_V])
        logits = a.place("logits", [P, 2, 3 * P])
        probs = a.place("probs", [P, 2, 3 * P])

        a = Arena(arena_start + 4 * 2 * C_TILES * T)
        pos_i = a.place("pos_i", [P, T], i32)
        ang = a.place("ang", [P, T])
        turns = a.place("turns", [P, T])
        turns_i = a.place("turns_i", [P, T], i32)
        red = a.place("red", [P, 2, T])
        wrap = a.place("wrap", [P, 2, T])

        def pcols(name):
            at = 0
            for n, k in PARAMS:
                if n == name:
                    return par[:, at:at + k]
                at += k

        par_mix = pcols("b_mix").rearrange("p (h c) -> p h c", h=M_HEADS)
        par_conv = pcols("w_conv").rearrange("p (h c) -> p h c", h=M_HEADS)
        par_head = pcols("g_head").rearrange("p (h c) -> p h c", h=M_HEADS)
        par_merge = pcols("b_merge").rearrange("p (m c) -> p m c", c=4)
        par_ffn = pcols("w_ffn").rearrange("p (f c) -> p f c", c=8)

        def gains(name):
            return pcols(name).rearrange("p (i m) -> p i m", m=2)

        def fours(columns):
            return columns.rearrange("p (g m) -> p g m", m=4)

        def pb(name):
            return ctx.enter_context(nc.psum_tensor(name, [P, 512], fp32))

        acc = [pb("acc0"), pb("acc1")]
        tok = [pb("tok0"), pb("tok1")]
        att = [pb(f"att{i}") for i in range(4)]

        loaded = sem("loaded")
        x_loaded = [sem(f"x_loaded{g}") for g in range(KT // 4)]
        gains_ready = sem("gains_ready")
        squares_ready = sem("squares_ready")
        bias_loaded = sem("bias_loaded")
        pos_loaded = sem("pos_loaded")
        gk2_loaded = sem("gk2_loaded")
        raw_ready = [sem("raw_ready0"), sem("raw_ready1")]
        hi_ready = sem("hi_ready")
        lo_ready = sem("lo_ready")
        unit_done = sem("unit_done")
        acc_taken = [used_sem("acc_taken0"), used_sem("acc_taken1")]
        tok_taken = used_sem("tok_taken")
        const_ready = sem("const_ready")
        sq_ready = sem("sq_ready")
        sq_added = used_sem("sq_added")
        stat_ready = sem("stat_ready")
        std_ready = sem("std_ready")
        rstd_ready = sem("rstd_ready")
        normed_ready = sem("normed_ready")
        nhi_ready = sem("nhi_ready")
        act_ready = sem("act_ready")
        act_ready_dve = sem("act_ready_dve")
        scaled_ready = sem("scaled_ready")
        x_normed = sem("x_normed")
        x_added = used_sem("x_added")
        x_added_pool = used_sem("x_added_pool")
        stored = sem("stored")
        dve_step = sem("dve_step")
        act_step = sem("act_step")
        pool_step = sem("pool_step")
        rows_ready = sem("rows_ready")
        row_pre = sem("row_pre")
        row_log = sem("row_log")
        a_col_ready = sem("a_col_ready")
        bcast_ready = sem("bcast_ready")
        mdecay_ready = sem("mdecay_ready")
        scores_ready = sem("scores_ready")
        st_ready = sem("st_ready")
        pv_ready = sem("pv_ready")
        den_ready = sem("den_ready")
        h_ready = used_sem("h_ready")
        hsq_ready = sem("hsq_ready")
        hsum_ready = sem("hsum_ready")
        hstat_ready = sem("hstat_ready")
        hstd_ready = sem("hstd_ready")
        hm_ready = used_sem("hm_ready")
        hmhi_ready = sem("hmhi_ready")
        hmlo_ready = used_sem("hmlo_ready")
        h_normed = sem("h_normed")
        ychi_ready = sem("ychi_ready")
        yclo_ready = used_sem("yclo_ready")
        merged_ready = used_sem("merged_ready")
        mghi_ready = sem("mghi_ready")
        mglo_ready = used_sem("mglo_ready")
        ftap_ready = sem("ftap_ready")
        fsilu_ready = used_sem("fsilu_ready")
        fact_ready = used_sem("fact_ready")
        fhi_ready = sem("fhi_ready")
        flo_ready = used_sem("flo_ready")
        rope_ready = sem("rope_ready")
        rope_red = sem("rope_red")
        gk_ready = sem("gk_ready")
        gk_taken = sem("gk_taken")
        glog_ready = sem("glog_ready")
        gcum_ready = sem("gcum_ready")
        restart_ready = sem("restart_ready")
        rank_ones = sem("rank_ones")
        at_init = sem("at_init")
        qe_ready = used_sem("qe_ready")
        qx_ready = used_sem("qx_ready")
        kk_ready = used_sem("kk_ready")
        decays_ready = used_sem("decays_ready")
        to_end_ready = sem("to_end_ready")
        gscores_ready = sem("gscores_ready")
        at_ready = sem("at_ready")
        gpv_ready = sem("gpv_ready")
        osb_ready = sem("osb_ready")
        osq_ready = sem("osq_ready")
        osum_ready = sem("osum_ready")
        ostat_ready = sem("ostat_ready")
        ostd_ready = sem("ostd_ready")
        og_ready = used_sem("og_ready")
        oghi_ready = sem("oghi_ready")
        oglo_ready = used_sem("oglo_ready")
        oglo_ready_dve = used_sem("oglo_ready_dve")
        lsq_added = sem("lsq_added")
        lstat_ready = sem("lstat_ready")
        lstd_ready = sem("lstd_ready")
        cnormed_ready = sem("cnormed_ready")
        chi_ready = sem("chi_ready")
        c_ready = sem("c_ready")
        krm_zero = sem("krm_zero")
        krm_ready = sem("krm_ready")
        causal_ready = sem("causal_ready")
        qrope_ready = used_sem("qrope_ready")
        qprod_ready = sem("qprod_ready")
        logits_ready = sem("logits_ready")
        neg_ready = sem("neg_ready")
        exp_ready = used_sem("exp_ready")
        inv_ready = sem("inv_ready")
        probs_ready = sem("probs_ready")
        ptp_ready = sem("ptp_ready")
        ptr_ready = used_sem("ptr_ready")
        apv_ready = sem("apv_ready")
        aout_ready = used_sem("aout_ready")
        mohi_ready = sem("mohi_ready")
        molo_ready = used_sem("molo_ready")

        block = ctx.enter_context(nc.Block())

        def taken(eng, b, name, i, j):
            eng.wait_ge(acc_taken[b], FREE + count(1 + b, name, i, j + 1))

        def split_after(j, results):
            if j + 1 in results:
                return []
            return [j - 1, j] if j in results else [j]

        class Chain:

            def __init__(self, eng, steps):
                self.eng, self.steps, self.n = eng, steps, 0
                self.i, self.per, self.start = None, 0, 0

            def loop(self, i, per):
                self.i, self.per, self.start = i, per, self.n

            def done(self, iterations):
                assert self.n - self.start == self.per, (self.n - self.start, self.per)
                self.n = self.start + iterations * self.per
                self.i = None

            def step(self, ins):
                ins.then_inc(self.steps, 1)
                self.n += 1

            def wait(self):
                self.eng.wait_ge(self.steps, self.n if self.i is None else self.i * self.per + self.n)

            def link(self, ins):
                self.step(ins)
                self.wait()

        NORM = {n: k for k, n in enumerate(["mix", "ffn", "pre0", "out", "post0", "pre1", "post1"])}
        STAT = {n: k for k, n in enumerate(["mix", "ffn", "out", "post0", "pre1", "post1"])}
        STAT["pre0"] = STAT["out"]
        POOLED = {n: k for k, n in enumerate(["ffn", "out", "post0", "post1"])}
        TO_ACT = {n: k for k, n in enumerate(["mix", "ffn", "pre0", "pre1"])}

        @block.sync
        def _(sp):
            for g in range(KT // 4):
                sp.dma_start(x[:, 4 * g:4 * g + 4, :], x_in[:, 4 * g:4 * g + 4, :])\
                    .then_inc(x_loaded[g], 16)
            for c in range(2):
                sp.dma_start(raw[:, 2 * c:2 * c + 2, :], stream_in[c].rearrange("p (u n) -> p u n", u=2))\
                    .then_inc(raw_ready[c], 16)
            with sp.Fori(1, N_CHUNKS // 2) as i:
                for c in range(2):
                    sp.wait_ge(lo_ready, 4 * i - 2 + 2 * c)
                    sp.dma_start(raw[:, 2 * c:2 * c + 2, :],
                                 stream_in[2 * i + c].rearrange("p (u n) -> p u n", u=2))\
                        .then_inc(raw_ready[c], 16)
            for g in range(KT // 4):
                sp.wait_ge(x_added, FREE + KT // 4 + g + 1)
                sp.wait_ge(x_added_pool, FREE + KT // 4 + g + 1)
                sp.dma_start(out[:, 4 * g:4 * g + 4, :], x[:, 4 * g:4 * g + 4, :]).then_inc(stored, 16)
            sp.wait_ge(stored, 16 * (KT // 4))

        @block.tensor
        def _(pe):
            def unit(name, i, j):
                u, s, _ = unit_of(name, i, j)
                pe.wait_ge(lo_ready, u + 1)
                return s

            def bank(b, name, i, j):
                uses = count(1 + b, name, i, j)
                if i is not None or uses:
                    pe.wait_ge(acc_taken[b], FREE + uses)
                return acc[b]

            def tile(out, s, c, hi, lo, k, first, last):
                wc = slice(c * P, (c + 1) * P)
                nc.tensor.matmul(out, w_hi[:, s, wc], hi[:, k, :], start=first, stop=False)
                nc.tensor.matmul(out, w_hi[:, s, wc], lo[:, k, :], start=False, stop=False)
                return nc.tensor.matmul(out, w_lo[:, s, wc], hi[:, k, :], start=False, stop=last)

            def feature_tile(name, i, j, b, use, hi, lo, wait_act=None, ready=()):
                o = bank(b, name, i, use)[:, 0:T]
                for n in range(2):
                    s = unit(name, i, j + n)
                    for c in range(8):
                        if wait_act is not None and c % 4 == 0:
                            four = wait_act * KT // 4 + 2 * n + c // 4 + 1
                            pe.wait_ge(act_ready, 3 * four)
                            pe.wait_ge(act_ready_dve, four)
                        if c % 4 == 0:
                            for signal, per in ready:
                                pe.wait_ge(signal, FREE + (8 * n + c + 4) // per)
                        last = tile(o, s, c, hi, lo, 8 * n + c, n + c == 0, 8 * n + c == KT - 1)
                    last.then_inc(unit_done, 1)

            def token_tiles(name, i, j, units, per_unit, width, hi, lo, k0=0):
                n_k = units * per_unit
                uses = count(3, name, i, 0)
                if i is not None or uses:
                    pe.wait_ge(tok_taken, FREE + 2 * uses)
                for n in range(units):
                    s = unit(name, i, j + n)
                    for c in range(per_unit):
                        k = n * per_unit + c
                        wc = slice(c * width, (c + 1) * width)
                        for t in range(2):
                            tt = slice(t * P, (t + 1) * P)
                            o = tok[t][:, 0:width]
                            nc.tensor.matmul(o, hi[:, k0 + k, tt], w_hi[:, s, wc], start=k == 0, stop=False)
                            nc.tensor.matmul(o, hi[:, k0 + k, tt], w_lo[:, s, wc], start=False, stop=False)
                            last = nc.tensor.matmul(o, lo[:, k0 + k, tt], w_hi[:, s, wc], start=False,
                                                    stop=k == n_k - 1)
                    last.then_inc(unit_done, 1)

            def norm_sum(n):
                pe.wait_ge(sq_added, FREE + KT * (POOLED[n] + 1))
                nc.tensor.matmul(att[3][:, 0:T], ones[:, :], sumsq[:, :], start=True, stop=True)\
                    .then_inc(stat_ready, 1)

            def norm_sum_all(n):
                for k in range(KT):
                    if k % 4 == 0:
                        pe.wait_ge(squares_ready, (n == "pre1") * KT // 4 + k // 4 + 1)
                    last = nc.tensor.matmul(att[3][:, 0:T], ones[:, :], squares_all[:, k, :],
                                            start=k == 0, stop=k == KT - 1)
                last.then_inc(stat_ready, 1)

            pe.wait_ge(const_ready, 4)
            norm_sum_all("mix")

            feature_tile("gates", None, 0, 0, 0, n_hi, n_lo, wait_act=0)
            def mix(i):
                feature_tile("mix", i, 0, 1, 0, n_hi, n_lo)
                feature_tile("mix", i, 2, 0, 0, n_hi, n_lo)
                pe.wait_ge(rows_ready, 1)
                pe.wait_ge(h_ready, FREE + i)
                for t in range(2):
                    nc.tensor.matmul(att[2][:, t:t + 1], a_row[:, t * P:(t + 1) * P],
                                     ident[0:M_HEADS, bass.ds(i, 1)], start=True, stop=True)
                nc.tensor.matmul(att[1][:, :], ones[0:M_HEADS, :], mm_own[:, i, :], start=True, stop=True)\
                    .then_inc(bcast_ready, 1)
                token_tiles("mix", i, 4, 4, 4, M_DV, n_hi, n_lo)
                taken(pe, 1, "mix", i, 0)
                taken(pe, 0, "mix", i, 0)
                nc.tensor.matmul(att[0][:, 0:T], kT[:, 0:P], qT[:, :], start=True, stop=True)
                nc.tensor.matmul(att[0][:, T:T + P], kT[:, P:T], qT[:, P:T], start=True, stop=True)\
                    .then_inc(scores_ready, 1)
                feature_tile("mix", i, 8, 1, 1, n_hi, n_lo)
                early = weighted[:, 0:2, :].rearrange("p b t -> p (b t)")
                late = weighted[:, 2, :]
                pe.wait_ge(st_ready, i + 1)
                pe.wait_ge(tok_taken, FREE + count(3, "mix", i, 1) * 2)
                for v in range(2):
                    o = att[1][:, v * T:(v + 1) * T]
                    vv = slice(v * P, (v + 1) * P)
                    nc.tensor.matmul(o, vm[:, 0, vv], early, start=True, stop=False)
                    nc.tensor.matmul(o[:, P:T], vm[:, 1, vv], late, start=False, stop=True)
                nc.tensor.matmul(att[2][:, 0:T], ones[:, :], early, start=True, stop=False)
                nc.tensor.matmul(att[2][:, P:T], ones[:, :], late, start=False, stop=True)\
                    .then_inc(pv_ready, 1)
                feature_tile("mix", i, 10, 0, 1, n_hi, n_lo)
                feature_tile("mix", i, 12, 1, 2, n_hi, n_lo)
                feature_tile("mix", i, 14, 0, 2, n_hi, n_lo)
                pe.wait_ge(hsum_ready, i + 1)
                nc.tensor.matmul(att[3][:, 0:T], ones[:, :], h_sum[:, :], start=True, stop=True)\
                    .then_inc(hstat_ready, 1)
                feature_tile("mix", i, 16, 1, 3, n_hi, n_lo)
                feature_tile("mix", i, 18, 0, 3, n_hi, n_lo)
                feature_tile("mix", i, 20, 1, 4, n_hi, n_lo)
                feature_tile("mix", i, 22, 0, 4, n_hi, n_lo)

            with pe.Fori(0, M_HEADS) as i:
                mix(i)
            with pe.Fori(0, KT // 2) as i:
                for m in range(2):
                    feature_tile("merge", i, 6 * m, 1, 2 * m, n_hi, n_lo)
                    feature_tile("merge", i, 6 * m + 2, 0, 2 * m, n_hi, n_lo)
                    for n, (hi, lo) in enumerate(((hm_hi, hm_lo), (yc_hi, yc_lo))):
                        if n == 0:
                            pe.wait_ge(hmlo_ready, FREE + M_HEADS)
                        else:
                            pe.wait_ge(yclo_ready, FREE + 2 * M_HEADS)
                        o = bank(1 - n, "merge", i, 2 * m + 1)[:, 0:T]
                        s = unit("merge", i, 6 * m + 4 + n)
                        for c in range(8):
                            last = tile(o, s, c, hi, lo, c, c == 0, c == 7)
                        last.then_inc(unit_done, 1)
            with pe.Fori(0, KT // 2) as i:
                for m in range(2):
                    feature_tile("wout", i, 2 * m, 1 - m, 0, mg_hi, mg_lo, ready=((mglo_ready, 1),))
            norm_sum("ffn")
            def up(i):
                for m in range(2):
                    feature_tile("wup", i, 2 * m, 1 - m, 0, n_hi, n_lo, wait_act=1)

            with pe.Fori(0, F_TILES // 2) as pair:
                up(2 * pair)
                up(2 * pair + 1)
            up(F_TILES - 1)
            with pe.Fori(0, KT // 2) as i:
                for m in range(2):
                    o = bank(1 - m, "wdown", i, 0)[:, 0:T]
                    for n in range(6):
                        s = unit("wdown", i, 6 * m + n)
                        pe.wait_ge(flo_ready, FREE + min(8 * n + 8, F_TILES))
                        for k in range(8 * n, min(8 * n + 8, F_TILES)):
                            last = tile(o, s, k - 8 * n, f_hi, f_lo, k, k == 0, k == F_TILES - 1)
                        last.then_inc(unit_done, 1)
            pe.wait_ge(sq_added, FREE + KT * (POOLED["out"] + 1))
            nc.tensor.matmul(att[3][:, 0:T], ones[:, :], sumsq[:, :], start=True, stop=True)
            nc.tensor.matmul(att[3][:, T:2 * T], ones[:, :], sumsq_g[:, :], start=True, stop=False)
            nc.tensor.matmul(att[3][:, T:2 * T], eps_tile[:, :], sumsq[:, :], start=False, stop=True)\
                .then_inc(stat_ready, 1)
            feature_tile("rank", None, 0, 1, 0, n_hi, n_lo, wait_act=2)
            taken(pe, 1, "rank", None, 0)
            pe.wait_ge(gk2_loaded, 16)
            for hd in range(G_HEADS):
                for t in range(2):
                    c = (2 * hd + t) * P
                    last = nc.tensor.matmul(att[hd][:, t * T:(t + 1) * T], gk2[:, c:c + P],
                                            rank_rows[0:G_RANK + 1, :], start=True, stop=True)
                last.then_inc(gk_ready, 1)
            with pe.Fori(0, G_HEADS) as i:
                for n in range(4):
                    feature_tile("gla", i, 2 * n, n % 2, n // 2, n_hi, n_lo)
                token_tiles("gla", i, 8, 8, 2, G_DV, n_hi, n_lo)
                pe.wait_ge(gk_taken, G_HEADS)
                pe.wait_ge(qx_ready, FREE + 4 * i + 4)
                pe.wait_ge(kk_ready, FREE + 2 * i + 2)
                for kc in range(4):
                    part = slice(CHUNK * (kc % 2), CHUNK * (kc % 2 + 1))
                    col = T * (kc // 2)
                    src = slice(CHUNK * kc, CHUNK * (kc + 1))
                    nxt = slice(CHUNK * (kc + 1), CHUNK * (kc + 2))
                    jobs = [(k_e, src, q_e, src, CHUNK * kc)]
                    if kc < 3:
                        jobs.append((k_l, src, q_e, nxt, CHUNK * (kc + 1)))
                    if kc == 0:
                        jobs.append((k_l, src, q_x, slice(0, 2 * CHUNK), 2 * CHUNK))
                    if kc == 1:
                        jobs.append((k_l, src, q_y, slice(0, CHUNK), 3 * CHUNK))
                    for keys, ks, queries, qs, at in jobs:
                        width = qs.stop - qs.start
                        for dk in range(2):
                            last = nc.tensor.matmul(att[0][part, col + at:col + at + width],
                                                    keys[:, dk, ks], queries[:, dk, qs],
                                                    start=dk == 0, stop=dk == 1)
                last.then_inc(gscores_ready, 1)
                feature_tile("gla", i, 16, 0, 2, n_hi, n_lo)
                pe.wait_ge(at_ready, 5 * i + 5)
                pe.wait_ge(tok_taken, FREE + 2 * count(3, "gla", i, 1))
                for v in range(4):
                    o = att[1 + v // 2][:, (v % 2) * T:(v % 2 + 1) * T]
                    vv = slice(v * P, (v + 1) * P)
                    nc.tensor.matmul(o, vg[:, 0, vv], a_t[:, 0, :], start=True, stop=False)
                    last = nc.tensor.matmul(o[:, P:T], vg[:, 1, vv], a_t[:, 1, P:T], start=False, stop=True)
                last.then_inc(gpv_ready, 1)
                feature_tile("gla", i, 18, 1, 2, n_hi, n_lo)
                feature_tile("gla", i, 20, 0, 3, n_hi, n_lo)
                pe.wait_ge(osum_ready, i + 1)
                nc.tensor.matmul(att[3][:, 0:T], ones[:, :], o_sum[:, :], start=True, stop=True)\
                    .then_inc(ostat_ready, 1)
                feature_tile("gla", i, 22, 1, 3, n_hi, n_lo)
            with pe.Fori(0, KT // 2) as i:
                for m in range(2):
                    feature_tile("glaout", i, 2 * m, m, 0, og_hi, og_lo,
                                 ready=((oglo_ready, 4), (oglo_ready_dve, 4)))
            norm_sum("post0")
            norm_sum_all("pre1")
            def latent_sum(n):
                pe.wait_ge(lsq_added, A_TILES * (n + 1))
                if n:
                    pe.wait_ge(lstd_ready, 1)
                nc.tensor.matmul(att[3][:, 0:T], ones[:, :], l_sumsq[:, n, :], start=True, stop=True)\
                    .then_inc(lstat_ready, 1)

            for k in range(2 * A_TILES):
                feature_tile("latent", None, 2 * k, k % 2, k // 2, n_hi, n_lo, wait_act=3)
                if k == A_TILES:
                    latent_sum(0)
            feature_tile("krope", None, 0, 0, 0, n_hi, n_lo)
            latent_sum(1)
            feature_tile("krope", None, 2, 1, 0, n_hi, n_lo)
            def pair_tile(i, j, b, use, k0):
                pe.wait_ge(c_ready, k0 + A_TILES)
                o = bank(b, "mla", i, use)
                s = unit("mla", i, j)
                for c in range(8):
                    m, k = divmod(c, A_TILES)
                    last = tile(o[:, m * T:(m + 1) * T], s, c, c_hi, c_lo, k0 + k, k == 0,
                                k == A_TILES - 1)
                return last

            def scores(i, n):
                pe.wait_ge(qrope_ready, FREE + 8 * i + 4 * (n // 2 + 1))
                pe.wait_ge(ptr_ready, FREE + 4 * i + max(n - 1, 0))
                for t, (at, width) in enumerate(((0, P), (P, T))):
                    tt = slice(t * P, (t + 1) * P)
                    o = att[n % 2][:, at:at + width]
                    nc.tensor.matmul(o, qn[:, n, tt], kn[:, n, 0:width], start=True, stop=False)
                    last = nc.tensor.matmul(o, q_rope[:, n // 2, tt], kr_m[:, n % 2, 0:width],
                                            start=False, stop=True)
                last.then_inc(logits_ready, 1)

            def transposes(i, n):
                pe.wait_ge(probs_ready, 4 * i + n + 1)
                for b in range(3):
                    last = nc.tensor.transpose(att[n % 2][:, b * P:(b + 1) * P],
                                               probs[:, n % 2, b * P:(b + 1) * P], ident[:, :])
                last.then_inc(ptp_ready, 1)

            def outputs(i, n):
                pe.wait_ge(aout_ready, FREE + 4 * i + 2 * (n // 2))
                pe.wait_ge(ptr_ready, FREE + 4 * i + n + 1)
                o = att[2 + n % 2][:, 0:T]
                vv = slice(n * A_V, (n + 1) * A_V)
                nc.tensor.matmul(o, va[:, 0, vv], probs_t[:, n % 2, 0:T], start=True, stop=False)
                nc.tensor.matmul(o[:, P:T], va[:, 1, vv], probs_t[:, n % 2, T:3 * P], start=False, stop=True)\
                    .then_inc(apv_ready, 1)

            with pe.Fori(0, A_HEADS // 4) as i:
                for n in range(2):
                    pair_tile(i, 2 * n, 0, n, 0).then_inc(unit_done, 1)
                    pair_tile(i, 2 * n + 1, 1, n, A_TILES).then_inc(unit_done, 1)
                last = pair_tile(i, 4, 0, 2, 0)
                unit("mla", i, 5)
                last.then_inc(unit_done, 2)
                token_tiles("mla", i, 6, 2, 2, 4 * A_V, c_hi, c_lo, k0=A_TILES)
                taken(pe, 0, "mla", i, 2)
                taken(pe, 1, "mla", i, 1)
                pe.wait_ge(krm_ready, 4)
                scores(i, 0)
                scores(i, 1)
                feature_tile("mla", i, 8, 1, 2, n_hi, n_lo)
                transposes(i, 0)
                transposes(i, 1)
                feature_tile("mla", i, 10, 0, 3, n_hi, n_lo)
                pe.wait_ge(tok_taken, FREE + 2 * count(3, "mla", i, 1))
                outputs(i, 0)
                outputs(i, 1)
                scores(i, 2)
                scores(i, 3)
                feature_tile("mla", i, 12, 1, 3, n_hi, n_lo)
                transposes(i, 2)
                transposes(i, 3)
                feature_tile("mla", i, 14, 0, 4, n_hi, n_lo)
                outputs(i, 2)
                outputs(i, 3)
            with pe.Fori(0, KT // 2) as i:
                for m in range(2):
                    feature_tile("mlaout", i, 2 * m, 1 - m, 0, mo_hi, mo_lo, ready=((molo_ready, 1),))
            norm_sum("post1")

        @block.scalar
        def _(act):
            chain = Chain(act, act_step)

            def split(name, i, j):
                u, s, use = unit_of(name, i, j + RING)
                high(u, s, use)

            def high(u, s, use):
                if s % 2 == 0:
                    act.wait_ge(raw_ready[s // 2], 16 * use + 16)
                if not isinstance(u, int) or u >= RING:
                    act.wait_ge(unit_done, u - RING + 1)
                nc.scalar.activation(w_hi[:, s, :], raw[:, s, :], ACT.Copy).then_inc(hi_ready, 1)

            def unit_is_done(name, i, j):
                act.wait_ge(unit_done, unit_of(name, i, j)[0] + 1)

            def one_square(n, i, m, source, gain=None):
                act.wait_ge(sq_added, FREE + 2 * i + max(POOLED[n] * KT + m - 1, 0))
                ins = nc.scalar.activation(square[:, m, :], source, ACT.Square)
                if gain is not None:
                    ins = nc.scalar.activation(square_g[:, m, :], source, ACT.Square, scale=gain)
                ins.then_inc(sq_ready, 1)

            def norm_std(n, total=att[3][:, 0:T], bias=eps_col[:, :]):
                act.wait_ge(stat_ready, STAT[n] + 1)
                nc.scalar.activation(std[:, :], total, ACT.Sqrt, bias=bias, scale=1.0 / D)\
                    .then_inc(std_ready, 1)

            def four_high(n, g):
                for m in range(4):
                    act.wait_ge(normed_ready, 4 * g + TO_ACT[n] * KT + m + 1)
                    nc.scalar.activation(n_hi[:, 4 * g + m, :], normed[:, m, :], ACT.Copy)\
                        .then_inc(nhi_ready, 1)

            def norm_high(n):
                with act.Fori(0, KT // 8) as pair:
                    for half in range(2):
                        four_high(n, 2 * pair + half)

            act.dma_start(par[:, :], params_in).then_inc(loaded, 16)
            act.dma_start(pos_i[:, :], positions_in.to_broadcast([P, T])).then_inc(pos_loaded, 16)
            act.dma_start(v_bias[:, :, :].rearrange("p h v -> p (h v)"),
                          v_bias_in.to_broadcast([P, M_HEADS * M_DV])).then_inc(bias_loaded, 16)
            eps = eps_col[:, :]
            act.wait_ge(const_ready, 1)
            for g in range(KT // 4):
                act.wait_ge(x_loaded[g], 16)
                nc.scalar.activation(squares_all[:, 4 * g:4 * g + 4, :], x[:, 4 * g:4 * g + 4, :],
                                     ACT.Square).then_inc(squares_ready, 1)
            norm_std("mix")
            for g in range(RING):
                high(g, g, 0)
                four_high("mix", g)

            act.wait_ge(rope_red, 1)
            nc.scalar.activation(sine[:, :], red[:, 0, :], ACT.Sin).then_inc(rope_ready, 1)
            nc.scalar.activation(cosine[:, :], red[:, 1, :], ACT.Sin).then_inc(rope_ready, 1)

            unit_is_done("gates", None, 1)
            nc.scalar.activation(i_row[0:32, :], acc[0][0:32, 0:T], ACT.Identity,
                                 bias=pcols("b_gate")[0:32, :]).then_inc(row_pre, 1)
            nc.scalar.activation(f_row[32:64, :], acc[0][32:64, 0:T], ACT.Identity,
                                 bias=pcols("b_gate")[32:64, :]).then_inc(acc_taken[0], 1)
            taken(act, 0, "gates", None, 0)
            split("gates", None, 0)
            split("gates", None, 1)
            chain.link(nc.scalar.activation(f_abs[32:64, :], f_row[32:64, :], ACT.Abs))
            chain.link(nc.scalar.activation(f_exp[32:64, :], f_abs[32:64, :], ACT.Exp, scale=-1.0))
            nc.scalar.activation(f_log[32:64, :], f_exp[32:64, :], ACT.Ln, bias=1.0).then_inc(row_log, 1)
            with act.Fori(0, M_HEADS) as i:
                for j in range(24):
                    if j == 1:
                        unit_is_done("mix", i, j)
                        nc.scalar.activation(qT[:, :], acc[1][:, 0:T], ACT.Identity,
                                             bias=par_mix[:, i, 0:1]).then_inc(acc_taken[1], 1)
                    if j == 3:
                        unit_is_done("mix", i, j)
                        nc.scalar.activation(kT[:, :], acc[0][:, 0:T], ACT.Identity,
                                             bias=par_mix[:, i, 1:2]).then_inc(acc_taken[0], 1)
                    if j == 5:
                        act.wait_ge(h_ready, FREE + i)
                        act.wait_ge(bcast_ready, i + 1)
                        nc.scalar.activation(a_col[:, :], att[2][:, 0:2], ACT.Copy).then_inc(a_col_ready, 1)
                        act.wait_ge(a_col_ready, i + 1)
                        nc.scalar.activation(decay[:, 0:2, :].rearrange("p b t -> p (b t)"),
                                             att[1][:, 0:T], ACT.Exp, scale=-1.0, bias=a_col[:, 0:1])
                        nc.scalar.activation(decay[:, 2, :], att[1][:, P:T], ACT.Exp, scale=-1.0,
                                             bias=a_col[:, 1:2])
                        nc.scalar.activation(floor[:, :], att[1][:, T:2 * T], ACT.Exp, scale=-1.0)\
                            .then_inc(mdecay_ready, 1)
                    if j in (9, 11):
                        n = (j - 9) // 2
                        unit_is_done("mix", i, j)
                        if n == 0:
                            act.wait_ge(hm_ready, FREE + 2 * i)
                        nc.scalar.activation(sig_o[:, n, :], acc[1 - n][:, 0:T], ACT.Sigmoid,
                                             bias=par_mix[:, i, 2 + n:3 + n]).then_inc(acc_taken[1 - n], 1)
                    if j == 10:
                        act.wait_ge(pv_ready, i + 1)
                        nc.scalar.activation(den_abs[:, :], att[2][:, 0:T], ACT.Abs)\
                            .then_inc(den_ready, 1)
                    if j in (13, 19):
                        n = (j - 13) // 6
                        unit_is_done("mix", i, j)
                        if n == 1:
                            taken(act, 0, "mix", i, 2)
                        nc.scalar.activation(cc[:, :], acc[1 - n][:, 0:T], ACT.Identity,
                                             bias=par_mix[:, i, 4 + 3 * n:5 + 3 * n])\
                            .then_inc(acc_taken[1 - n], 1)
                    if j == 12:
                        act.wait_ge(h_ready, FREE + i + 1)
                        nc.scalar.activation(h_sq[:, :, :], h[:, :, :], ACT.Square).then_inc(hsq_ready, 1)
                    if j == 16:
                        act.wait_ge(hstat_ready, i + 1)
                        nc.scalar.activation(h_std[:, :], att[3][:, 0:T], ACT.Sqrt, bias=eps,
                                             scale=1.0 / M_DV).then_inc(hstd_ready, 1)
                    if j == 18:
                        act.wait_ge(hm_ready, FREE + 2 * i + 2)
                        nc.scalar.activation(hm_hi[:, bass.ds(2 * i, 2), :], hm[:, :, :], ACT.Copy)\
                            .then_inc(hmhi_ready, 1)
                    if j in (19, 23):
                        n = (j - 19) // 4
                        taken(act, 1 - n, "mix", i, 3 + n)
                        nc.scalar.activation(yc_hi[:, 2 * i + n, :], cz[:, :], ACT.Copy)\
                            .then_inc(ychi_ready, 1)
                    split("mix", i, j)
            with act.Fori(0, KT // 2) as i:
                for j in range(12):
                    m, jj = divmod(j, 6)
                    if jj in (1, 3):
                        n = jj // 2
                        unit_is_done("merge", i, j)
                        act.wait_ge(acc_taken[1 - n], FREE + count(2 - n, "merge", i, 2 * m))
                        nc.scalar.activation((sig_m, sig_c)[n][:, :], acc[1 - n][:, 0:T], ACT.Sigmoid,
                                             bias=par_merge[:, i, 2 * m + n:2 * m + n + 1])\
                            .then_inc(acc_taken[1 - n], 1)
                    if jj == 5:
                        act.wait_ge(merged_ready, FREE + 2 * i + m + 1)
                        nc.scalar.activation(mg_hi[:, 2 * i + m, :], merged[:, :], ACT.Copy)\
                            .then_inc(mghi_ready, 1)
                    split("merge", i, j)

            def last_splits(name, per):
                for j in (per - 2, per - 1):
                    split(name, KT // 2 - 1, j)

            def residual_squares(name, n, per, gain=None):
                def body(i, last):
                    for j in range(per):
                        if j in (per // 2 - 1, per - 1):
                            m = 2 * j // per
                            taken(act, 1 - m, name, i, 0)
                            one_square(n, i, m, x[:, 2 * i + m, :],
                                       gains(gain)[:, i, m:m + 1] if gain else None)
                        if not (last and j == per - 1):
                            for k in split_after(j, (per // 2 - 1, per - 1)):
                                split(name, i, k)

                with act.Fori(0, KT // 2 - 1) as i:
                    body(i, False)
                body(KT // 2 - 1, True)

            residual_squares("wout", "ffn", 4)
            norm_std("ffn")
            last_splits("wout", 4)
            norm_high("ffn")
            def up(i):
                for j in range(4):
                    if j in (1, 3):
                        n = j // 2
                        unit_is_done("wup", i, j)
                        if n == 0:
                            act.wait_ge(fsilu_ready, FREE + i)
                        else:
                            act.wait_ge(fact_ready, FREE + i)
                        nc.scalar.activation((f_gate, f_val)[n][:, :], acc[1 - n][:, 0:T], ACT.Identity,
                                             bias=par_ffn[:, i, 4 * n + 3:4 * n + 4],
                                             scale=par_ffn[:, i, 4 * n + 2:4 * n + 3])
                        nc.scalar.activation(f_pre[:, n, :], acc[1 - n][:, 0:T], ACT.Copy)\
                            .then_inc(acc_taken[1 - n], 1)
                    if j == 2:
                        act.wait_ge(ftap_ready, 2 * i + 1)
                        act.wait_ge(fact_ready, FREE + i)
                        nc.scalar.activation(f_silu[:, :], f_gate[:, :], ACT.Silu)\
                            .then_inc(fsilu_ready, 1)
                    split("wup", i, j)
                    if j == 3:
                        act.wait_ge(fact_ready, FREE + i + 1)
                        nc.scalar.activation(f_hi[:, i, :], f_act[:, :], ACT.Copy)\
                            .then_inc(fhi_ready, 1)

            with act.Fori(0, F_TILES // 2) as pair:
                up(2 * pair)
                up(2 * pair + 1)
            up(F_TILES - 1)
            residual_squares("wdown", "out", 12, "g_out")
            norm_std("pre0", att[3][:, T:2 * T], eps_eps_col[:, :])
            last_splits("wdown", 12)
            norm_high("pre0")
            norm_std("out")
            act.dma_start(gk2[:, :], gk2_in).then_inc(gk2_loaded, 16)
            act.wait_ge(rank_ones, 1)
            unit_is_done("rank", None, 1)
            nc.scalar.activation(rank_rows[0:G_RANK, :], acc[1][0:G_RANK, 0:T], ACT.Copy)\
                .then_inc(acc_taken[1], 1)
            split("rank", None, 0)
            split("rank", None, 1)
            for hd in range(G_HEADS):
                act.wait_ge(gk_ready, hd + 1)
                chain.step(nc.scalar.activation(g_log[:, hd, :], att[hd][:, :], ACT.Abs))
            chain.wait()
            for hd in range(G_HEADS):
                chain.step(nc.scalar.activation(g_log[:, hd, :], g_log[:, hd, :], ACT.Exp, scale=-1.0))
            chain.wait()
            for hd in range(G_HEADS):
                nc.scalar.activation(g_log[:, hd, :], g_log[:, hd, :], ACT.Ln, bias=1.0)\
                    .then_inc(glog_ready, 1)
            with act.Fori(0, G_HEADS) as i:
                for j in range(24):
                    if j in (1, 3):
                        n = j // 2
                        unit_is_done("gla", i, j)
                        act.wait_ge(qe_ready, FREE + 2 * i)
                        nc.scalar.activation(q_sb[:, n, :], acc[n][:, 0:T], ACT.Copy)\
                            .then_inc(acc_taken[n], 1)
                    if j == 4:
                        act.wait_ge(gcum_ready, G_HEADS)
                        act.wait_ge(qx_ready, FREE + 4 * i)
                        act.wait_ge(kk_ready, FREE + 2 * i)
                        nc.scalar.activation(e_pos[:, :, :], gcum[:, i, :, :], ACT.Exp,
                                             scale=1.0 / G_TAU).then_inc(decays_ready, 1)
                        nc.scalar.activation(e_neg[:, :, :], gcum[:, i, :, :], ACT.Exp,
                                             scale=-1.0 / G_TAU).then_inc(decays_ready, 1)
                        act.wait_ge(to_end_ready, i + 1)
                        nc.scalar.activation(e_end[:, :, :], to_end[:, :, :], ACT.Exp,
                                             scale=1.0 / G_TAU).then_inc(decays_ready, 1)
                    if j in (5, 7):
                        n = (j - 5) // 2
                        unit_is_done("gla", i, j)
                        nc.scalar.activation(k_sb[:, n, :], acc[n][:, 0:T], ACT.Copy)\
                            .then_inc(acc_taken[n], 1)
                    if j == 18:
                        act.wait_ge(gpv_ready, i + 1)
                        act.wait_ge(og_ready, FREE + i)
                        for n in range(2):
                            nc.scalar.activation(o_sb[:, 2 * n:2 * n + 2, :], att[1 + n][:, :], ACT.Copy)\
                                .then_inc(osb_ready, 1)
                        for n in range(2):
                            nc.scalar.activation(o_sq[:, 2 * n:2 * n + 2, :], att[1 + n][:, :], ACT.Square)\
                                .then_inc(osq_ready, 1)
                    if j in (17, 19, 21, 23):
                        n = (j - 17) // 2
                        unit_is_done("gla", i, j)
                        if n == 0:
                            act.wait_ge(og_ready, FREE + i)
                        nc.scalar.activation(o_sg[:, n, :], acc[n % 2][:, 0:T], ACT.Silu)\
                            .then_inc(acc_taken[n % 2], 1)
                    if j == 22:
                        act.wait_ge(ostat_ready, i + 1)
                        nc.scalar.activation(o_std[:, :], att[3][:, 0:T], ACT.Sqrt, bias=eps,
                                             scale=1.0 / G_DV).then_inc(ostd_ready, 1)
                    if j == 23:
                        act.wait_ge(og_ready, FREE + i + 1)
                        for n in range(2):
                            nc.scalar.activation(og_hi[:, bass.ds(4 * i + 2 * n, 2), :],
                                                 o_norm[:, 2 * n:2 * n + 2, :], ACT.Copy)\
                                .then_inc(oghi_ready, 1)
                    split("gla", i, j)

            def mixer_output(name, n, gain, to, flip):
                def body(i, last):
                    for j in range(4):
                        if j in (1, 3):
                            m = j // 2
                            unit_is_done(name, i, j)
                            b = 1 - m if flip else m
                            one_square(n, i, m, acc[b][:, 0:T])
                            nc.scalar.activation(to[:, 2 * i + m, :], acc[b][:, 0:T], ACT.Identity,
                                                 scale=gains(gain)[:, i, m:m + 1])\
                                .then_inc(acc_taken[b], 1)
                        if not last:
                            for k in split_after(j, (1, 3)):
                                split(name, i, k)
                        elif name == "glaout" and j == 1:
                            split(name, i, 0)
                            split(name, i, 1)

                with act.Fori(0, KT // 2 - 1) as i:
                    body(i, False)
                body(KT // 2 - 1, True)

            mixer_output("glaout", "post0", "g_post0", y, False)
            norm_std("post0")
            last_splits("glaout", 4)
            for g in range(KT // 4):
                act.wait_ge(x_added, FREE + g + 1)
                act.wait_ge(x_added_pool, FREE + g + 1)
                nc.scalar.activation(squares_all[:, 4 * g:4 * g + 4, :], x[:, 4 * g:4 * g + 4, :],
                                     ACT.Square).then_inc(squares_ready, 1)
            norm_std("pre1")
            norm_high("pre1")
            def latent_std(n):
                act.wait_ge(lstat_ready, n + 1)
                nc.scalar.activation(l_std[:, n, :], att[3][:, 0:T], ACT.Sqrt, bias=eps,
                                     scale=1.0 / A_RANK).then_inc(lstd_ready, 1)

            def latent_high(n):
                for k in range(A_TILES * n, A_TILES * (n + 1)):
                    act.wait_ge(cnormed_ready, k + 1)
                    nc.scalar.activation(c_hi[:, k, :], normed[:, k % 4, :], ACT.Copy)\
                        .then_inc(chi_ready, 1)

            for j in range(16):
                if j % 2:
                    k = j // 2
                    unit_is_done("latent", None, j)
                    nc.scalar.activation(latent[:, k, :], acc[k % 2][:, 0:T], ACT.Copy)
                    if k >= 2:
                        act.wait_ge(lsq_added, k - 1)
                    nc.scalar.activation(l_square[:, k % 2, :], acc[k % 2][:, 0:T], ACT.Square)\
                        .then_inc(acc_taken[k % 2], 1)
                split("latent", None, j)
                if j == 2 * A_TILES + 1:
                    latent_std(0)
                if j == 2 * A_TILES + 3:
                    latent_high(0)
            for j in range(4):
                if j in (1, 3):
                    n = j // 2
                    unit_is_done("krope", None, j)
                    nc.scalar.activation(kr[:, n, :], acc[n][:, 0:T], ACT.Copy).then_inc(acc_taken[n], 1)
                split("krope", None, j)
                if j == 1:
                    latent_std(1)
                    latent_high(1)
            with act.Fori(0, A_HEADS // 4) as i:
                for j in range(16):
                    if j in (0, 2):
                        n = j // 2
                        unit_is_done("mla", i, j)
                        nc.scalar.activation(qn[:, 2 * n:2 * n + 2, :], acc[0][:, :], ACT.Copy)\
                            .then_inc(acc_taken[0], 1)
                    if j == 4:
                        unit_is_done("mla", i, j)
                        act.wait_ge(qrope_ready, FREE + 8 * i)
                        nc.scalar.activation(q_r[:, :, :], acc[0][:, :], ACT.Copy)\
                            .then_inc(acc_taken[0], 1)
                    if j == 7:
                        unit_is_done("mla", i, j)
                        for t in range(2):
                            nc.scalar.activation(va[:, t, :], tok[t][:, :], ACT.Copy).then_inc(tok_taken, 1)
                    if j in (8, 12):
                        for n in range((j - 8) // 2, (j - 8) // 2 + 2):
                            act.wait_ge(neg_ready, 4 * i + n + 1)
                            for t, blocks in enumerate((slice(0, P), slice(P, 3 * P))):
                                nc.scalar.activation(probs[:, n % 2, blocks], logits[:, n % 2, blocks],
                                                     ACT.Exp, bias=neg_max[:, n % 2, t:t + 1],
                                                     accum_out=row_sum[:, n % 2, t:t + 1])\
                                    .then_inc(exp_ready, 1)
                    if j in (10, 14):
                        for n in range((j - 10) // 2, (j - 10) // 2 + 2):
                            act.wait_ge(ptp_ready, 4 * i + n + 1)
                            nc.scalar.activation(probs_t[:, n % 2, :], att[n % 2][:, 0:3 * P], ACT.Copy)\
                                .then_inc(ptr_ready, 1)
                    if j in (9, 11, 13, 15):
                        n = (j - 9) // 2
                        unit_is_done("mla", i, j)
                        if n == 0:
                            act.wait_ge(aout_ready, FREE + 4 * i)
                        b = 1 - n % 2
                        nc.scalar.activation(a_gate[:, n, :], acc[b][:, 0:T], ACT.Silu)\
                            .then_inc(acc_taken[b], 1)
                    if j in (13, 15):
                        for n in range(j - 13, j - 11):
                            act.wait_ge(aout_ready, FREE + 4 * i + n + 1)
                            nc.scalar.activation(mo_hi[:, 4 * i + n, :], a_out[:, n, :], ACT.Copy)\
                                .then_inc(mohi_ready, 1)
                    split("mla", i, j)
            mixer_output("mlaout", "post1", "g_post1", y2, True)
            norm_std("post1")

        @block.vector
        def _(dve):
            chain = Chain(dve, dve_step)

            def split(name, i, j):
                u, s, _ = unit_of(name, i, j + RING)
                rest(u, s)

            def rest(u, s):
                dve.wait_ge(hi_ready, u + 1)
                nc.vector.tensor_tensor(w_lo[:, s, :], raw[:, s, :], w_hi[:, s, :].bitcast(fp32),
                                        ALU.subtract).then_inc(lo_ready, 1)

            def unit_is_done(name, i, j):
                dve.wait_ge(unit_done, unit_of(name, i, j)[0] + 1)

            def norm_rstd(n):
                dve.wait_ge(std_ready, NORM[n] + 1)
                nc.vector.reciprocal(rstd[:, :], std[:, :]).then_inc(rstd_ready, 1)
                dve.wait_ge(rstd_ready, NORM[n] + 1)

            def four_normed(n, g, gain, scale):
                at = TO_ACT[n] * KT // 4
                for m in range(4):
                    if isinstance(g, int) and g + at == 0:
                        pass
                    elif m == 0:
                        dve.wait_ge(act_ready_dve, g + at)
                    else:
                        dve.wait_ge(act_ready, 3 * g + max(3 * at + m - 3, 0))
                    nc.vector.scalar_tensor_tensor(
                        out=normed[:, m, :], in0=x[:, 4 * g + m, :], scalar=gain[:, g, m:m + 1],
                        in1=scale[:, :], op0=ALU.mult, op1=ALU.mult).then_inc(normed_ready, 1)
                dve.wait_ge(nhi_ready, 4 * (g + at) + 1)
                nc.vector.tensor_tensor(n_lo[:, 4 * g, :], normed[:, 0, :], n_hi[:, 4 * g, :].bitcast(fp32),
                                        ALU.subtract).then_inc(act_ready_dve, 1)

            def norm_tiles(n, gain, scale):
                with dve.Fori(0, KT // 8) as pair:
                    for half in range(2):
                        four_normed(n, 2 * pair + half, gain, scale)

            dve.wait_ge(loaded, 16)
            dve.wait_ge(pos_loaded, 16)
            chain.link(nc.vector.tensor_scalar(ang[:, :], pos_i[:, :], pcols("inv_freq"), None, ALU.mult))
            chain.link(nc.vector.tensor_scalar(turns_i[:, :], ang[:, :], 0.15915494309189535, None, ALU.mult))
            chain.link(nc.vector.tensor_copy(turns[:, :], turns_i[:, :]))
            source = ang[:, :]
            for part in (6.28125, 0.0019340515136718750, 1.2556659146e-06):
                chain.link(nc.vector.scalar_tensor_tensor(out=red[:, 0, :], in0=turns[:, :], scalar=-part,
                                                          in1=source, op0=ALU.mult, op1=ALU.add))
                source = red[:, 0, :]
            chain.link(nc.vector.tensor_scalar(red[:, 1, :], red[:, 0, :], 1.5707963267948966, None, ALU.add))
            for compare, edge, turn in ((ALU.is_gt, PI, -2 * PI), (ALU.is_lt, -PI, 2 * PI)):
                chain.link(nc.vector.tensor_scalar(wrap[:, :, :], red[:, :, :], edge, turn, compare, ALU.mult))
                chain.link(nc.vector.tensor_tensor(red[:, :, :], red[:, :, :], wrap[:, :, :], ALU.add))
            nc.vector.tensor_scalar(red[:, :, :], red[:, :, :], -PI_INSIDE, PI_INSIDE, ALU.max, ALU.min)\
                .then_inc(rope_red, 1)
            nc.vector.tensor_tensor(g_both[:, :], pcols("g_out"), pcols("g_pre0"), ALU.mult)\
                .then_inc(gains_ready, 1)
            norm_rstd("mix")
            for g in range(RING):
                four_normed("mix", g, fours(pcols("g_mix")), rstd)
                rest(g, g)
            split("gates", None, 0)
            split("gates", None, 1)
            dve.wait_ge(row_log, 1)
            chain.link(nc.vector.tensor_scalar(f_min[32:64, :], f_row[32:64, :], 0.0, None, ALU.min))
            chain.link(nc.vector.tensor_tensor(logf[32:64, :], f_min[32:64, :], f_log[32:64, :],
                                               ALU.subtract))
            chain.link(nc.vector.tensor_copy(logf0[:, :], logf[32:32 + M_HEADS, :]))
            chain.link(nc.vector.memset(ones_row[:, :], 1.0))
            chain.link(nc.vector.tensor_tensor_scan(b_row[:, :], ones_row[:, :], logf0[:, :], 0.0,
                                                    ALU.mult, ALU.add))
            dve.wait_ge(row_pre, 1)
            chain.link(nc.vector.tensor_tensor(a_row[:, :], i_row[0:M_HEADS, :], b_row[:, :], ALU.subtract))
            chain.link(nc.vector.tensor_tensor_scan(mm_row[:, 0, :], a_row[:, :], a_row[:, :], 0.0,
                                                    ALU.max, ALU.max))
            chain.link(nc.vector.tensor_tensor(mm_row[:, 1, :], mm_row[:, 0, :], b_row[:, :], ALU.add))
            dve.wait_ge(const_ready, 4)
            for hd in range(M_HEADS):
                last = nc.vector.tensor_scalar(mm_own[:, hd, :], mm_row[:, :, :].rearrange("h a t -> h (a t)"),
                                               ident[0:M_HEADS, hd:hd + 1], None, ALU.mult)
            last.then_inc(rows_ready, 1)

            dve.wait_ge(bias_loaded, 16)
            with dve.Fori(0, M_HEADS) as i:
                chain.loop(i, 11)
                for j in range(24):
                    if j == 7:
                        unit_is_done("mix", i, j)
                        nc.vector.tensor_tensor(vm[:, 0, :], tok[0][:, 0:M_DV], v_bias[:, i, :],
                                                ALU.add).then_inc(tok_taken, 1)
                    if j == 8:
                        dve.wait_ge(scores_ready, i + 1)
                        dve.wait_ge(mdecay_ready, i + 1)
                        chain.link(nc.vector.scalar_tensor_tensor(
                            out=weighted[:, :, :].rearrange("p b t -> p (b t)"), in0=att[0][:, 0:3 * P],
                            scalar=M_DQK ** -0.5, in1=decay[:, :, :].rearrange("p b t -> p (b t)"),
                            op0=ALU.mult, op1=ALU.mult))
                        nc.vector.tensor_tensor(vm[:, 1, :], tok[1][:, 0:M_DV], v_bias[:, i, :],
                                                ALU.add).then_inc(tok_taken, 1)
                        for b in (0, 2):
                            ins = nc.vector.copy_predicated(weighted[:, b, :], future[:, :].bitcast(i32),
                                                            zeros[:, :])
                        ins.then_inc(st_ready, 1)
                    if j == 10:
                        dve.wait_ge(den_ready, i + 1)
                        chain.link(nc.vector.tensor_tensor(den[:, :], den_abs[:, :], floor[:, :],
                                                           ALU.max))
                        chain.link(nc.vector.reciprocal(rden[:, :], den[:, :]))
                        for v in range(2):
                            ins = nc.vector.tensor_tensor(h[:, v, :], att[1][:, v * T:(v + 1) * T],
                                                          rden[:, :], ALU.mult)
                            if v == 0:
                                chain.link(ins)
                            else:
                                ins.then_inc(h_ready, 1)
                    if j in (15, 21):
                        n = (j - 15) // 6
                        unit_is_done("mix", i, j)
                        taken(dve, 1 - n, "mix", i, 2 + n)
                        nc.vector.scalar_tensor_tensor(
                            out=cu[:, :], in0=acc[n][:, 0:T], scalar=par_mix[:, i, 5 + 3 * n:6 + 3 * n],
                            in1=cc[:, :], op0=ALU.add, op1=ALU.mult).then_inc(acc_taken[n], 1)
                        taken(dve, n, "mix", i, 2 + 2 * n)
                        chain.link(nc.vector.tensor_scalar(cy[:, :], cu[:, :],
                                                           par_conv[:, i, 3 * n + 2:3 * n + 3], None,
                                                           ALU.mult))
                        for back, w in ((1, 1), (2, 0)):
                            chain.link(nc.vector.scalar_tensor_tensor(
                                out=cy[:, back:T], in0=cu[:, 0:T - back],
                                scalar=par_conv[:, i, 3 * n + w:3 * n + w + 1], in1=cy[:, back:T],
                                op0=ALU.mult, op1=ALU.add))
                    if j == 17 or j == 23:
                        n = (j - 17) // 6
                        unit_is_done("mix", i, j)
                        dve.wait_ge(yclo_ready, FREE + 2 * i + n)
                        nc.vector.scalar_tensor_tensor(
                            out=cz[:, :], in0=acc[1 - n][:, 0:T],
                            scalar=par_mix[:, i, 6 + 3 * n:7 + 3 * n],
                            in1=cy[:, :], op0=ALU.add, op1=ALU.mult).then_inc(acc_taken[1 - n], 1)
                    if j == 17:
                        dve.wait_ge(hstd_ready, i + 1)
                        chain.link(nc.vector.reciprocal(h_rstd[:, :], h_std[:, :]))
                        dve.wait_ge(hmlo_ready, FREE + i)
                        taken(dve, 0, "mix", i, 1)
                        for v in range(2):
                            nc.vector.scalar_tensor_tensor(
                                out=h_norm[:, v, :], in0=h[:, v, :], scalar=par_head[:, i, v:v + 1],
                                in1=h_rstd[:, :], op0=ALU.mult, op1=ALU.mult).then_inc(h_normed, 1)
                        for v in range(2):
                            dve.wait_ge(h_normed, 2 * i + v + 1)
                            nc.vector.tensor_tensor(hm[:, v, :], h_norm[:, v, :], sig_o[:, v, :],
                                                    ALU.mult).then_inc(hm_ready, 1)
                    split("mix", i, j)
                chain.done(M_HEADS)
            with dve.Fori(0, KT // 2) as i:
                for j in range(12):
                    m, jj = divmod(j, 6)
                    if jj in (4, 5):
                        n = jj - 4
                        unit_is_done("merge", i, j)
                        taken(dve, 1 - n, "merge", i, 2 * m)
                        dve.wait_ge(merged_ready, FREE + 2 * i + m)
                        nc.vector.tensor_tensor((part_m, part_c)[n][:, :], acc[1 - n][:, 0:T],
                                                (sig_m, sig_c)[n][:, :], ALU.mult)\
                            .then_inc(acc_taken[1 - n], 1)
                    split("merge", i, j)

            def last_splits(name, per):
                for j in (per - 2, per - 1):
                    split(name, KT // 2 - 1, j)

            def residual(name, per):
                def body(i, last):
                    for j in range(per):
                        if j in (per // 2 - 1, per - 1):
                            m = 2 * j // per
                            unit_is_done(name, i, j)
                            nc.vector.tensor_tensor(x[:, 2 * i + m, :], acc[1 - m][:, 0:T],
                                                    x[:, 2 * i + m, :], ALU.add)\
                                .then_inc(acc_taken[1 - m], 1)
                        if not (last and j == per - 1):
                            for k in split_after(j, (per // 2 - 1, per - 1)):
                                split(name, i, k)

                with dve.Fori(0, KT // 2 - 1) as i:
                    body(i, False)
                body(KT // 2 - 1, True)

            residual("wout", 4)
            norm_rstd("ffn")
            norm_tiles("ffn", fours(pcols("g_ffn")), rstd)
            last_splits("wout", 4)
            def up(i):
                for j in range(4):
                    if j in (1, 3):
                        n = j // 2
                        u = (f_gate, f_val)[n]
                        taken(dve, 1 - n, "wup", i, 0)
                        src = f_pre[:, n, :]
                        chain.link(nc.vector.scalar_tensor_tensor(
                            out=u[:, 1:T], in0=src[:, 0:T - 1],
                            scalar=par_ffn[:, i, 4 * n + 1:4 * n + 2], in1=u[:, 1:T],
                            op0=ALU.mult, op1=ALU.add))
                        nc.vector.scalar_tensor_tensor(
                            out=u[:, 2:T], in0=src[:, 0:T - 2],
                            scalar=par_ffn[:, i, 4 * n:4 * n + 1], in1=u[:, 2:T],
                            op0=ALU.mult, op1=ALU.add).then_inc(ftap_ready, 1)
                    if j == 3:
                        dve.wait_ge(fsilu_ready, FREE + i + 1)
                        dve.wait_ge(ftap_ready, 2 * i + 2)
                        dve.wait_ge(flo_ready, FREE + i)
                        nc.vector.tensor_tensor(f_act[:, :], f_silu[:, :], f_val[:, :], ALU.mult)\
                            .then_inc(fact_ready, 1)
                    split("wup", i, j)

            with dve.Fori(0, F_TILES // 2) as pair:
                chain.loop(pair, 4)
                up(2 * pair)
                up(2 * pair + 1)
                chain.done(F_TILES // 2)
            up(F_TILES - 1)
            residual("wdown", 12)
            norm_rstd("pre0")
            dve.wait_ge(gains_ready, 1)
            norm_tiles("pre0", fours(g_both[:, :]), rstd)
            last_splits("wdown", 12)
            split("rank", None, 0)
            split("rank", None, 1)
            dve.wait_ge(std_ready, NORM["out"] + 1)
            nc.vector.reciprocal(out_rstd[:, :], std[:, :]).then_inc(rstd_ready, 1)
            dve.wait_ge(restart_ready, 1)
            for hd in range(G_HEADS):
                dve.wait_ge(glog_ready, hd + 1)
                nc.vector.scalar_tensor_tensor(out=log_a[:, hd, :], in0=att[hd][:, :], scalar=0.0,
                                               in1=g_log[:, hd, :], op0=ALU.min, op1=ALU.subtract)\
                    .then_inc(gk_taken, 1)
                dve.wait_ge(gk_taken, hd + 1)
                nc.vector.tensor_tensor_scan(gcum[:, hd, :, :].rearrange("p a t -> p (a t)"),
                                             restart[:, :, :].rearrange("p a t -> p (a t)"),
                                             log_a[:, hd, :], 0.0, ALU.mult, ALU.add).then_inc(gcum_ready, 1)
            dve.wait_ge(gcum_ready, G_HEADS)
            dve.wait_ge(at_init, 2)
            with dve.Fori(0, G_HEADS) as i:
                chain.loop(i, 7)
                for j in range(24):
                    if j == 0:
                        dve.wait_ge(decays_ready, FREE + 3 * i)
                        b = gcum[:, i, :, :].rearrange("p a (c t) -> p (a c) t", t=CHUNK)
                        nc.vector.tensor_tensor(
                            to_end[:, :, :].rearrange("p a (c t) -> p (a c) t", t=CHUNK),
                            b[:, :, CHUNK - 1:CHUNK].to_broadcast([P, 2 * T // CHUNK, CHUNK]), b,
                            ALU.subtract).then_inc(to_end_ready, 1)
                    if j in (4, 5):
                        n = j - 4
                        taken(dve, n, "gla", i, 0)
                        dve.wait_ge(decays_ready, FREE + 3 * i + 1)
                        nc.vector.scalar_tensor_tensor(out=q_e[:, n, :], in0=q_sb[:, n, :],
                                                       scalar=G_DK ** -0.5, in1=e_pos[:, n, :],
                                                       op0=ALU.mult, op1=ALU.mult)\
                            .then_inc(qe_ready, 1)
                    if j == 5:
                        dve.wait_ge(qe_ready, FREE + 2 * i + 2)
                        over1, over2 = 2 * CHUNK - 1, 3 * CHUNK - 1
                        for n in range(2):
                            chain.step(nc.vector.tensor_scalar(
                                q_y[:, n, :], q_e[:, n, 3 * CHUNK:T], e_pos[:, n, over2:over2 + 1],
                                None, ALU.mult))
                        chain.wait()
                        for n in range(2):
                            nc.vector.tensor_scalar(
                                q_x[:, n, 0:CHUNK], q_e[:, n, 2 * CHUNK:3 * CHUNK],
                                e_pos[:, n, over1:over1 + 1], None, ALU.mult).then_inc(qx_ready, 1)
                            nc.vector.tensor_scalar(
                                q_x[:, n, CHUNK:2 * CHUNK], q_y[:, n, :],
                                e_pos[:, n, over1:over1 + 1], None, ALU.mult).then_inc(qx_ready, 1)
                    if j == 15:
                        unit_is_done("gla", i, j)
                        for t in range(2):
                            nc.vector.tensor_copy(vg[:, t, :], tok[t][:, :]).then_inc(tok_taken, 1)
                    if j == 16:
                        dve.wait_ge(gscores_ready, i + 1)
                        nc.vector.tensor_copy(a_t[:, 0, P:T], att[0][:, P:T]).then_inc(at_ready, 1)
                        for s in range(2):
                            for p, lo, hi in ((CHUNK, 0, CHUNK), (P, CHUNK, P)):
                                at = s * P
                                nc.vector.copy_predicated(
                                    a_t[0:p, s, at + lo:at + hi], kept[0:p, lo:hi].bitcast(i32),
                                    att[0][0:p, s * T + at + lo:s * T + at + hi]).then_inc(at_ready, 1)
                    if j == 22:
                        dve.wait_ge(ostd_ready, i + 1)
                        chain.link(nc.vector.reciprocal(o_rstd[:, :], o_std[:, :]))
                        dve.wait_ge(oglo_ready, FREE + i)
                        dve.wait_ge(oglo_ready_dve, FREE + i)
                        dve.wait_ge(osb_ready, 2 * i + 2)
                        for v in range(4):
                            chain.step(nc.vector.scalar_tensor_tensor(
                                out=o_norm[:, v, :], in0=o_sb[:, v, :], scalar=pcols("g_gla")[:, v:v + 1],
                                in1=o_rstd[:, :], op0=ALU.mult, op1=ALU.mult))
                    if j == 23:
                        chain.wait()
                        taken(dve, 0, "gla", i, 3)
                        taken(dve, 1, "gla", i, 3)
                        nc.vector.tensor_tensor(o_norm[:, :, :], o_norm[:, :, :], o_sg[:, :, :],
                                                ALU.mult).then_inc(og_ready, 1)
                        dve.wait_ge(oghi_ready, 2 * i + 2)
                        nc.vector.tensor_tensor(og_lo[:, bass.ds(4 * i + 2, 2), :], o_norm[:, 2:4, :],
                                                og_hi[:, bass.ds(4 * i + 2, 2), :].bitcast(fp32),
                                                ALU.subtract).then_inc(oglo_ready_dve, 1)
                    split("gla", i, j)
                chain.done(G_HEADS)

            def add_normed(n, source, k):
                norm_rstd(n)
                both = rstd[:, :].rearrange("p (o t) -> p o t", o=1).to_broadcast([P, 2, T])

                def four(g):
                    for half in range(2):
                        dve.wait_ge((x_added_pool, x_added)[half], FREE + g + k * KT // 4)
                        nc.vector.tensor_tensor(normed[:, 2 * half:2 * half + 2, :],
                                                source[:, bass.ds(4 * g + 2 * half, 2), :], both, ALU.mult)\
                            .then_inc(scaled_ready, 1)
                    dve.wait_ge(scaled_ready, 2 * g + (k * KT // 2 + 2))
                    tiles = bass.ds(4 * g + 2, 2)
                    nc.vector.tensor_tensor(x[:, tiles, :], x[:, tiles, :], normed[:, 2:4, :], ALU.add)\
                        .then_inc(x_added, 1)

                with dve.Fori(0, KT // 8) as pair:
                    for half in range(2):
                        four(2 * pair + half)

            def out_normed(i):
                for m in range(2):
                    nc.vector.scalar_tensor_tensor(
                        out=x[:, 2 * i + m, :], in0=x[:, 2 * i + m, :],
                        scalar=gains("g_out")[:, i, m:m + 1],
                        in1=out_rstd[:, :], op0=ALU.mult, op1=ALU.mult).then_inc(x_normed, 1)

            dve.wait_ge(rstd_ready, NORM["out"] + 1)
            with dve.Fori(0, KT // 2 - 1) as i:
                for j in range(4):
                    split("glaout", i, j)
                out_normed(i)
            split("glaout", KT // 2 - 1, 0)
            split("glaout", KT // 2 - 1, 1)
            out_normed(KT // 2 - 1)
            dve.wait_ge(x_normed, KT)
            add_normed("post0", y, 0)
            last_splits("glaout", 4)
            norm_rstd("pre1")
            norm_tiles("pre1", fours(pcols("g_pre1")), rstd)
            def latent_normed(n):
                dve.wait_ge(lstd_ready, n + 1)
                chain.link(nc.vector.reciprocal(l_rstd[:, n, :], l_std[:, n, :]))
                for k in range(A_TILES * n, A_TILES * (n + 1)):
                    if k < 4:
                        dve.wait_ge(act_ready, 3 * KT)
                        dve.wait_ge(act_ready_dve, KT)
                    else:
                        dve.wait_ge(c_ready, k - 3)
                    nc.vector.scalar_tensor_tensor(
                        out=normed[:, k % 4, :], in0=latent[:, k, :],
                        scalar=pcols("g_latent")[:, k:k + 1], in1=l_rstd[:, n, :],
                        op0=ALU.mult, op1=ALU.mult).then_inc(cnormed_ready, 1)

            for j in range(16):
                split("latent", None, j)
                if j == 2 * A_TILES + 1:
                    latent_normed(0)
            for j in range(4):
                split("krope", None, j)
                if j == 1:
                    latent_normed(1)
            def rotated(n, to, ready):
                rows = slice(HALF * n, HALF * (n + 1))
                at = A_ROPE * (n % 2)
                nc.vector.tensor_tensor(to[at:at + HALF, :], rope_t[rows, 0, :], rope_t[rows, 1, :],
                                        ALU.subtract).then_inc(ready, 1)
                nc.vector.tensor_tensor(to[at + HALF:at + A_ROPE, :], rope_t[rows, 2, :],
                                        rope_t[rows, 3, :], ALU.add).then_inc(ready, 1)

            taken(dve, 0, "krope", None, 0)
            taken(dve, 1, "krope", None, 0)
            dve.wait_ge(rope_ready, 2)
            dve.wait_ge(krm_zero, 1)
            for n, (part, angle) in enumerate(((0, cosine), (1, sine), (1, cosine), (0, sine))):
                chain.step(nc.vector.tensor_tensor(rope_t[:, n, :], kr[:, part, :], angle[:, :], ALU.mult))
            chain.wait()
            for n in range(2):
                rotated(n, kr_m[:, n, :], krm_ready)
            dve.wait_ge(krm_ready, 4)
            dve.wait_ge(causal_ready, 3)
            with dve.Fori(0, A_HEADS // 4) as i:
                chain.loop(i, 2 + 4 * 2)
                for j in range(16):
                    if j in (1, 3):
                        n = j // 2
                        unit_is_done("mla", i, j)
                        nc.vector.tensor_copy(kn[:, 2 * n:2 * n + 2, :], acc[1][:, :])\
                            .then_inc(acc_taken[1], 1)
                    if j == 5:
                        taken(dve, 0, "mla", i, 2)
                        chain.step(nc.vector.tensor_tensor(rope_t[:, 0, :], q_r[:, 0, :], cosine[:, :],
                                                           ALU.mult))
                        chain.step(nc.vector.tensor_tensor(rope_t[:, 1, :], q_r[:, 1, :], sine[:, :],
                                                           ALU.mult))
                        chain.wait()
                        dve.wait_ge(qprod_ready, 2 * i + 2)
                        for n in range(4):
                            rotated(n, q_rope[:, n // 2, :], qrope_ready)
                    if j in (7, 12):
                        first = 2 * (j // 12)
                        for n in (first, first + 1):
                            dve.wait_ge(logits_ready, 4 * i + n + 1)
                            dve.wait_ge(exp_ready, FREE + 8 * i + max(2 * (n - 1), 0))
                            chain.link(nc.vector.scalar_tensor_tensor(
                                out=logits[:, n % 2, :], in0=att[n % 2][:, 0:3 * P],
                                scalar=(A_NOPE + A_ROPE) ** -0.5, in1=causal[:, :],
                                op0=ALU.mult, op1=ALU.add))
                            nc.vector.reduce_max(row_max[:, n % 2, 0:1], logits[:, n % 2, 0:P], AX)
                            chain.link(nc.vector.reduce_max(row_max[:, n % 2, 1:2],
                                                            logits[:, n % 2, P:3 * P], AX))
                            nc.vector.tensor_scalar(neg_max[:, n % 2, :], row_max[:, n % 2, :], -1.0,
                                                    None, ALU.mult).then_inc(neg_ready, 1)
                        for n in (first, first + 1):
                            dve.wait_ge(exp_ready, FREE + 8 * i + 2 * n + 2)
                            nc.vector.reciprocal(row_inv[:, n % 2, :], row_sum[:, n % 2, :])\
                                .then_inc(inv_ready, 1)
                    if j in (12, 15):
                        for n in range(2 * (j // 15), 2 * (j // 15) + 2):
                            dve.wait_ge(apv_ready, 4 * i + n + 1)
                            taken(dve, 1 - n % 2, "mla", i, (2, 3, 3, 4)[n])
                            dve.wait_ge(molo_ready, FREE + 4 * i)
                            nc.vector.tensor_tensor(a_out[:, n, :], att[2 + n % 2][:, 0:T],
                                                    a_gate[:, n, :], ALU.mult).then_inc(aout_ready, 1)
                    split("mla", i, j)
                chain.done(A_HEADS // 4)
            with dve.Fori(0, KT // 2 - 1) as i:
                for j in range(4):
                    split("mlaout", i, j)
            add_normed("post1", y2, 1)

        @block.gpsimd
        def _(pool):
            chain = Chain(pool, pool_step)
            gp = nc.gpsimd

            def add_squares(n, with_gain=False):
                k = POOLED[n]
                pool.wait_ge(stat_ready, STAT[n])
                if with_gain:
                    chain.step(gp.memset(eps_tile[:, :], EPS))
                    chain.link(gp.memset(sumsq_g[:, :], 0.0))
                chain.link(gp.memset(sumsq[:, :], 0.0))
                with pool.Fori(0, KT // 2) as i:
                    for m in range(2):
                        pool.wait_ge(sq_ready, 2 * i + (k * KT + m + 1))
                        pool.wait_ge(sq_added, FREE + 2 * i + (k * KT + m))
                        ins = gp.tensor_tensor(sumsq[:, :], sumsq[:, :], square[:, m, :], ALU.add)
                        if with_gain:
                            ins = gp.tensor_tensor(sumsq_g[:, :], sumsq_g[:, :], square_g[:, m, :], ALU.add)
                        ins.then_inc(sq_added, 1)

            def norm_low(n):
                at = TO_ACT[n] * KT

                def four(g):
                    for m in (1, 2, 3):
                        pool.wait_ge(nhi_ready, 4 * g + (at + m + 1))
                        gp.tensor_tensor(n_lo[:, 4 * g + m, :], normed[:, m, :],
                                         n_hi[:, 4 * g + m, :].bitcast(fp32), ALU.subtract)\
                            .then_inc(act_ready, 1)

                with pool.Fori(0, KT // 8) as pair:
                    for half in range(2):
                        four(2 * pair + half)

            def add_scaled(k):
                def four(g):
                    pool.wait_ge(scaled_ready, 2 * g + (k * KT // 2 + 1))
                    tiles = bass.ds(4 * g, 2)
                    gp.tensor_tensor(x[:, tiles, :], x[:, tiles, :], normed[:, 0:2, :], ALU.add)\
                        .then_inc(x_added_pool, 1)

                with pool.Fori(0, KT // 8) as pair:
                    for half in range(2):
                        four(2 * pair + half)

            for signal in free_from_start:
                pool.sem_inc(signal, FREE)
            gp.memset(eps_eps_col[:, :], EPS * EPS)
            gp.memset(eps_col[:, :], EPS).then_inc(const_ready, 1)
            chain.step(gp.memset(ident[:, :], 0.0))
            chain.step(gp.memset(future[:, :], 1.0))
            chain.step(gp.memset(zeros[:, :], 0.0))
            gp.memset(ones[:, :], 1.0).then_inc(const_ready, 1)
            chain.wait()
            gp.affine_select(out=ident[:, :], in_=ident[:, :], compare_op=ALU.not_equal, fill=1.0, base=0,
                             pattern=[[-1, P]], channel_multiplier=1).then_inc(const_ready, 1)
            gp.affine_select(out=future[:, :], in_=future[:, :], compare_op=ALU.is_gt, fill=0.0, base=0,
                             pattern=[[-1, P]], channel_multiplier=1).then_inc(const_ready, 1)
            norm_low("mix")
            with pool.Fori(0, M_HEADS) as i:
                pool.wait_ge(hsq_ready, i + 1)
                gp.tensor_tensor(h_sum[:, :], h_sq[:, 0, :], h_sq[:, 1, :], ALU.add).then_inc(hsum_ready, 1)
                pool.wait_ge(hmhi_ready, i + 1)
                gp.tensor_tensor(hm_lo[:, bass.ds(2 * i, 2), :], hm[:, :, :],
                                 hm_hi[:, bass.ds(2 * i, 2), :].bitcast(fp32), ALU.subtract)\
                    .then_inc(hmlo_ready, 1)
                for n in range(2):
                    pool.wait_ge(ychi_ready, 2 * i + n + 1)
                    gp.tensor_tensor(yc_lo[:, 2 * i + n, :], cz[:, :],
                                     yc_hi[:, 2 * i + n, :].bitcast(fp32), ALU.subtract)\
                        .then_inc(yclo_ready, 1)
            with pool.Fori(0, KT // 2) as i:
                for m in range(2):
                    taken(pool, 1, "merge", i, 2 * m + 1)
                    taken(pool, 0, "merge", i, 2 * m + 1)
                    pool.wait_ge(mglo_ready, FREE + 2 * i + m)
                    gp.tensor_tensor(merged[:, :], part_m[:, :], part_c[:, :], ALU.add)\
                        .then_inc(merged_ready, 1)
                    pool.wait_ge(mghi_ready, 2 * i + m + 1)
                    gp.tensor_tensor(mg_lo[:, 2 * i + m, :], merged[:, :],
                                     mg_hi[:, 2 * i + m, :].bitcast(fp32), ALU.subtract)\
                        .then_inc(mglo_ready, 1)
            add_squares("ffn")
            norm_low("ffn")
            with pool.Fori(0, F_TILES) as i:
                pool.wait_ge(fhi_ready, i + 1)
                gp.tensor_tensor(f_lo[:, i, :], f_act[:, :], f_hi[:, i, :].bitcast(fp32), ALU.subtract)\
                    .then_inc(flo_ready, 1)
            add_squares("out", with_gain=True)
            norm_low("pre0")
            gp.memset(rank_rows[:, :], 1.0).then_inc(rank_ones, 1)
            chain.step(gp.memset(restart[:, :, :], 1.0))
            chain.step(gp.memset(kept[:, :], 1.0))
            gp.memset(a_t[:, :, :], 0.0).then_inc(at_init, 1)
            chain.wait()
            gp.affine_select(out=kept[:, :], in_=kept[:, :], compare_op=ALU.is_ge, fill=0.0, base=0,
                             pattern=[[1, P]], channel_multiplier=-1).then_inc(at_init, 1)
            gp.memset(restart[:, :, :].rearrange("p a (c t) -> p (a c) t", t=CHUNK)[:, :, 0:1], 0.0)\
                .then_inc(restart_ready, 1)
            with pool.Fori(0, G_HEADS) as i:
                taken(pool, 0, "gla", i, 1)
                taken(pool, 1, "gla", i, 1)
                pool.wait_ge(decays_ready, FREE + 3 * i + 3)
                gp.tensor_tensor(k_e[:, :, :], k_sb[:, :, :], e_neg[:, :, :], ALU.mult).then_inc(kk_ready, 1)
                gp.tensor_tensor(k_l[:, :, :], k_sb[:, :, :], e_end[:, :, :], ALU.mult).then_inc(kk_ready, 1)
                pool.wait_ge(osq_ready, 2 * i + 2)
                chain.loop(i, 1)
                chain.link(gp.tensor_tensor(o_sum2[:, :, :], o_sq[:, 0:2, :], o_sq[:, 2:4, :], ALU.add))
                gp.tensor_tensor(o_sum[:, :], o_sum2[:, 0, :], o_sum2[:, 1, :], ALU.add)\
                    .then_inc(osum_ready, 1)
                pool.wait_ge(oghi_ready, 2 * i + 1)
                gp.tensor_tensor(og_lo[:, bass.ds(4 * i, 2), :], o_norm[:, 0:2, :],
                                 og_hi[:, bass.ds(4 * i, 2), :].bitcast(fp32), ALU.subtract)\
                    .then_inc(oglo_ready, 1)
                chain.done(G_HEADS)
            add_squares("post0")
            pool.wait_ge(x_normed, KT)
            add_scaled(0)
            norm_low("pre1")
            def latent_low(n):
                for k in range(A_TILES * n, A_TILES * (n + 1)):
                    pool.wait_ge(chi_ready, k + 1)
                    gp.tensor_tensor(c_lo[:, k, :], normed[:, k % 4, :], c_hi[:, k, :].bitcast(fp32),
                                     ALU.subtract).then_inc(c_ready, 1)

            chain.link(gp.memset(l_sumsq[:, :, :], 0.0))
            chain.step(gp.memset(causal[:, :], 0.0))
            gp.memset(kr_m[:, :, :], 0.0).then_inc(krm_zero, 1)
            chain.wait()
            for b in (0, 2):
                d = causal[:, b * P:(b + 1) * P]
                gp.affine_select(out=d, in_=d, compare_op=ALU.is_ge, fill=-1e30, base=0,
                                 pattern=[[-1, P]], channel_multiplier=1).then_inc(causal_ready, 1)
            gp.memset(row_max[:, :, :], 0.0).then_inc(causal_ready, 1)
            for k in range(2 * A_TILES):
                taken(pool, k % 2, "latent", None, k // 2)
                if k:
                    pool.wait_ge(lsq_added, k)
                n = k // A_TILES
                gp.tensor_tensor(l_sumsq[:, n, :], l_sumsq[:, n, :], l_square[:, k % 2, :], ALU.add)\
                    .then_inc(lsq_added, 1)
                if k == A_TILES + 1:
                    latent_low(0)
            latent_low(1)
            pool.wait_ge(krm_ready, 4)
            with pool.Fori(0, A_HEADS // 4) as i:
                chain.loop(i, 4)
                taken(pool, 0, "mla", i, 2)
                pool.wait_ge(qrope_ready, FREE + 8 * i)
                gp.tensor_tensor(rope_t[:, 2, :], q_r[:, 1, :], cosine[:, :], ALU.mult)\
                    .then_inc(qprod_ready, 1)
                gp.tensor_tensor(rope_t[:, 3, :], q_r[:, 0, :], sine[:, :], ALU.mult)\
                    .then_inc(qprod_ready, 1)
                for n in range(4):
                    pool.wait_ge(inv_ready, 4 * i + n + 1)
                    chain.step(gp.tensor_tensor(
                        probs[:, n % 2, 0:P], probs[:, n % 2, 0:P],
                        row_inv[:, n % 2, 0:1].to_broadcast([P, P]), ALU.mult))
                    gp.tensor_tensor(
                        probs[:, n % 2, P:3 * P], probs[:, n % 2, P:3 * P],
                        row_inv[:, n % 2, 1:2].to_broadcast([P, 2 * P]), ALU.mult)\
                        .then_inc(probs_ready, 1)
                for n in range(4):
                    pool.wait_ge(mohi_ready, 4 * i + n + 1)
                    gp.tensor_tensor(mo_lo[:, 4 * i + n, :], a_out[:, n, :],
                                     mo_hi[:, 4 * i + n, :].bitcast(fp32), ALU.subtract)\
                        .then_inc(molo_ready, 1)
                chain.done(A_HEADS // 4)
            add_squares("post1")
            add_scaled(1)


def kernel(**inputs):
    import concourse.bacc as _bacc
    import numpy as np
    from concourse.bass_utils import run_bass_kernel_spmd as _run

    arrays = lay_out({k: np.asarray(v) for k, v in inputs.items()})
    nc = _bacc.Bacc("TRN2", target_bir_lowering=False, num_devices=1)
    ins = {n: nc.dram_tensor(n, v.shape, mybir.dt.from_np(v.dtype), kind="ExternalInput").ap()
           for n, v in arrays.items()}
    out = nc.dram_tensor("out", (P, KT, T), mybir.dt.float32, kind="ExternalOutput").ap()
    program(nc, out=out, **ins)
    got = _run(nc, [arrays], core_ids=[0]).results[0]["out"]
    return np.ascontiguousarray(got.transpose(2, 1, 0).reshape(1, T, D))


def lay_out(a):
    import numpy as np

    splits = (M_HEADS * M_DQK, M_HEADS * M_DQK, M_HEADS * M_DV, M_HEADS * M_DV, M_HEADS, M_HEADS,
              C_TILES * P, C_TILES * P, C_TILES * P, D, D)
    offs = [sum(splits[:n]) for n in range(len(splits))]
    cols = {n: slice(o, o + w) for n, o, w in zip("q k v o i f cb cc ch gm gc".split(), offs, splits)}
    w_in = {n: a["w_in"][:, s] for n, s in cols.items()}
    b_in = {n: a["b_in"][s] for n, s in cols.items()}

    chunks = np.zeros((N_CHUNKS, P, 2 * UNIT), np.float32)
    at = [0, 0]

    def put(w, width=P):
        k, n = w.shape
        for c in range(0, n, width):
            for r in range(0, k, P):
                block = w[r:r + P, c:c + width]
                chunks[at[0], 0:block.shape[0], at[1]:at[1] + block.shape[1]] = block
                at[1] += width
                if at[1] == 2 * UNIT:
                    at[0], at[1] = at[0] + 1, 0

    def end():
        if at[1]:
            at[0], at[1] = at[0] + 1, 0

    def tile_of(w, m):
        return w[:, m * P:(m + 1) * P]

    gates = np.zeros((D, P), np.float32)
    gates[:, 0:M_HEADS] = w_in["i"]
    gates[:, 32:32 + M_HEADS] = w_in["f"]
    put(gates)
    for h in range(M_HEADS):
        put(tile_of(w_in["q"], h))
        put(tile_of(w_in["k"], h))
        put(w_in["v"][:, h * M_DV:(h + 1) * M_DV], M_DV)
        for n in range(2):
            put(tile_of(w_in["o"], 2 * h + n))
        for n in range(2):
            for part in ("cc", "ch", "cb"):
                put(tile_of(w_in[part], 2 * h + n))
    for m in range(KT):
        put(tile_of(w_in["gm"], m))
        put(tile_of(w_in["gc"], m))
        put(tile_of(a["w_branch_m"], m))
        put(tile_of(a["w_branch_c"], m))
    put(a["w_out"])
    for f in range(F_TILES):
        put(tile_of(a["w_up"], f))
        put(tile_of(a["w_up"], F_TILES + f))
    for m in range(KT):
        put(tile_of(a["w_down"], m))
        end()
    gla = a["l0_gla_w_in_2"]
    qk, vv = G_HEADS * G_DK, G_HEADS * G_DV
    ranks = np.zeros((D, P), np.float32)
    ranks[:, 0:G_RANK] = gla[:, 2 * qk + 2 * vv:]
    put(ranks)
    for h in range(G_HEADS):
        put(gla[:, h * G_DK:(h + 1) * G_DK])
        put(gla[:, qk + h * G_DK:qk + (h + 1) * G_DK])
        put(gla[:, 2 * qk + h * G_DV:2 * qk + (h + 1) * G_DV], G_DV)
        put(gla[:, 2 * qk + vv + h * G_DV:2 * qk + vv + (h + 1) * G_DV])
    put(a["l0_gla_w_out_2"])
    mla = a["l1_mla_w_in_2"]
    put(mla[:, 0:2 * A_RANK])
    k_rope = mla[:, 2 * A_RANK:2 * A_RANK + A_ROPE]
    for half in range(2):
        put(np.concatenate([k_rope[:, half * HALF:(half + 1) * HALF]] * 4, axis=1))
    w_q = a["l1_mla_w_qb_2"].reshape(A_RANK, A_HEADS, A_NOPE + A_ROPE)
    w_kv = a["l1_mla_w_kvb_2"].reshape(A_RANK, A_HEADS, A_NOPE + A_V)
    for g in range(0, A_HEADS, 4):
        for n in (0, 2):
            for w in (w_q, w_kv):
                put(w[:, g + n, 0:A_NOPE])
                put(w[:, g + n + 1, 0:A_NOPE])
        for half in range(2):
            r = A_NOPE + half * HALF
            put(np.ascontiguousarray(w_q[:, g:g + 4, r:r + HALF]).reshape(A_RANK, 4 * HALF))
        end()
        put(np.ascontiguousarray(w_kv[:, g:g + 4, A_NOPE:]).reshape(A_RANK, 4 * A_V), 4 * A_V)
        for n in range(4):
            put(tile_of(mla[:, 2 * A_RANK + A_ROPE:], g + n))
    put(a["l1_mla_w_out_2"])
    assert at == [N_CHUNKS, 0], at

    def col(v):
        return v.reshape(-1, P).T

    b_gate = np.zeros((P, 1), np.float32)
    b_gate[0:M_HEADS, 0] = b_in["i"]
    b_gate[32:32 + M_HEADS, 0] = b_in["f"]
    b_mix = []
    for h in range(M_HEADS):
        b_mix += [col(b_in["q"])[:, h], col(b_in["k"])[:, h]]
        b_mix += [col(b_in["o"])[:, 2 * h + n] for n in range(2)]
        b_mix += [col(b_in[part])[:, 2 * h + n] for n in range(2) for part in ("cc", "ch", "cb")]
    b_merge = [col(b_in[part])[:, m] for m in range(KT) for part in ("gm", "gc")]
    conv = a["conv_w"].reshape(3, C_TILES, P).transpose(2, 1, 0).reshape(P, -1)
    ffn = np.concatenate([a["ffn_conv_w"], a["ffn_conv_b"][None]]).reshape(4, 2, F_TILES, P)
    ffn = ffn.transpose(3, 2, 1, 0).reshape(P, -1)
    freq = np.float32(10000.0) ** (-np.arange(0, A_ROPE, 2, dtype=np.float32) / np.float32(A_ROPE))
    params = {
        "g_mix": col(a["norm_mix_g"]), "g_ffn": col(a["norm_ffn_g"]), "g_out": col(a["norm_out_g"]),
        "g_pre0": col(a["l0_pre_norm_2"]), "g_post0": col(a["l0_post_norm_2"]),
        "g_pre1": col(a["l1_pre_norm_2"]), "g_post1": col(a["l1_post_norm_2"]),
        "b_gate": b_gate, "b_mix": np.stack(b_mix, 1), "b_merge": np.stack(b_merge, 1),
        "g_head": col(a["mlstm_head_g"]), "w_conv": conv, "w_ffn": ffn, "g_gla": col(a["l0_gla_g_onorm_2"]),
        "g_latent": np.concatenate([col(a["l1_mla_g_qa_2"]), col(a["l1_mla_g_kva_2"])], 1),
        "inv_freq": np.tile(freq.astype(np.float32), 4)[:, None],
    }
    for n, k in PARAMS:
        assert params[n].shape == (P, k), (n, params[n].shape)
    return {
        "x_in": np.ascontiguousarray(a["x"][0].T.reshape(KT, P, T).transpose(1, 0, 2)),
        "stream_in": chunks,
        "params_in": np.concatenate([params[n] for n, _ in PARAMS], 1),
        "v_bias_in": np.ascontiguousarray(b_in["v"])[None],
        "gk2_in": np.concatenate([a["l0_gla_w_gk2_2"], a["l0_gla_b_gk_2"][None]]),
        "positions_in": np.ascontiguousarray(a["positions_2"]),
    }
```
